# Optimizing a Trainium2 kernel written in Bass

```python
import jax, jax.numpy as jnp
from jax import lax
import numpy as np

D_MODEL = 1024
BATCH = 1
SEQ = 2048
DEPTH = 1

PLE_DIM = 256
SSM_EXPAND = 2
D_INNER = SSM_EXPAND * D_MODEL
SSM_HEAD_DIM = 64
SSM_HEADS = D_INNER // SSM_HEAD_DIM
SSM_GROUPS = 4
HEADS_PER_GROUP = SSM_HEADS // SSM_GROUPS
D_STATE = 128
CONV_WIDTH = 4
CHUNK = 128
D_CONV_CH = D_INNER + 2 * SSM_GROUPS * D_STATE
D_POOL = D_MODEL
POOL_WINDOWS = (2, 4, 8, 16)
POOL_GROUPS = len(POOL_WINDOWS)
POOL_GROUP_DIM = D_POOL // POOL_GROUPS
IN_SPLITS = (D_INNER, D_CONV_CH, SSM_HEADS, D_POOL, D_POOL, D_MODEL, D_MODEL)
N_IN = sum(IN_SPLITS)
EPS = 1e-6

kernel_name = "hybrid_ssd_multipool_gated_merge"

def rms_norm(x, g):
    xf = x.astype(jnp.float32)
    y = xf * lax.rsqrt(jnp.mean(xf * xf, axis=-1, keepdims=True) + EPS)
    return (y * g.astype(jnp.float32)).astype(x.dtype)

def causal_depthwise_conv(u, w, b):
    out = lax.conv_general_dilated(
        u, w[:, None, :].astype(u.dtype), window_strides=(1,),
        padding=[(CONV_WIDTH - 1, 0)],
        dimension_numbers=("NWC", "WIO", "NWC"),
        feature_group_count=u.shape[-1])
    return out + b

def ssd_chunked(xs, dt, a_neg, bm, cm):
    bsz, seqlen = xs.shape[0], xs.shape[1]
    nc = seqlen // CHUNK
    dtype = xs.dtype
    x = xs.reshape(bsz, nc, CHUNK, SSM_GROUPS, HEADS_PER_GROUP, SSM_HEAD_DIM)
    dtc = dt.reshape(bsz, nc, CHUNK, SSM_GROUPS, HEADS_PER_GROUP)
    bc = bm.reshape(bsz, nc, CHUNK, SSM_GROUPS, D_STATE)
    cc = cm.reshape(bsz, nc, CHUNK, SSM_GROUPS, D_STATE)
    xdt = x * dtc[..., None]
    a_dt = dtc.astype(jnp.float32) * a_neg.astype(jnp.float32).reshape(SSM_GROUPS, HEADS_PER_GROUP)
    a_cs = jnp.cumsum(a_dt, axis=2)

    seg = a_cs[:, :, :, None] - a_cs[:, :, None, :]
    mask = jnp.tril(jnp.ones((CHUNK, CHUNK), dtype=bool))[:, :, None, None]
    decay_ls = jnp.exp(jnp.where(mask, seg, -jnp.inf)).astype(dtype)
    cb = jnp.einsum("bclgn,bcsgn->bclsg", cc, bc)
    m = cb[..., None] * decay_ls
    y_diag = jnp.einsum("bclsge,bcsgep->bclgep", m, xdt)

    decay_to_end = jnp.exp(a_cs[:, :, -1:] - a_cs).astype(dtype)
    states = jnp.einsum("bclgn,bclgep->bcgepn", bc, xdt * decay_to_end[..., None])
    chunk_decay = jnp.exp(a_cs[:, :, -1]).astype(dtype)

    def step(h, inp):
        s_c, d_c = inp
        return h * d_c[..., None, None] + s_c, h

    h0 = jnp.zeros_like(states[:, 0])
    _, prev = lax.scan(step, h0, (jnp.moveaxis(states, 1, 0), jnp.moveaxis(chunk_decay, 1, 0)))
    prev = jnp.moveaxis(prev, 0, 1)

    y_off = jnp.einsum("bclgn,bcgepn->bclgep", cc, prev) * jnp.exp(a_cs).astype(dtype)[..., None]
    return (y_diag + y_off).reshape(bsz, seqlen, D_INNER)

def causal_multiscale_pool(u, mix_w, mix_b, scale):
    bsz, seqlen = u.shape[0], u.shape[1]
    ug = u.reshape(bsz, seqlen, POOL_GROUPS, POOL_GROUP_DIM)
    csum = jnp.cumsum(ug.astype(jnp.float32), axis=1)
    pos = jnp.arange(1, seqlen + 1, dtype=jnp.float32)
    means = []
    for gi, w in enumerate(POOL_WINDOWS):
        cs = csum[:, :, gi]
        lag = jnp.pad(cs, ((0, 0), (w, 0), (0, 0)))[:, :seqlen]
        means.append((cs - lag) / jnp.minimum(pos, float(w))[None, :, None])
    pooled = jnp.stack(means, axis=2).astype(u.dtype) - ug
    mixed = jnp.einsum("bsgc,gcd->bsgd", pooled, mix_w).reshape(bsz, seqlen, D_POOL) + mix_b
    return mixed * scale

def setup_inputs(seed: int = 0) -> dict:
    key = jax.random.key(seed)
    ks = jax.random.split(key, 20)
    f32 = jnp.float32
    nrm = lambda k, shape, s: jax.random.normal(k, shape, f32) * s
    dt0 = jnp.exp(jax.random.uniform(ks[6], (DEPTH, SSM_HEADS), f32, np.log(1e-3), np.log(1e-1)))
    return {
        "x": nrm(ks[0], (BATCH, SEQ, D_MODEL), 1.0),
        "p": nrm(ks[1], (DEPTH, BATCH, SEQ, PLE_DIM), 1.0),
        "norm_g": 1.0 + nrm(ks[2], (DEPTH, D_MODEL), 0.05),
        "w_in": nrm(ks[3], (DEPTH, D_MODEL, N_IN), D_MODEL ** -0.5),
        "conv_w": nrm(ks[4], (DEPTH, CONV_WIDTH, D_CONV_CH), CONV_WIDTH ** -0.5),
        "conv_b": nrm(ks[5], (DEPTH, D_CONV_CH), 0.02),
        "dt_bias": dt0 + jnp.log(-jnp.expm1(-dt0)),
        "a_log": jnp.log(jax.random.uniform(ks[7], (DEPTH, SSM_HEADS), f32, 1.0, 16.0)),
        "d_skip": 1.0 + nrm(ks[8], (DEPTH, SSM_HEADS), 0.1),
        "gnorm_g": 1.0 + nrm(ks[9], (DEPTH, D_INNER), 0.05),
        "pool_mix_w": nrm(ks[10], (DEPTH, POOL_GROUPS, POOL_GROUP_DIM, POOL_GROUP_DIM), POOL_GROUP_DIM ** -0.5),
        "pool_mix_b": nrm(ks[11], (DEPTH, D_POOL), 0.02),
        "pool_scale": 1.0 + nrm(ks[12], (DEPTH, D_POOL), 0.1),
        "w_branch_a": nrm(ks[13], (DEPTH, D_INNER, D_MODEL), D_INNER ** -0.5),
        "w_branch_b": nrm(ks[14], (DEPTH, D_POOL, D_MODEL), D_POOL ** -0.5),
        "w_out": nrm(ks[15], (DEPTH, D_MODEL, D_MODEL), D_MODEL ** -0.5),
        "ple_norm_g": 1.0 + nrm(ks[16], (DEPTH, D_MODEL), 0.05),
        "w_ple_gate": nrm(ks[17], (DEPTH, D_MODEL, D_MODEL), D_MODEL ** -0.5),
        "w_ple_up": nrm(ks[18], (DEPTH, PLE_DIM, D_MODEL), PLE_DIM ** -0.5),
        "final_g": 1.0 + nrm(ks[19], (D_MODEL,), 0.05),
    }

def reference(x, p, norm_g, w_in, conv_w, conv_b, dt_bias, a_log, d_skip, gnorm_g,
              pool_mix_w, pool_mix_b, pool_scale, w_branch_a, w_branch_b, w_out,
              ple_norm_g, w_ple_gate, w_ple_up, final_g):
    split_idx = [int(v) for v in np.cumsum(IN_SPLITS)[:-1]]
    bsz, seqlen = x.shape[0], x.shape[1]
    for i in range(DEPTH):
        h = rms_norm(x, norm_g[i])
        proj = h @ w_in[i]
        z, xbc, dt_raw, u, z_pool, g_a, g_b = jnp.split(proj, split_idx, axis=-1)

        xbc = jax.nn.silu(causal_depthwise_conv(xbc, conv_w[i], conv_b[i]))
        x_ssm, b_ssm, c_ssm = jnp.split(xbc, [D_INNER, D_INNER + SSM_GROUPS * D_STATE], axis=-1)
        dt = jax.nn.softplus(dt_raw + dt_bias[i])
        a_neg = -jnp.exp(a_log[i])
        y_a = ssd_chunked(x_ssm, dt, a_neg, b_ssm, c_ssm)
        y_a = y_a + x_ssm * jnp.repeat(d_skip[i], SSM_HEAD_DIM)
        y_a = (y_a * jax.nn.silu(z)).reshape(bsz, seqlen, SSM_GROUPS, D_INNER // SSM_GROUPS)
        y_a = rms_norm(y_a, gnorm_g[i].reshape(SSM_GROUPS, D_INNER // SSM_GROUPS)).reshape(bsz, seqlen, D_INNER)

        y_b = causal_multiscale_pool(u, pool_mix_w[i], pool_mix_b[i], pool_scale[i]) * jax.nn.silu(z_pool)

        merged = jax.nn.sigmoid(g_a) * (y_a @ w_branch_a[i]) + jax.nn.sigmoid(g_b) * (y_b @ w_branch_b[i])
        x = x + merged @ w_out[i]

        gate = jax.nn.sigmoid(rms_norm(x, ple_norm_g[i]) @ w_ple_gate[i])
        x = x + gate * (p[i] @ w_ple_up[i])
    return rms_norm(x, final_g)


_drawn_inputs = setup_inputs


def setup_inputs(seed=0):
    import zlib

    import numpy as np

    out = dict(_drawn_inputs(seed))
    spreads = {}
    factors = {'conv_b': 4.494,
     'gnorm_g': 2.696,
     'pool_mix_b': 8.0,
     'ple_norm_g': 22.673,
     'pool_scale': 3.564}
    for name, (base, spread) in spreads.items():
        noise = np.random.default_rng([zlib.crc32(name.encode()), seed]).standard_normal(out[name].shape)
        drawn = base * np.exp(spread * noise) if base else spread * noise
        out[name] = __import__('jax').numpy.asarray(drawn.astype(out[name].dtype))
    for name, factor in factors.items():
        out[name] = (out[name] * factor).astype(out[name].dtype)
    return out
```

```python
from collections import namedtuple
from contextlib import ExitStack

import concourse.bass as bass
import numpy as np
from concourse import mybir
from concourse.alu_op_type import AluOpType as ALU

ACT = mybir.ActivationFunctionType
F32 = mybir.dt.float32
F32R = mybir.dt.float32r
BF16 = mybir.dt.bfloat16

P = 128
SEQ, DM, PLE = 2048, 1024, 256
DI = 2 * DM
HEADS, HD, GROUPS, NS = 32, 64, 4, 128
HG = HEADS // GROUPS
GC = DI // GROUPS
TAPS = 4
T = 512
NB = SEQ // T
NC = T // P
KT = DM // P
GT = GC // P
PG = DM // GROUPS
PT = PG // P
EPS = 1e-6
COL_Z, COL_X = 0, DI
COL_B = COL_X + DI
COL_C = COL_B + GROUPS * NS
COL_DT = COL_C + GROUPS * NS
COL_U = COL_DT + HEADS
COL_ZP = COL_U + DM
COL_GA = COL_ZP + DM
COL_GB = COL_GA + DM
ATANH = [1.0 / (2 * k + 1) for k in range(1, 8)]

UW = 1024
RING = 3
U_B, U_C, U_X, U_Z, U_ZP, U_U, U_A = 0, 1, 2, 6, 10, 12, 14
G_UNITS = 18
J_UNITS = 6
O_UNITS = 18
JP = KT // 2
N_LOADS = 9 + TAPS + 1


def half_bank(h, c):
    return (0, 1, 6, 7)[c] if h else 2 + c


def acc_bank(j):
    return (0, 1)[j % 2] if j // 2 % 2 else (6, 7)[j % 2]


def k_bank(pos, k):
    return k if pos.phase == "P" else 2 + k

Pos = namedtuple("Pos", "phase b i")


class Signal:

    TRIPS = {"P": 1, "G": GROUPS, "J": JP, "O": 1}

    def __init__(self, sem, P=0, G=0, J=0, O=0, credit=0, step=1):
        self.sem, self.credit, self.step = sem, credit, step
        self.n = {"P": P, "G": G, "J": J, "O": O}
        self.total = sum(self.n[ph] * self.TRIPS[ph] for ph in self.n)

    def at(self, pos, k, back=0):
        before = 0
        for ph in "PGJO":
            if ph == pos.phase:
                break
            before += self.n[ph] * self.TRIPS[ph]
        assert self.credit >= back or isinstance(pos.b, int) or before + k >= back
        const = self.step * (self.credit + before + k + 1 - back)
        value = pos.b * (self.step * self.total) + const
        if self.TRIPS[pos.phase] > 1 and self.n[pos.phase]:
            value = value + pos.i * (self.step * self.n[pos.phase])
        return value

    def start_of(self, pos, phase, back=0):
        before = 0
        for ph in "PGJO":
            if ph == phase:
                break
            before += self.n[ph] * self.TRIPS[ph]
        return pos.b * (self.step * self.total) + self.step * (self.credit + before - back)


def build(nc, x, p, norm_g, w_in, conv_w, conv_b, dt_bias, a_log, d_skip, gnorm_g, pool_mix_w,
          pool_mix_b, pool_scale, w_branch_a, w_branch_b, w_out, ple_norm_g, w_ple_gate,
          w_ple_up, final_g, out):
    ctx = ExitStack()
    with ctx:
        base = [16512]

        def sb(name, shape, dt=F32, at=None):
            size = int(np.prod(shape[1:])) * (2 if dt == BF16 else 4)
            size = (size + 31) // 32 * 32
            if at is None:
                at = base[0]
                base[0] += size
            assert at + size <= nc.sbuf_usable_end, (name, at + size)
            return nc.alloc_sbuf_tensor_at(name, shape, dt, offset=at)

        KB = 1024
        h_hi = sb("h_hi", [P, KT, T], F32R)
        h_lo = sb("h_lo", [P, KT, T], F32R)
        wring = base[0]
        w_hi = [sb(f"w_hi{s}", [P, UW], F32R) for s in range(RING)]
        w_raw = [sb(f"w_raw{s}", [P, UW]) for s in range(RING)]
        w_lo = [sb(f"w_lo{s}", [P, UW], F32R, at=wring + (RING + s) * UW * 4) for s in range(RING)]
        state = sb("state", [P, GROUPS, GC])
        yb_at = base[0]
        yb_hi = sb("yb_hi", [P, KT, T], F32R)
        yb_lo = sb("yb_lo", [P, KT, T], F32R)
        acc_at = base[0]
        a_acc = sb("a_acc", [P, KT, T])
        ya_at = base[0]
        ya_hi = sb("ya_hi", [P, GT, T], F32R)
        ya_lo = sb("ya_lo", [P, GT, T], F32R)
        pl_hi = sb("pl_hi", [P, PT, T], F32R, at=ya_at)
        pl_lo = sb("pl_lo", [P, PT, T], F32R, at=ya_at + PT * T * 4)
        NDT = (KT + 3) * HEADS
        wdt_hi = sb("wdt_hi", [P, NDT], F32R)
        wdt_lo = sb("wdt_lo", [P, NDT], F32R)
        conv_halo = sb("conv_halo", [P, GROUPS, 6, TAPS - 1])
        pool_halo = sb("pool_halo", [P, GROUPS, PT, 16])
        ident = sb("ident", [P, P])
        cap = sb("cap", [P, P])
        tok_dt = sb("tok_dt", [P, NC, HEADS])
        tok_acs = sb("tok_acs", [P, NC, HEADS])
        exp_acs = sb("exp_acs", [P, NC, HEADS])
        taps = sb("taps", [P, TAPS + 1, (DI + 2 * GROUPS * NS) // P])
        ng = sb("ng", [P, KT])
        pg = sb("pg", [P, KT])
        gn = sb("gn", [P, GROUPS, GT])
        mixb = sb("mixb", [P, GROUPS, PT])
        pscale = sb("pscale", [P, GROUPS, PT])
        dskip = sb("dskip", [P, HEADS])
        dtb = sb("dtb", [HEADS, 1])
        aneg = sb("aneg", [HEADS, 2])
        inv16 = sb("inv16", [P, GROUPS, 16])
        invw = sb("invw", [P, GROUPS])
        ss = sb("ss", [P, NC])
        rr = sb("rr", [P, NC])
        rq = sb("rq", [P, NC])
        ssy = sb("ssy", [P, NC])
        rry = sb("rry", [P, NC])
        rqy = sb("rqy", [P, NC])
        junk = sb("junk", [P, DM], BF16)
        junk_y = sb("junk_y", [P, GC], BF16)
        tmp = base[0]
        xc = sb("xc", [P, GT, T])
        zs = sb("zs", [P, NC, GC])
        abc = [sb(f"abc{s}", [P, HG, P]) for s in range(2)]
        MX = HG * P
        m = sb("m", [P, MX + 2 * HG])
        xt = sb("xt", [P, GC])
        xdt = sb("xdt", [P, GC])
        xdd = sb("xdd", [P, GC])
        cbuf = [sb(f"cbuf{s}", [P, TAPS - 1 + T]) for s in range(2)]
        bc = [sb("b_ch", [P, T]), sb("c_ch", [P, T])]
        zps = sb("zps", [P, PT, T])
        ubuf = sb("ubuf", [P, 16 + T])
        cs = sb("cs", [P, 16 + T])
        pf = sb("pf", [P, T])
        bt = sb("bt", [P, P])
        cbs = sb("cbs", [P, P])
        mx_hi = sb("mx_hi", [P, PT, PG], F32R)
        mx_at = base[0]
        mx_raw = sb("mx_raw", [P, PT, PG])
        mx_lo = sb("mx_lo", [P, PT, PG], F32R, at=mx_at)
        xin = sb("xin", [P, NC, DM], at=tmp)
        xs = sb("xs", [P, NC, DM], at=tmp + 16 * KB)
        dtw = [sb(f"dtw{s}", [HEADS, T], at=tmp + (32 + 2 * s) * KB) for s in range(7)]
        wdt_raw = sb("wdt_raw", [P, NDT], at=tmp + 46 * KB)
        pos16 = sb("pos16", [P, 16], at=tmp + 48 * KB)
        m_hi = sb("m_hi", [P, KT, T], F32R, at=tmp)
        m_lo = sb("m_lo", [P, KT, T], F32R, at=tmp + 16 * KB)
        sga = [sb(f"sga{s}", [P, T], at=tmp + (32 + 4 * s) * KB) for s in range(2)]
        sgb = [sb(f"sgb{s}", [P, T], at=tmp + (34 + 4 * s) * KB) for s in range(2)]
        x2 = sb("x2", [P, NC, DM], at=acc_at)
        xs2 = sb("xs2", [P, NC, DM], at=ya_at)
        pin = sb("pin", [P, NC, PLE], at=yb_at)
        p_hi = sb("p_hi", [P, 2, T], F32R, at=yb_at + 4 * KB)
        p_lo = sb("p_lo", [P, 2, T], F32R, at=yb_at + 8 * KB)
        fg = sb("fg", [P, DM], at=yb_at + 12 * KB)
        sg = sb("sg", [P, NC, T], at=yb_at + 16 * KB)

        bank = [ctx.enter_context(nc.psum_tensor(f"bank{i}", [P, 512], F32)) for i in range(8)]
        acs_dram = nc.dram_tensor("acs_scratch", (NB, HEADS, T), F32).ap()

        def sig(name, **counts):
            return Signal(ctx.enter_context(nc.semaphore(name)), **counts)

        passed = ctx.enter_context(nc.semaphore("passed"))
        params_in = ctx.enter_context(nc.semaphore("params_in"))
        w_in_s = [sig(f"w_loaded{s}", G=6, J=2, O=6, step=16) for s in range(RING)]
        x_in = sig("x_in", P=1, step=16)
        acs_out = sig("acs_out", P=1, step=16)
        abc_in = [sig(f"abc_in{s}", G=2, step=16) for s in range(2)]
        mix_in = sig("mix_in", G=1, step=16)
        x2_in = sig("x2_in", O=1, step=16)
        pin_in = sig("pin_in", O=1, step=16)
        fg_in = sig("fg_in", O=1, step=16)
        out_done = sig("out_done", O=NC, step=16)
        consts = ctx.enter_context(nc.semaphore("consts"))
        w_ready = sig("w_ready", G=G_UNITS, J=J_UNITS, O=O_UNITS)
        w_hi_done = sig("w_hi_done", G=G_UNITS, J=J_UNITS, O=O_UNITS)
        squares = sig("squares", P=NC, O=2 * NC, credit=1)
        root = sig("root", P=1, O=2)
        t_hi = sig("t_hi", P=KT, O=KT + 2)
        dt_exp = sig("dt_exp", P=1)
        acs_exp = sig("acs_exp", P=1)
        a_exp = ctx.enter_context(nc.semaphore("a_exp"))
        cbuf_full = sig("cbuf_full", G=6)
        silu_done = sig("silu_done", G=6)
        z_silu = sig("z_silu", G=NC)
        decay = sig("decay", G=NC)
        xt_full = sig("xt_full", G=NC)
        bt_full = sig("bt_full", G=2 * NC)
        zp_full = sig("zp_full", G=PT)
        zp_silu = sig("zp_silu", G=1)
        u_full = sig("u_full", G=PT)
        pl_hi_done = sig("pl_hi_done", G=PT)
        yb_hi_done = sig("yb_hi_done", G=PT)
        mx_hi_done = sig("mx_hi_done", G=1)
        y_squares = sig("y_squares", G=NC, credit=1)
        y_root = sig("y_root", G=1)
        ya_hi_done = sig("ya_hi_done", G=GT)
        gates = sig("gates", J=4)
        m_hi_done = sig("m_hi_done", J=2)
        ple_gate = sig("ple_gate", O=2 * NC)
        link_s = sig("vector_link", P=18, G=61, J=4, O=3)
        setup_link = ctx.enter_context(nc.semaphore("setup_link"))
        setup_done = ctx.enter_context(nc.semaphore("setup_done"))
        meansq = sig("meansq", P=1, O=2)
        xs_full = sig("xs_full", P=NC, O=NC)
        t_lo = sig("t_lo", P=KT, O=KT + 2)
        dt_abs = sig("dt_abs", P=1)
        dt_full = sig("dt_full", P=1)
        tok_full = sig("tok_full", P=1)
        acc_zero = sig("acc_zero", P=1)
        conv_done = sig("conv_done", G=6, credit=2)
        seg_full = sig("seg_full", G=NC, credit=2)
        xdt_full = sig("xdt_full", G=NC)
        m_full = sig("m_full", G=NC)
        y_gated = sig("y_gated", G=NC, credit=1)
        state_new = sig("state_new", G=NC, credit=1)
        pf_full = sig("pf_full", G=PT)
        pooled = sig("pooled", G=PT, credit=1)
        mx_full = sig("mx_full", G=1, credit=1)
        mix_read = sig("mix_read", G=PT)
        yb_val = sig("yb_val", G=PT)
        yb_full = sig("yb_full", G=PT)
        y_meansq = sig("y_meansq", G=1)
        y_normed = sig("y_normed", G=NC)
        ya_full = sig("ya_full", G=GT)
        acc_added = sig("acc_added", G=KT, credit=1)
        m_val = sig("m_val", J=2)
        merged = sig("merged", J=2, credit=2)
        x2_sum = sig("x2_sum", O=2 * NC)
        up_gated = sig("up_gated", O=2 * NC)
        x3_sum = sig("x3_sum", O=2 * NC)
        out_full = sig("out_full", O=NC)
        unit_done = sig("unit_done", G=G_UNITS, J=J_UNITS, O=O_UNITS, credit=RING)
        t_psum = sig("t_psum", P=KT, O=KT + 2)
        dt_psum = sig("dt_psum", P=1)
        tok_psum = sig("tok_psum", P=1)
        xt_psum = sig("xt_psum", G=NC)
        bcb_psum = sig("bcb_psum", G=NC)
        ssd_psum = sig("ssd_psum", G=3 * NC, credit=3)
        mix_psum = sig("mix_psum", G=PT, credit=1)
        yt_psum = sig("yt_psum", G=GT)

        xb = x.rearrange("a (b c p) d -> (a b) p c d", c=NC, p=P)
        ob = out.rearrange("a (b c p) d -> (a b) c p d", c=NC, p=P)
        pb = p.rearrange("l a (b c p) d -> (l a b) p c d", c=NC, p=P)
        win = w_in.rearrange("l (k p) n -> p (l k) n", p=P)
        wa = w_branch_a.rearrange("l (g k p) n -> p (l g) k n", g=GROUPS, p=P)
        wb = w_branch_b.rearrange("l (k p) n -> p (l k) n", p=P)
        wo = w_out.rearrange("l (k p) n -> p (l k) n", p=P)
        wg = w_ple_gate.rearrange("l (k p) n -> p (l k) n", p=P)
        wu = w_ple_up.rearrange("l (k p) n -> p (l k) n", p=P)
        mixw = pool_mix_w.rearrange("l g (k p) n -> p (l g) k n", p=P)

        def one(ap, i):
            if isinstance(i, int):
                return ap[:, i]
            view = ap[:, bass.ds(i, 1)]
            names = "abcd"[: len(view.shape) - 2]
            return view.rearrange(f"p x {' '.join(names)} -> p (x {names[0]}) {' '.join(names[1:])}")

        def col(ap, i, j):
            return ap[:, bass.ds(i, 1), j:j + 1].rearrange("p a b -> p (a b)")

        def heads(ap):
            return ap.rearrange("p (h d) -> p h d", h=HG)

        def per_head(ap, n):
            return ap.unsqueeze(2).to_broadcast([P, HG, n])

        def on_its_own(eng):
            eng.sem_inc(passed, 1)

        block = ctx.enter_context(nc.Block())

        @block.sync
        def _(sp):
            loads = [
                (ng[:], norm_g.rearrange("l (k p) -> p (l k)", p=P)),
                (pg[:], ple_norm_g.rearrange("l (k p) -> p (l k)", p=P)),
                (gn[:], gnorm_g.rearrange("l (g k p) -> p (l g) k", p=P, g=GROUPS)),
                (mixb[:], pool_mix_b.rearrange("l (g k p) -> p (l g) k", p=P, g=GROUPS)),
                (pscale[:], pool_scale.rearrange("l (g k p) -> p (l g) k", p=P, g=GROUPS)),
                (dtb[:], dt_bias.rearrange("l (h a) -> (l h) a", a=1)),
                (aneg[:, 0:1], a_log.rearrange("l (h a) -> (l h) a", a=1)),
                (dskip[:], d_skip.rearrange("l h -> (l h)").partition_broadcast(P)),
                (wdt_raw[:, 0:KT * HEADS].rearrange("p (k h) -> p k h", k=KT),
                 win[:, :, COL_DT:COL_DT + HEADS]),
            ]
            loads += [(taps[:, j], conv_w[0, j].rearrange("(n p) -> p n", p=P)) for j in range(TAPS)]
            loads.append((taps[:, TAPS], conv_b[0].rearrange("(n p) -> p n", p=P)))
            assert len(loads) == N_LOADS
            for dst, src in loads:
                sp.dma_start(dst, src, allow_slow_non_contiguous=True).then_inc(params_in, 16)

            def load_unit(pos, k, src, shape):
                sp.wait_ge(unit_done.sem, unit_done.at(pos, k, back=RING))
                on_its_own(sp)
                dst = w_raw[k % RING][:].rearrange("p (a b) -> p a b", a=shape)
                sp.dma_start(dst, src).then_inc(w_in_s[k % RING].sem, 16)

            def cols(first, i, stride=P):
                return win[:, :, bass.ds(i * stride + first, P)]

            sp.dma_start(xin[:], xb[0]).then_inc(x_in.sem, 16)
            with sp.Fori(0, NB) as b:
                with sp.Fori(0, GROUPS) as g:
                    pos = Pos("G", b, g)
                    load_unit(pos, U_B, cols(COL_B, g), KT)
                    load_unit(pos, U_C, cols(COL_C, g), KT)
                    sp.wait_ge(mix_psum.sem, mix_psum.at(pos, 0, back=1))
                    sp.dma_start(mx_raw[:], one(mixw, g)).then_inc(mix_in.sem, 16)
                    for j in range(GT):
                        load_unit(pos, U_X + j, cols(COL_X + j * P, g, GC), KT)
                    for k in range(4):
                        load_unit(pos, U_Z + k, win[:, 2 * k:2 * k + 2, bass.ds(g * GC, GC)], 2)
                    for j in range(PT):
                        load_unit(pos, U_ZP + j, cols(COL_ZP + j * P, g, PG), KT)
                    for j in range(PT):
                        load_unit(pos, U_U + j, cols(COL_U + j * P, g, PG), KT)
                    for k in range(4):
                        load_unit(pos, U_A + k, one(wa, g)[:, :, 256 * k:256 * k + 256], GT)
                with sp.Fori(0, JP) as jj:
                    pos = Pos("J", b, jj)
                    for s in range(2):
                        load_unit(pos, 3 * s, cols(COL_GA + s * P, jj, 2 * P), KT)
                        load_unit(pos, 3 * s + 1, cols(COL_GB + s * P, jj, 2 * P), KT)
                        load_unit(pos, 3 * s + 2, wb[:, :, bass.ds(jj * 2 * P + s * P, P)], KT)
                pos = Pos("O", b, 0)
                def out_unit(k):
                    h, q = k // 4, k % 4
                    load_unit(pos, k, wo[:, 2 * q:2 * q + 2, 512 * h:512 * h + 512], 2)

                out_unit(0)
                out_unit(1)
                sp.wait_ge(merged.sem, merged.start_of(pos, "O"))
                on_its_own(sp)
                sp.wait_ge(unit_done.sem, unit_done.start_of(pos, "O"))
                on_its_own(sp)
                sp.dma_start(x2[:], xb[bass.ds(b, 1)].rearrange("b p c d -> (b p) c d"))\
                    .then_inc(x2_in.sem, 16)
                sp.dma_start(pin[:], pb[bass.ds(b, 1)].rearrange("b p c d -> (b p) c d"))\
                    .then_inc(pin_in.sem, 16)
                sp.dma_start(fg[:], final_g.partition_broadcast(P)).then_inc(fg_in.sem, 16)
                for k in range(2, 8):
                    out_unit(k)
                for h in range(2):
                    for k in range(4):
                        load_unit(pos, 8 + 5 * h + k, wg[:, 2 * k:2 * k + 2, 512 * h:512 * h + 512], 2)
                    load_unit(pos, 12 + 5 * h, wu[:, :, 512 * h:512 * h + 512], 2)
                sp.dma_start(xin[:], xb[bass.ds((b + 1) & (NB - 1), 1)].rearrange("b p c d -> (b p) c d"))\
                    .then_inc(x_in.sem, 16)
            last = Pos("P", NB, 0)
            for k in range(2):
                sp.wait_ge(unit_done.sem, unit_done.at(last, k, back=RING))
                sp.dma_start(w_raw[k][:].rearrange("p (a b) -> p a b", a=KT), win[:, :, 0:P])\
                    .then_inc(w_in_s[k].sem, 16)

        @block.gpsimd
        def _(pool):
            pool.memset(ident[:], 0.0).then_inc(consts, 1)
            pool.memset(cap[:], 0.0).then_inc(consts, 1)
            pool.memset(state[:], 0.0).then_inc(consts, 1)
            pool.memset(conv_halo[:], 0.0).then_inc(consts, 1)
            pool.memset(pool_halo[:], 0.0).then_inc(consts, 1)
            pool.iota(pos16[:], [[1, 16]], base=1, channel_multiplier=0,
                      allow_small_or_imprecise_dtypes=True).then_inc(consts, 1)
            pool.wait_ge(consts, 2)
            pool.affine_select(out=ident[:], in_=ident[:], compare_op=ALU.not_equal, fill=1.0,
                               base=0, pattern=[[-1, P]], channel_multiplier=1).then_inc(consts, 1)
            pool.affine_select(out=cap[:], in_=cap[:], compare_op=ALU.is_ge, fill=-1e30,
                               base=0, pattern=[[1, P]], channel_multiplier=-1).then_inc(consts, 1)
            for k in range(2):
                pool.wait_ge(w_hi_done.sem, k + 1)
                pool.tensor_tensor(w_lo[k][:], w_raw[k][:], w_hi[k][:].bitcast(F32), ALU.subtract)\
                    .then_inc(w_ready.sem, 1)
            per = 6
            with pool.Fori(0, NB * unit_done.total // per) as r:
                for k in range(per):
                    s = (k + 2) % RING
                    pool.wait_ge(w_hi_done.sem, r * per + (k + 3))
                    pool.tensor_tensor(w_lo[s][:], w_raw[s][:], w_hi[s][:].bitcast(F32), ALU.subtract)\
                        .then_inc(w_ready.sem, 1)

        @block.scalar
        def _(act):
            def split_ahead(pos, k):
                s = (k + 2) % RING
                in_s = w_in_s[s]
                act.wait_ge(in_s.sem, in_s.at(pos, (k + 2) // RING))
                act.wait_ge(unit_done.sem, unit_done.at(pos, k + 2, back=RING))
                act.activation(w_hi[s][:], w_raw[s][:], ACT.Copy).then_inc(w_hi_done.sem, 1)

            act.sem_inc(squares.sem, 1)
            act.sem_inc(y_squares.sem, 1)
            act.wait_ge(params_in, 16 * N_LOADS)
            act.activation(aneg[:, 1:2], aneg[:, 0:1], ACT.Exp).then_inc(a_exp, 1)
            first = Pos("G", 0, 0)
            for k in range(2):
                act.wait_ge(w_in_s[k].sem, 16)
                act.activation(w_hi[k][:], w_raw[k][:], ACT.Copy).then_inc(w_hi_done.sem, 1)

            def transposed_hi(pos, k, dst, i, scale):
                act.wait_ge(t_psum.sem, t_psum.at(pos, k))
                if scale is None:
                    act.activation(dst[:, i], bank[k_bank(pos, k)][:], ACT.Copy).then_inc(t_hi.sem, 1)
                else:
                    act.activation(dst[:, i], bank[k_bank(pos, k)][:], ACT.Copy,
                                   scale=scale[:, i:i + 1]).then_inc(t_hi.sem, 1)

            def sums_of_squares(pos, k0, src, ready):
                for c in range(NC):
                    ready(c)
                    act.wait_ge(squares.sem, squares.at(pos, k0 + c, back=1))
                    act.activation(junk[:], src[:, c], ACT.Square, accum_out=ss[:, c:c + 1])\
                        .then_inc(squares.sem, 1)

            with act.Fori(0, NB) as b:
                pos = Pos("P", b, 0)
                sums_of_squares(pos, 0, xin, lambda c: act.wait_ge(x_in.sem, x_in.at(pos, 0)) if c == 0 else None)
                act.wait_ge(meansq.sem, meansq.at(pos, 0))
                act.activation(rr[:], ss[:], ACT.Sqrt).then_inc(root.sem, 1)
                for k in range(KT):
                    transposed_hi(pos, k, h_hi, k, ng)
                act.wait_ge(dt_abs.sem, dt_abs.at(pos, 0))
                act.activation(dtw[1][:], dtw[1][:], ACT.Exp).then_inc(dt_exp.sem, 1)
                act.wait_ge(dt_full.sem, dt_full.at(pos, 0))
                act.dma_start(acs_dram[bass.ds(b, 1)].rearrange("b h t -> (b h) t"), dtw[6][:])\
                    .then_inc(acs_out.sem, 16)
                act.wait_ge(tok_full.sem, tok_full.at(pos, 0))
                act.activation(exp_acs[:], tok_acs[:], ACT.Exp).then_inc(acs_exp.sem, 1)
                with act.Fori(0, GROUPS) as g:
                    pos = Pos("G", b, g)

                    def load_abc(c):
                        act.wait_ge(seg_full.sem, seg_full.at(pos, c, back=2))
                        src = acs_dram[bass.ds(b, 1), bass.ds(g * HG, HG), c * P:(c + 1) * P]
                        act.dma_start(abc[c % 2][:], src.rearrange("b h t -> (b h) t").partition_broadcast(P))\
                            .then_inc(abc_in[c % 2].sem, 16)

                    act.wait_ge(acs_out.sem, acs_out.at(Pos("P", b, 0), 0))
                    load_abc(0)
                    load_abc(1)

                    def silu(t):
                        dst = bc[t][:] if t < 2 else xc[:, t - 2]
                        act.wait_ge(conv_done.sem, conv_done.at(pos, t))
                        act.activation(dst, dst, ACT.Silu).then_inc(silu_done.sem, 1)

                    for t in range(6):
                        split_ahead(pos, t)
                        act.wait_ge(conv_done.sem, conv_done.at(pos, t, back=2))
                        act.wait_ge(unit_done.sem, unit_done.at(pos, t))
                        act.activation(cbuf[t % 2][:, TAPS - 1:], bank[t % 2][:], ACT.Copy)\
                            .then_inc(cbuf_full.sem, 1)
                        if t:
                            silu(t - 1)
                    split_ahead(pos, 6)
                    silu(5)
                    for k in range(1, 4):
                        split_ahead(pos, U_Z + k)
                    act.wait_ge(unit_done.sem, unit_done.at(pos, U_Z + 3))
                    for c in range(NC):
                        act.activation(zs[:, c], bank[2 + c][:], ACT.Silu).then_inc(z_silu.sem, 1)
                    act.wait_ge(mix_in.sem, mix_in.at(pos, 0))
                    act.activation(mx_hi[:], mx_raw[:], ACT.Copy).then_inc(mx_hi_done.sem, 1)

                    def chunk_in(c):
                        act.wait_ge(y_gated.sem, y_gated.at(pos, c, back=1))
                        act.wait_ge(ssd_psum.sem, ssd_psum.at(pos, 3 * c + 2, back=3))
                        act.wait_ge(xt_psum.sem, xt_psum.at(pos, c))
                        act.activation(xt[:], bank[6][:], ACT.Copy).then_inc(xt_full.sem, 1)
                        act.wait_ge(bcb_psum.sem, bcb_psum.at(pos, c))
                        act.activation(bt[:], bank[7][:, 0:P], ACT.Copy).then_inc(bt_full.sem, 1)
                        act.activation(cbs[:], bank[7][:, P:2 * P], ACT.Copy).then_inc(bt_full.sem, 1)

                    def decays(c):
                        act.wait_ge(seg_full.sem, seg_full.at(pos, c))
                        act.activation(m[:], m[:], ACT.Exp).then_inc(decay.sem, 1)
                        if c + 2 < NC:
                            load_abc(c + 2)

                    def square(c):
                        act.wait_ge(y_gated.sem, y_gated.at(pos, c))
                        act.wait_ge(y_squares.sem, y_squares.at(pos, c, back=1))
                        act.activation(junk_y[:], zs[:, c], ACT.Square, accum_out=ssy[:, c:c + 1])\
                            .then_inc(y_squares.sem, 1)

                    def unit_out(k, dst, done):
                        split_ahead(pos, k)
                        act.wait_ge(unit_done.sem, unit_done.at(pos, k))
                        act.activation(dst, bank[k % 2][:], ACT.Copy).then_inc(done.sem, 1)

                    decays(0)
                    chunk_in(0)
                    unit_out(U_ZP, zps[:, 0], zp_full)
                    unit_out(U_ZP + 1, zps[:, 1], zp_full)
                    decays(1)
                    chunk_in(1)
                    split_ahead(pos, U_U)
                    act.wait_ge(unit_done.sem, unit_done.at(pos, U_U))
                    act.activation(ubuf[:, 16:], bank[0][:], ACT.Copy).then_inc(u_full.sem, 1)
                    square(0)
                    decays(2)
                    chunk_in(2)
                    act.wait_ge(pf_full.sem, pf_full.at(pos, 0))
                    act.activation(pl_hi[:, 0], pf[:], ACT.Copy).then_inc(pl_hi_done.sem, 1)
                    split_ahead(pos, U_U + 1)
                    act.wait_ge(pooled.sem, pooled.at(pos, 0))
                    act.wait_ge(unit_done.sem, unit_done.at(pos, U_U + 1))
                    act.activation(ubuf[:, 16:], bank[1][:], ACT.Copy).then_inc(u_full.sem, 1)
                    square(1)
                    decays(3)
                    chunk_in(3)
                    act.wait_ge(pf_full.sem, pf_full.at(pos, 1))
                    act.activation(pl_hi[:, 1], pf[:], ACT.Copy).then_inc(pl_hi_done.sem, 1)
                    square(2)
                    act.wait_ge(zp_full.sem, zp_full.at(pos, 1))
                    act.activation(zps[:], zps[:], ACT.Silu).then_inc(zp_silu.sem, 1)
                    square(3)
                    act.wait_ge(y_meansq.sem, y_meansq.at(pos, 0))
                    act.activation(rry[:], ssy[:], ACT.Sqrt).then_inc(y_root.sem, 1)
                    for j in range(PT):
                        act.wait_ge(yb_val.sem, yb_val.at(pos, j))
                        act.activation(one(yb_hi, g * PT + j), zps[:, j], ACT.Copy)\
                            .then_inc(yb_hi_done.sem, 1)
                    for k in range(GT):
                        act.wait_ge(yt_psum.sem, yt_psum.at(pos, k))
                        act.activation(ya_hi[:, k], bank[2 + k][:], ACT.Copy, scale=col(gn, g, k))\
                            .then_inc(ya_hi_done.sem, 1)
                    for k in range(4):
                        split_ahead(pos, U_A + k)
                with act.Fori(0, JP) as jj:
                    pos = Pos("J", b, jj)
                    for s in range(2):
                        j = jj * 2 + s
                        split_ahead(pos, 3 * s)
                        act.wait_ge(merged.sem, merged.at(pos, s, back=2))
                        act.wait_ge(unit_done.sem, unit_done.at(pos, 3 * s))
                        act.activation(sga[s][:], bank[3 * s][:], ACT.Sigmoid).then_inc(gates.sem, 1)
                        split_ahead(pos, 3 * s + 1)
                        act.wait_ge(unit_done.sem, unit_done.at(pos, 3 * s + 1))
                        act.activation(sgb[s][:], bank[3 * s + 1][:], ACT.Sigmoid).then_inc(gates.sem, 1)
                        split_ahead(pos, 3 * s + 2)
                        act.wait_ge(m_val.sem, m_val.at(pos, s))
                        act.activation(one(m_hi, j), sga[s][:], ACT.Copy).then_inc(m_hi_done.sem, 1)
                pos = Pos("O", b, 0)
                for k in range(8):
                    split_ahead(pos, k)
                for k in range(2):
                    transposed_hi(pos, k, p_hi, k, None)
                sums_of_squares(pos, 0, x2, lambda c: act.wait_ge(x2_sum.sem, x2_sum.at(pos, NC + c)))
                act.wait_ge(meansq.sem, meansq.at(pos, 0))
                act.activation(rr[:], ss[:], ACT.Sqrt).then_inc(root.sem, 1)
                for k in range(KT):
                    act.wait_ge(t_psum.sem, t_psum.at(pos, 2 + k))
                    act.activation(h_hi[:, k], bank[k][:], ACT.Copy, scale=pg[:, k:k + 1])\
                        .then_inc(t_hi.sem, 1)
                for h in range(2):
                    for k in range(4):
                        split_ahead(pos, 8 + 5 * h + k)
                    act.wait_ge(unit_done.sem, unit_done.at(pos, 8 + 5 * h + 3))
                    for c in range(NC):
                        if h:
                            act.wait_ge(x3_sum.sem, x3_sum.at(pos, c))
                        act.activation(sg[:, c], bank[2 + c][:], ACT.Sigmoid).then_inc(ple_gate.sem, 1)
                    split_ahead(pos, 8 + 5 * h + 4)
                sums_of_squares(pos, NC, x2, lambda c: act.wait_ge(x3_sum.sem, x3_sum.at(pos, NC + c)))
                act.wait_ge(meansq.sem, meansq.at(pos, 1))
                act.activation(rr[:], ss[:], ACT.Sqrt).then_inc(root.sem, 1)
                for c in range(NC):
                    act.wait_ge(out_full.sem, out_full.at(pos, c))
                    act.dma_start(ob[bass.ds(b, 1), c].rearrange("b p d -> (b p) d"), xs2[:, c])\
                        .then_inc(out_done.sem, 16)
                act.wait_ge(out_done.sem, out_done.at(pos, NC - 1))
            act.wait_ge(acs_out.sem, 16 * NB)

        @block.vector
        def _(dve):
            n_link = {"k": 0}

            def link(pos, ins):
                ins.then_inc(link_s.sem, 1)
                dve.wait_ge(link_s.sem, link_s.at(pos, n_link["k"]))
                n_link["k"] += 1

            def links_done(phase):
                assert n_link["k"] == link_s.n[phase], (phase, n_link["k"])
                n_link["k"] = 0

            for s in (conv_done, seg_full):
                dve.sem_inc(s.sem, 2)
            for s in (y_gated, state_new, pooled, mx_full, acc_added):
                dve.sem_inc(s.sem, 1)
            dve.sem_inc(merged.sem, 2)
            dve.wait_ge(params_in, 16 * N_LOADS)
            dve.wait_ge(consts, 8)
            dve.wait_ge(a_exp, 1)
            n = [0]

            def setup(ins):
                n[0] += 1
                ins.then_inc(setup_link, 1)
                dve.wait_ge(setup_link, n[0])

            for g in range(GROUPS):
                dve.memset(invw[:, g:g + 1], 1.0 / 2 ** (g + 1))
                setup(dve.tensor_scalar(inv16[:, g], pos16[:], float(2 ** (g + 1)), None, ALU.min))
            setup(dve.reciprocal(inv16[:].rearrange("p g n -> p (g n)"), inv16[:].rearrange("p g n -> p (g n)")))
            setup(dve.tensor_scalar(aneg[:, 1:2], aneg[:, 1:2], -1.0, None, ALU.mult))
            setup(dve.tensor_copy(wdt_raw[:, KT * HEADS:NDT], wdt_raw[:, 0:NDT - KT * HEADS]))
            setup(dve.tensor_copy(wdt_hi[:], wdt_raw[:]))
            dve.tensor_tensor(wdt_lo[:], wdt_raw[:], wdt_hi[:].bitcast(F32), ALU.subtract)\
                .then_inc(setup_done, 1)
            dve.wait_ge(setup_done, 1)

            def inv_rms(pos, k, sums, mean, roots, inv, width, sq, sqk, rt, rtk):
                dve.wait_ge(sq.sem, sq.at(pos, sqk))
                dve.tensor_scalar(sums[:], sums[:], 1.0 / width, EPS, ALU.mult, ALU.add)\
                    .then_inc(mean.sem, 1)
                dve.wait_ge(rt.sem, rt.at(pos, rtk))
                link(pos, dve.reciprocal(inv[:], roots[:]))

            def transposed_lo(pos, k, hi, lo, i, scale):
                dve.wait_ge(t_hi.sem, t_hi.at(pos, k))
                src = bank[k_bank(pos, k)][:]
                if scale is None:
                    dve.tensor_tensor(lo[:, i], src, hi[:, i].bitcast(F32), ALU.subtract)\
                        .then_inc(t_lo.sem, 1)
                else:
                    dve.scalar_tensor_tensor(lo[:, i], src, scale[:, i:i + 1], hi[:, i].bitcast(F32),
                                             ALU.mult, ALU.subtract).then_inc(t_lo.sem, 1)

            with dve.Fori(0, NB) as b:
                pos = Pos("P", b, 0)
                inv_rms(pos, 0, ss, meansq, rr, rq, DM, squares, NC - 1, root, 0)
                for c in range(NC):
                    dve.tensor_scalar(xs[:, c], xin[:, c], rq[:, c:c + 1], None, ALU.mult)\
                        .then_inc(xs_full.sem, 1)
                dve.memset(a_acc[:], 0.0).then_inc(acc_zero.sem, 1)
                for k in range(KT):
                    transposed_lo(pos, k, h_hi, h_lo, k, ng)
                v, e, r_, s_, s2, q_, acs = (t[:] for t in dtw)
                dve.wait_ge(dt_psum.sem, dt_psum.at(pos, 0))
                link(pos, dve.tensor_scalar(v, bank[0][0:HEADS, :], dtb[:, 0:1], None, ALU.add))
                dve.scalar_tensor_tensor(e, v, -1.0, v, ALU.mult, ALU.min).then_inc(dt_abs.sem, 1)
                dve.wait_ge(dt_exp.sem, dt_exp.at(pos, 0))
                link(pos, dve.tensor_scalar(r_, e, 2.0, None, ALU.add))
                link(pos, dve.reciprocal(r_, r_))
                link(pos, dve.tensor_tensor(s_, e, r_, ALU.mult))
                link(pos, dve.tensor_tensor(s2, s_, s_, ALU.mult))
                link(pos, dve.tensor_scalar(q_, s2, ATANH[-1], None, ALU.mult))
                for coef in reversed(ATANH[:-1]):
                    link(pos, dve.scalar_tensor_tensor(q_, q_, coef, s2, ALU.add, ALU.mult))
                link(pos, dve.scalar_tensor_tensor(q_, q_, 1.0, s_, ALU.add, ALU.mult))
                link(pos, dve.tensor_scalar(v, v, 0.0, None, ALU.max))
                link(pos, dve.scalar_tensor_tensor(v, q_, 2.0, v, ALU.mult, ALU.add))
                link(pos, dve.tensor_scalar(r_, v, aneg[:, 1:2], None, ALU.mult))
                link(pos, dve.memset(e, 0.0))
                for c in range(NC):
                    part = slice(c * P, (c + 1) * P)
                    scan = dve.tensor_tensor_scan(acs[:, part], r_[:, part], e[:, part], 0.0,
                                                  ALU.add, ALU.add)
                scan.then_inc(dt_full.sem, 1)
                dve.wait_ge(tok_psum.sem, tok_psum.at(pos, 0))
                dve.tensor_copy(tok_dt[:].rearrange("p c h -> p (c h)"), bank[1][:, 0:NC * HEADS])
                dve.tensor_copy(tok_acs[:].rearrange("p c h -> p (c h)"),
                                bank[1][:, NC * HEADS:2 * NC * HEADS]).then_inc(tok_full.sem, 1)
                dve.wait_ge(acs_exp.sem, acs_exp.at(pos, 0))
                on_its_own(dve)
                links_done("P")
                with dve.Fori(0, GROUPS) as g:
                    pos = Pos("G", b, g)
                    dve.wait_ge(acc_added.sem, acc_added.at(pos, 0, back=1))
                    for t in range(6):
                        buf = cbuf[t % 2]
                        dst = bc[t][:] if t < 2 else xc[:, t - 2]
                        halo = conv_halo[:, bass.ds(g, 1), t, :].rearrange("p a n -> p (a n)")
                        tile = g + (DI // P + GROUPS * t) if t < 2 else g * GT + (t - 2)
                        tap = [taps[:, j, bass.ds(tile, 1)] for j in range(TAPS + 1)]
                        dve.wait_ge(cbuf_full.sem, cbuf_full.at(pos, t))
                        link(pos, dve.tensor_copy(buf[:, 0:TAPS - 1], halo))
                        link(pos, dve.tensor_scalar(dst, buf[:, 0:T], tap[0], tap[TAPS],
                                                    ALU.mult, ALU.add))
                        for j in range(1, TAPS - 1):
                            link(pos, dve.scalar_tensor_tensor(dst, buf[:, j:j + T], tap[j], dst,
                                                               ALU.mult, ALU.add))
                        dve.scalar_tensor_tensor(dst, buf[:, TAPS - 1:TAPS - 1 + T], tap[TAPS - 1],
                                                 dst, ALU.mult, ALU.add)
                        dve.tensor_copy(halo, buf[:, T:T + TAPS - 1]).then_inc(conv_done.sem, 1)

                    seg = m[:, 0:MX].rearrange("p (h l) -> p h l", h=HG)
                    to_end = m[:, MX:MX + HG]
                    chunk_decay = m[:, MX + HG:MX + 2 * HG]

                    def segments(c):
                        acs_s = tok_acs[:, c, bass.ds(g * HG, HG)]
                        last = abc[c % 2][:, :, P - 1]
                        dve.wait_ge(abc_in[c % 2].sem, abc_in[c % 2].at(pos, c // 2))
                        dve.wait_ge(ssd_psum.sem, ssd_psum.at(pos, 3 * c, back=3))
                        dve.tensor_tensor(to_end, last, acs_s, ALU.subtract)
                        dve.tensor_copy(chunk_decay, last)
                        link(pos, dve.tensor_tensor(seg, abc[c % 2][:], per_head(acs_s, P), ALU.subtract))
                        dve.tensor_tensor(seg, seg, cap[:].unsqueeze(1).to_broadcast([P, HG, P]), ALU.min)\
                            .then_inc(seg_full.sem, 1)

                    def inputs(c):
                        dt_s = tok_dt[:, c, bass.ds(g * HG, HG)]
                        dve.wait_ge(xt_full.sem, xt_full.at(pos, c))
                        link(pos, dve.tensor_tensor(heads(xdt[:]), heads(xt[:]), per_head(dt_s, HD), ALU.mult))
                        link(pos, dve.tensor_tensor(heads(xt[:]), heads(xt[:]),
                                                    per_head(dskip[:, bass.ds(g * HG, HG)], HD), ALU.mult))
                        dve.wait_ge(decay.sem, decay.at(pos, c))
                        dve.tensor_tensor(heads(xdd[:]), heads(xdt[:]), per_head(to_end, HD), ALU.mult)\
                            .then_inc(xdt_full.sem, 1)
                        dve.wait_ge(bt_full.sem, bt_full.at(pos, 2 * c + 1))
                        dve.tensor_tensor(seg, seg, cbs[:].unsqueeze(1).to_broadcast([P, HG, P]), ALU.mult)\
                            .then_inc(m_full.sem, 1)

                    def outputs(c):
                        ea = exp_acs[:, c, bass.ds(g * HG, HG)]
                        st = one(state, g)
                        dve.wait_ge(ssd_psum.sem, ssd_psum.at(pos, 3 * c + 1))
                        link(pos, dve.tensor_tensor(heads(xdt[:]), heads(bank[3][:]), per_head(ea, HD), ALU.mult))
                        link(pos, dve.tensor_tensor(xdt[:], xdt[:], bank[2][:], ALU.add))
                        link(pos, dve.tensor_tensor(xdt[:], xdt[:], xt[:], ALU.add))
                        if c == 0:
                            dve.wait_ge(z_silu.sem, z_silu.at(pos, NC - 1))
                        dve.tensor_tensor(zs[:, c], xdt[:], zs[:, c], ALU.mult).then_inc(y_gated.sem, 1)
                        dve.wait_ge(ssd_psum.sem, ssd_psum.at(pos, 3 * c + 2))
                        link(pos, dve.tensor_tensor(heads(st), heads(st), per_head(chunk_decay, HD), ALU.mult))
                        dve.tensor_tensor(st, st, bank[4][:], ALU.add).then_inc(state_new.sem, 1)
                        dve.wait_ge(state_new.sem, state_new.at(pos, c))

                    def pool_tile(j):
                        halo = pool_halo[:, bass.ds(g, 1), j, :].rearrange("p a n -> p (a n)")
                        inv = one(inv16, g)
                        dve.wait_ge(u_full.sem, u_full.at(pos, j))
                        link(pos, dve.tensor_copy(ubuf[:, 0:16], halo))
                        link(pos, dve.tensor_tensor_scan(cs[:], ubuf[:], ubuf[:], 0.0, ALU.add, ALU.bypass))
                        on_its_own(dve)
                        if j:
                            dve.wait_ge(pooled.sem, pooled.at(pos, j - 1))
                            on_its_own(dve)
                        link(pos, dve.tensor_tensor(pf[:], cs[:, 16:16 + T], cs[:, bass.ds(16 - (2 << g), T)],
                                                    ALU.subtract))
                        dve.scalar_tensor_tensor(pf[:, 16:T], pf[:, 16:T], invw[:, bass.ds(g, 1)],
                                                 ubuf[:, 32:T + 16], ALU.mult, ALU.subtract)
                        dve.tensor_copy(halo, ubuf[:, T:T + 16])
                        link(pos, dve.tensor_tensor(pf[:, 0:16], pf[:, 0:16], inv, ALU.mult))
                        dve.tensor_tensor(pf[:, 0:16], pf[:, 0:16], ubuf[:, 16:32], ALU.subtract)\
                            .then_inc(pf_full.sem, 1)
                        dve.wait_ge(pl_hi_done.sem, pl_hi_done.at(pos, j))
                        dve.tensor_tensor(pl_lo[:, j], pf[:], pl_hi[:, j].bitcast(F32), ALU.subtract)\
                            .then_inc(pooled.sem, 1)

                    segments(0)
                    inputs(0)
                    outputs(0)
                    segments(1)
                    dve.wait_ge(mx_hi_done.sem, mx_hi_done.at(pos, 0))
                    dve.tensor_tensor(mx_lo[:], mx_raw[:], mx_hi[:].bitcast(F32), ALU.subtract)\
                        .then_inc(mx_full.sem, 1)
                    inputs(1)
                    outputs(1)
                    segments(2)
                    pool_tile(0)
                    inputs(2)
                    outputs(2)
                    segments(3)
                    inputs(3)
                    pool_tile(1)
                    outputs(3)
                    inv_rms(pos, 0, ssy, y_meansq, rry, rqy, GC, y_squares, NC - 1, y_root, 0)
                    for c in range(NC):
                        dve.tensor_scalar(zs[:, c], zs[:, c], rqy[:, c:c + 1], None, ALU.mult)\
                            .then_inc(y_normed.sem, 1)
                    dve.wait_ge(zp_silu.sem, zp_silu.at(pos, 0))
                    for j in range(PT):
                        dve.wait_ge(mix_psum.sem, mix_psum.at(pos, j))
                        dve.tensor_scalar(pf[:], bank[j][:], col(mixb, g, j), col(pscale, g, j),
                                          ALU.add, ALU.mult).then_inc(mix_read.sem, 1)
                        dve.wait_ge(mix_read.sem, mix_read.at(pos, j))
                        dve.tensor_tensor(zps[:, j], zps[:, j], pf[:], ALU.mult).then_inc(yb_val.sem, 1)
                        dve.wait_ge(yb_hi_done.sem, yb_hi_done.at(pos, j))
                        dve.tensor_tensor(one(yb_lo, g * PT + j), zps[:, j],
                                          one(yb_hi, g * PT + j).bitcast(F32), ALU.subtract)\
                            .then_inc(yb_full.sem, 1)
                    for k in range(GT):
                        dve.wait_ge(ya_hi_done.sem, ya_hi_done.at(pos, k))
                        dve.scalar_tensor_tensor(ya_lo[:, k], bank[2 + k][:], col(gn, g, k),
                                                 ya_hi[:, k].bitcast(F32), ALU.mult, ALU.subtract)\
                            .then_inc(ya_full.sem, 1)
                    for j in range(KT):
                        dve.wait_ge(unit_done.sem, unit_done.at(pos, U_A + j // 2))
                        dve.tensor_tensor(a_acc[:, j], a_acc[:, j], bank[acc_bank(j)][:], ALU.add)\
                            .then_inc(acc_added.sem, 1)
                    links_done("G")
                with dve.Fori(0, JP) as jj:
                    pos = Pos("J", b, jj)
                    for s in range(2):
                        j = jj * 2 + s
                        dve.wait_ge(gates.sem, gates.at(pos, 2 * s + 1))
                        link(pos, dve.tensor_tensor(sga[s][:], sga[s][:], one(a_acc, j), ALU.mult))
                        dve.wait_ge(unit_done.sem, unit_done.at(pos, 3 * s + 2))
                        link(pos, dve.tensor_tensor(sgb[s][:], sgb[s][:], bank[3 * s + 2][:], ALU.mult))
                        dve.tensor_tensor(sga[s][:], sga[s][:], sgb[s][:], ALU.add).then_inc(m_val.sem, 1)
                        dve.wait_ge(m_hi_done.sem, m_hi_done.at(pos, s))
                        dve.tensor_tensor(one(m_lo, j), sga[s][:], one(m_hi, j).bitcast(F32), ALU.subtract)\
                            .then_inc(merged.sem, 1)
                    links_done("J")
                pos = Pos("O", b, 0)
                dve.wait_ge(x2_in.sem, x2_in.at(pos, 0))
                for h in range(2):
                    dve.wait_ge(unit_done.sem, unit_done.at(pos, 4 * h + 3))
                    for c in range(NC):
                        part = x2[:, c, 512 * h:512 * h + 512]
                        dve.tensor_tensor(part, part, bank[half_bank(h, c)][:], ALU.add)\
                            .then_inc(x2_sum.sem, 1)
                for k in range(2):
                    transposed_lo(pos, k, p_hi, p_lo, k, None)
                inv_rms(pos, 0, ss, meansq, rr, rq, DM, squares, NC - 1, root, 0)
                for c in range(NC):
                    dve.tensor_scalar(xs2[:, c], x2[:, c], rq[:, c:c + 1], None, ALU.mult)\
                        .then_inc(xs_full.sem, 1)
                for k in range(KT):
                    dve.wait_ge(t_hi.sem, t_hi.at(pos, 2 + k))
                    dve.scalar_tensor_tensor(h_lo[:, k], bank[k][:], pg[:, k:k + 1],
                                             h_hi[:, k].bitcast(F32), ALU.mult, ALU.subtract)\
                        .then_inc(t_lo.sem, 1)
                for h in range(2):
                    dve.wait_ge(unit_done.sem, unit_done.at(pos, 8 + 5 * h + 4))
                    for c in range(NC):
                        part = x2[:, c, 512 * h:512 * h + 512]
                        dve.wait_ge(ple_gate.sem, ple_gate.at(pos, NC * h + c))
                        if h:
                            dve.wait_ge(x3_sum.sem, x3_sum.at(pos, c))
                        dve.tensor_tensor(xs2[:, c, 0:512], sg[:, c], bank[half_bank(1, c)][:], ALU.mult)\
                            .then_inc(up_gated.sem, 1)
                        dve.wait_ge(up_gated.sem, up_gated.at(pos, NC * h + c))
                        dve.tensor_tensor(part, part, xs2[:, c, 0:512], ALU.add).then_inc(x3_sum.sem, 1)
                inv_rms(pos, 1, ss, meansq, rr, rq, DM, squares, 2 * NC - 1, root, 1)
                dve.wait_ge(fg_in.sem, fg_in.at(pos, 0))
                for c in range(NC):
                    dve.scalar_tensor_tensor(xs2[:, c], x2[:, c], rq[:, c:c + 1], fg[:], ALU.mult, ALU.mult)\
                        .then_inc(out_full.sem, 1)
                for g in range(GROUPS):
                    ins = dve.memset(inv16[:, g], 1.0 / 2 ** (g + 1))
                link(pos, ins)
                on_its_own(dve)
                links_done("O")

        @block.tensor
        def _(pe):
            def three(out_, lhs, rhs, start, stop, last=None):
                (lh, ll), (rh, rl) = lhs, rhs
                pe.matmul(out_, lh, rh, start=start, stop=False)
                pe.matmul(out_, lh, rl, start=False, stop=False)
                return pe.matmul(out_, ll, rh, start=False, stop=stop)

            def unit(k, parts):
                s = k % RING
                return [w[s][:].rearrange("p (a b) -> p a b", a=parts) for w in (w_hi, w_lo)]

            def wait_unit(pos, k):
                pe.wait_ge(w_ready.sem, w_ready.at(pos, k))

            def stationary_unit(pos, k, dst, moving, parts=KT):
                wait_unit(pos, k)
                hi, lo = unit(k, parts)
                for i in range(parts):
                    last = three(dst, (hi[:, i], lo[:, i]), (moving[0][:, i], moving[1][:, i]),
                                 i == 0, i == parts - 1)
                last.then_inc(unit_done.sem, 1)

            def moving_unit(pos, k, dsts, still, k0, ktiles):
                wait_unit(pos, k)
                hi, lo = unit(k, 2)
                for i in range(2):
                    kt = k0 + i
                    for c in range(NC):
                        part = slice(c * P, (c + 1) * P)
                        last = three(dsts[c][:], (still[0][:, kt, part], still[1][:, kt, part]),
                                     (hi[:, i], lo[:, i]), kt == 0, kt == ktiles - 1)
                last.then_inc(unit_done.sem, 1)

            def transposes(dst, src, first):
                for c in range(NC):
                    last = pe.transpose(dst[:, c * P:(c + 1) * P], src[:, c, first:first + P], ident[:])
                return last

            H = (h_hi, h_lo)
            pe.sem_inc(unit_done.sem, RING)
            pe.sem_inc(ssd_psum.sem, 3)
            pe.sem_inc(mix_psum.sem, 1)
            pe.wait_ge(consts, 8)
            pe.wait_ge(setup_done, 1)
            with pe.Fori(0, NB) as b:
                pos = Pos("P", b, 0)
                pe.wait_ge(xs_full.sem, xs_full.at(pos, NC - 1))
                for k in range(KT):
                    transposes(bank[k], xs, k * P).then_inc(t_psum.sem, 1)
                pe.wait_ge(t_lo.sem, t_lo.at(pos, KT - 1))
                for k in range(KT):
                    last = three(bank[0][:], (wdt_hi[:, k * HEADS:k * HEADS + P], wdt_lo[:, k * HEADS:k * HEADS + P]),
                                 (h_hi[:, k], h_lo[:, k]), k == 0, k == KT - 1)
                last.then_inc(dt_psum.sem, 1)
                pe.wait_ge(dt_full.sem, dt_full.at(pos, 0))
                on_its_own(pe)
                for n_, src in enumerate((dtw[0], dtw[6])):
                    for c in range(NC):
                        at = (n_ * NC + c) * HEADS
                        last = pe.transpose(bank[1][:, at:at + HEADS], src[:, c * P:(c + 1) * P],
                                            ident[0:HEADS, 0:HEADS])
                last.then_inc(tok_psum.sem, 1)
                pe.wait_ge(tok_full.sem, tok_full.at(pos, 0))
                on_its_own(pe)
                with pe.Fori(0, GROUPS) as g:
                    pos = Pos("G", b, g)
                    pe.wait_ge(acc_added.sem, acc_added.at(pos, 0, back=1))
                    for t in range(6):
                        if t >= 2:
                            pe.wait_ge(cbuf_full.sem, cbuf_full.at(pos, t - 2))
                        stationary_unit(pos, t, bank[t % 2][:], H)
                    for k in range(4):
                        moving_unit(pos, U_Z + k, bank[2:6], H, 2 * k, KT)

                    def chunk_in(c):
                        part = slice(c * P, (c + 1) * P)
                        if c == 0:
                            pe.wait_ge(silu_done.sem, silu_done.at(pos, 5))
                        else:
                            pe.wait_ge(bt_full.sem, bt_full.at(pos, 2 * c - 1))
                        for j in range(GT):
                            last = pe.transpose(bank[6][:, j * P:(j + 1) * P], xc[:, j, part], ident[:])
                        last.then_inc(xt_psum.sem, 1)
                        pe.transpose(bank[7][:, 0:P], bc[0][:, part], ident[:])
                        pe.matmul(bank[7][:, P:2 * P], bc[0][:, part], bc[1][:, part], start=True, stop=True)\
                            .then_inc(bcb_psum.sem, 1)

                    def chunk_out(c):
                        part = slice(c * P, (c + 1) * P)
                        pe.wait_ge(m_full.sem, m_full.at(pos, c))
                        if c == 0:
                            pe.wait_ge(z_silu.sem, z_silu.at(pos, NC - 1))
                        pe.wait_ge(state_new.sem, state_new.at(pos, c, back=1))
                        for h in range(HG):
                            cols_ = slice(h * HD, (h + 1) * HD)
                            last = pe.matmul(bank[2][:, cols_], m[:, h * P:(h + 1) * P], xdt[:, cols_],
                                             start=True, stop=True)
                        last.then_inc(ssd_psum.sem, 1)
                        pe.matmul(bank[3][:], bc[1][:, part], one(state, g), start=True, stop=True)\
                            .then_inc(ssd_psum.sem, 1)
                        pe.matmul(bank[4][:], bt[:], xdd[:], start=True, stop=True).then_inc(ssd_psum.sem, 1)

                    chunk_in(0)
                    for k in range(PT):
                        pe.wait_ge(cbuf_full.sem, cbuf_full.at(pos, 4 + k))
                        stationary_unit(pos, U_ZP + k, bank[k][:], H)
                    chunk_out(0)
                    chunk_in(1)
                    pe.wait_ge(zp_full.sem, zp_full.at(pos, 0))
                    stationary_unit(pos, U_U, bank[0][:], H)
                    chunk_out(1)
                    chunk_in(2)
                    chunk_out(2)
                    chunk_in(3)
                    pe.wait_ge(zp_full.sem, zp_full.at(pos, 1))
                    stationary_unit(pos, U_U + 1, bank[1][:], H)
                    chunk_out(3)
                    pe.wait_ge(pooled.sem, pooled.at(pos, PT - 1))
                    pe.wait_ge(mx_full.sem, mx_full.at(pos, 0))
                    for j in range(PT):
                        pe.wait_ge(u_full.sem, u_full.at(pos, j))
                        cols_ = slice(j * P, (j + 1) * P)
                        for i in range(PT):
                            last = three(bank[j][:], (mx_hi[:, i, cols_], mx_lo[:, i, cols_]),
                                         (pl_hi[:, i], pl_lo[:, i]), i == 0, i == PT - 1)
                        last.then_inc(mix_psum.sem, 1)
                    pe.wait_ge(y_normed.sem, y_normed.at(pos, NC - 1))
                    for k in range(GT):
                        transposes(bank[2 + k], zs, k * P).then_inc(yt_psum.sem, 1)
                    pe.wait_ge(ya_full.sem, ya_full.at(pos, GT - 1))
                    pe.wait_ge(mix_read.sem, mix_read.at(pos, PT - 1))
                    pe.wait_ge(bt_full.sem, bt_full.at(pos, 2 * NC - 1))
                    for q in range(4):
                        if q >= 2:
                            pe.wait_ge(acc_added.sem, acc_added.at(pos, 2 * q - 3))
                        wait_unit(pos, U_A + q)
                        hi, lo = unit(U_A + q, GT)
                        for s in range(2):
                            cols_ = slice(s * P, (s + 1) * P)
                            for i in range(GT):
                                last = three(bank[acc_bank(2 * q + s)][:], (hi[:, i, cols_], lo[:, i, cols_]),
                                             (ya_hi[:, i], ya_lo[:, i]), i == 0, i == GT - 1)
                        last.then_inc(unit_done.sem, 1)
                last_g = Pos("G", b, GROUPS - 1)
                pe.wait_ge(acc_added.sem, acc_added.at(last_g, KT - 1))
                on_its_own(pe)
                with pe.Fori(0, JP) as jj:
                    pos = Pos("J", b, jj)
                    for s in range(2):
                        pe.wait_ge(merged.sem, merged.at(pos, s, back=2))
                        stationary_unit(pos, 3 * s, bank[3 * s][:], H)
                        stationary_unit(pos, 3 * s + 1, bank[3 * s + 1][:], H)
                        stationary_unit(pos, 3 * s + 2, bank[3 * s + 2][:], (yb_hi, yb_lo))
                pos = Pos("O", b, 0)
                pe.wait_ge(merged.sem, merged.start_of(pos, "O"))
                for h in range(2):
                    for k in range(4):
                        moving_unit(pos, 4 * h + k, [bank[half_bank(h, c)] for c in range(NC)],
                                    (m_hi, m_lo), 2 * k, KT)
                pe.wait_ge(x2_sum.sem, x2_sum.at(pos, NC - 1))
                pe.wait_ge(pin_in.sem, pin_in.at(pos, 0))
                for k in range(2):
                    transposes(bank[k_bank(pos, k)], pin, k * P).then_inc(t_psum.sem, 1)
                pe.wait_ge(xs_full.sem, xs_full.at(pos, NC - 1))
                pe.wait_ge(t_lo.sem, t_lo.at(pos, 1))
                for k in range(KT):
                    transposes(bank[k], xs2, k * P).then_inc(t_psum.sem, 1)
                pe.wait_ge(t_lo.sem, t_lo.at(pos, KT + 1))
                for h in range(2):
                    if h:
                        pe.wait_ge(ple_gate.sem, ple_gate.at(pos, NC - 1))
                    for k in range(4):
                        moving_unit(pos, 8 + 5 * h + k, bank[2:6], H, 2 * k, KT)
                    if h:
                        pe.wait_ge(x3_sum.sem, x3_sum.at(pos, NC - 1))
                    moving_unit(pos, 12 + 5 * h, [bank[i] for i in (0, 1, 6, 7)], (p_hi, p_lo), 0, 2)


INPUTS = ["x", "p", "norm_g", "w_in", "conv_w", "conv_b", "dt_bias", "a_log", "d_skip", "gnorm_g",
          "pool_mix_w", "pool_mix_b", "pool_scale", "w_branch_a", "w_branch_b", "w_out",
          "ple_norm_g", "w_ple_gate", "w_ple_up", "final_g"]


def kernel(**inputs):
    import concourse.bacc as bacc
    from concourse.bass_utils import run_bass_kernel_spmd

    nc = bacc.Bacc("TRN2", target_bir_lowering=False, num_devices=1)
    arrays, args = {}, []
    for name in INPUTS:
        a = np.ascontiguousarray(inputs[name])
        arrays[f"in_{name}"] = a
        args.append(nc.dram_tensor(f"in_{name}", a.shape, mybir.dt.from_np(a.dtype),
                                   kind="ExternalInput").ap())
    args.append(nc.dram_tensor("out", (1, SEQ, DM), F32, kind="ExternalOutput").ap())
    build(nc, *args)
    result = run_bass_kernel_spmd(nc, [arrays], core_ids=[0])
    return result.results[0]["out"]
```

```python
from collections import namedtuple
from contextlib import ExitStack

import concourse.bass as bass
import numpy as np
from concourse import mybir
from concourse.alu_op_type import AluOpType as ALU

ACT = mybir.ActivationFunctionType
F32 = mybir.dt.float32
F32R = mybir.dt.float32r
BF16 = mybir.dt.bfloat16

P = 128
SEQ, DM, PLE = 2048, 1024, 256
DI = 2 * DM
HEADS, HD, GROUPS, NS = 32, 64, 4, 128
HG = HEADS // GROUPS
GC = DI // GROUPS
TAPS = 4
T = 512
NB = SEQ // T
NC = T // P
KT = DM // P
GT = GC // P
PG = DM // GROUPS
PT = PG // P
EPS = 1e-6
COL_Z, COL_X = 0, DI
COL_B = COL_X + DI
COL_C = COL_B + GROUPS * NS
COL_DT = COL_C + GROUPS * NS
COL_U = COL_DT + HEADS
COL_ZP = COL_U + DM
COL_GA = COL_ZP + DM
COL_GB = COL_GA + DM
ATANH = [1.0 / (2 * k + 1) for k in range(1, 8)]

UW = 1024
RING = 3
U_B, U_C, U_X, U_ZP, U_U, U_Z, U_A = 0, 1, 2, 6, 8, 10, 14
J_UNITS = 6
U_UP0, U_GATE, U_UP1 = 8, 9, 17
PHASES = "FGWJO"
TRIPS = {"F": 1, "G": GROUPS - 1, "W": 1, "J": KT // 2, "O": 1}
UNITS = {"F": U_A, "G": 18, "W": 4, "J": J_UNITS, "O": 18}
UNIT_0 = {}
_n = 0
for _ph in PHASES:
    UNIT_0[_ph] = _n
    _n += UNITS[_ph] * TRIPS[_ph]
BLOCK_UNITS = _n
assert BLOCK_UNITS % (2 * RING) == 0 and UNITS["G"] % RING == 0 and UNITS["J"] % RING == 0
N_LOADS = 9 + TAPS + 1
DT_BANK, TOK_BANK = 2, 6


def half_bank(h, c):
    return 4 * h + c


def acc_bank(j):
    return (0, 1, 5)[j % 3]


Pos = namedtuple("Pos", "phase b i")


def slot(pos, k):
    return (UNIT_0[pos.phase] + k) % RING


def loaded_at(pos, k):
    value = pos.b * (16 * BLOCK_UNITS // RING) + 16 * ((UNIT_0[pos.phase] + k) // RING + 1)
    if TRIPS[pos.phase] > 1:
        value = value + pos.i * (16 * UNITS[pos.phase] // RING)
    return value


class Signal:

    def __init__(self, sem, credit=0, step=1, pre=0, **turns):
        self.sem, self.credit, self.step, self.pre = sem, credit, step, pre
        self.n = {ph: turns.get(ph, 0) for ph in PHASES}
        self.total = sum(self.n[ph] * TRIPS[ph] for ph in PHASES)

    def before(self, phase):
        n = self.credit + self.pre
        for ph in PHASES:
            if ph == phase:
                break
            n += self.n[ph] * TRIPS[ph]
        return n

    def at(self, pos, k, back=0):
        if pos.phase == "PRE":
            return self.step * (self.credit + k + 1 - back)
        value = pos.b * (self.step * self.total) + self.step * (self.before(pos.phase) + k + 1 - back)
        if TRIPS[pos.phase] > 1 and self.n[pos.phase]:
            value = value + pos.i * (self.step * self.n[pos.phase])
        return value

    def start_of(self, pos, phase):
        return pos.b * (self.step * self.total) + self.step * self.before(phase)


def build(nc, x, p, norm_g, w_in, conv_w, conv_b, dt_bias, a_log, d_skip, gnorm_g, pool_mix_w,
          pool_mix_b, pool_scale, w_branch_a, w_branch_b, w_out, ple_norm_g, w_ple_gate,
          w_ple_up, final_g, out):
    ctx = ExitStack()
    with ctx:
        base = [16512]

        def sb(name, shape, dt=F32, at=None):
            size = int(np.prod(shape[1:])) * (2 if dt == BF16 else 4)
            size = (size + 31) // 32 * 32
            if at is None:
                at = base[0]
                base[0] += size
            assert at + size <= nc.sbuf_usable_end, (name, at + size)
            return nc.alloc_sbuf_tensor_at(name, shape, dt, offset=at)

        KB = 1024
        h_hi = sb("h_hi", [P, KT, T], F32R)
        h_lo = sb("h_lo", [P, KT, T], F32R)
        wring = base[0]
        w_hi = [sb(f"w_hi{s}", [P, UW], F32R) for s in range(RING)]
        w_raw = [sb(f"w_raw{s}", [P, UW]) for s in range(RING)]
        w_lo = [sb(f"w_lo{s}", [P, UW], F32R, at=wring + (RING + s) * UW * 4) for s in range(RING)]
        state = sb("state", [P, GROUPS, GC])
        yb_at = base[0]
        yb_hi = sb("yb_hi", [P, KT, T], F32R)
        yb_lo = sb("yb_lo", [P, KT, T], F32R)
        acc_at = base[0]
        a_acc = sb("a_acc", [P, KT, T])
        ya_at = base[0]
        ya_hi = sb("ya_hi", [P, GT, T], F32R)
        ya_lo = sb("ya_lo", [P, GT, T], F32R)
        zps = sb("zps", [P, KT, T], at=yb_at)
        NDT = (KT + 3) * HEADS
        wdt_hi = sb("wdt_hi", [P, NDT], F32R)
        wdt_lo = sb("wdt_lo", [P, NDT], F32R)
        conv_halo = sb("conv_halo", [P, GROUPS, 6, TAPS - 1])
        pool_halo = sb("pool_halo", [P, GROUPS, PT, 16])
        ident = sb("ident", [P, P])
        cap = sb("cap", [P, P])
        tok_dt = sb("tok_dt", [P, NC, HEADS])
        tok_acs = sb("tok_acs", [P, NC, HEADS])
        exp_acs = sb("exp_acs", [P, NC, HEADS])
        taps = sb("taps", [P, TAPS + 1, (DI + 2 * GROUPS * NS) // P])
        ng = sb("ng", [P, KT])
        pg = sb("pg", [P, KT])
        gn = sb("gn", [P, GROUPS, GT])
        mixb = sb("mixb", [P, GROUPS, PT])
        pscale = sb("pscale", [P, GROUPS, PT])
        dskip = sb("dskip", [P, HEADS])
        dtb = sb("dtb", [HEADS, 1])
        aneg = sb("aneg", [HEADS, 2])
        inv16 = sb("inv16", [P, GROUPS, 16])
        invw = sb("invw", [P, GROUPS])
        ssx, rrx, rqx = (sb(n, [P, NC]) for n in ("ssx", "rrx", "rqx"))
        ss = sb("ss", [P, 2, NC])
        ms, rr, rq = (sb(n, [P, NC]) for n in ("ms", "rr", "rq"))
        ssy, rry, rqy = (sb(n, [P, NC]) for n in ("ssy", "rry", "rqy"))
        junk = sb("junk", [P, DM], BF16)
        junk_y = sb("junk_y", [P, GC], BF16)
        tmp = base[0]
        xc = sb("xc", [P, GT, T])
        zs_at = base[0]
        zs = sb("zs", [P, NC, GC])
        pl_hi = sb("pl_hi", [P, PT, T], F32R, at=zs_at)
        pl_lo = sb("pl_lo", [P, PT, T], F32R, at=zs_at + PT * T * 4)
        cbuf = [sb(f"cbuf{s}", [P, TAPS - 1 + T]) for s in range(2)]
        bc = [sb("b_ch", [P, T]), sb("c_ch", [P, T])]
        ubuf = sb("ubuf", [P, 16 + T])
        cs = sb("cs", [P, 16 + T])
        pf = sb("pf", [P, T])
        bt = [sb(f"bt{s}", [P, P]) for s in range(2)]
        cbs = [sb(f"cbs{s}", [P, P]) for s in range(2)]
        mx_hi = sb("mx_hi", [P, PT, PG], F32R)
        mx_at = base[0]
        mx_raw = sb("mx_raw", [P, PT, PG])
        mx_lo = sb("mx_lo", [P, PT, PG], F32R, at=mx_at)
        assert base[0] - tmp >= 32 * KB
        late = base[0]
        MX = HG * P
        m = [sb(f"m{s}", [P, MX + 2 * HG]) for s in range(3)]
        xt = [sb(f"xt{s}", [P, GC]) for s in range(2)]
        xdt = [sb(f"xdt{s}", [P, GC]) for s in range(2)]
        xdd = [sb(f"xdd{s}", [P, GC]) for s in range(2)]
        xin = sb("xin", [P, NC, DM], at=tmp)
        xs = sb("xs", [P, NC, DM], at=tmp + 16 * KB)
        dtw = [sb(f"dtw{s}", [HEADS, T], at=late + 2 * s * KB) for s in range(7)]
        wdt_raw = sb("wdt_raw", [P, NDT], at=late)
        pos16 = sb("pos16", [P, 16], at=late + 2 * KB)
        m_hi = sb("m_hi", [P, KT, T], F32R, at=tmp)
        m_lo = sb("m_lo", [P, KT, T], F32R, at=tmp + 16 * KB)
        sga = [sb(f"sga{s}", [P, T], at=late + 4 * s * KB) for s in range(2)]
        sgb = [sb(f"sgb{s}", [P, T], at=late + (2 + 4 * s) * KB) for s in range(2)]
        x2 = sb("x2", [P, NC, DM], at=acc_at)
        xs2 = sb("xs2", [P, NC, DM], at=ya_at)
        pin = sb("pin", [P, NC, PLE], at=yb_at)
        p_hi = sb("p_hi", [P, 2, T], F32R, at=yb_at + 4 * KB)
        p_lo = sb("p_lo", [P, 2, T], F32R, at=yb_at + 8 * KB)
        fg = sb("fg", [P, DM], at=yb_at + 12 * KB)
        sg = sb("sg", [P, NC, T], at=yb_at + 16 * KB)
        up0 = sb("up0", [P, NC, T], at=yb_at + 24 * KB)


        bank = [ctx.enter_context(nc.psum_tensor(f"bank{i}", [P, 512], F32)) for i in range(8)]
        acs_dram = nc.dram_tensor("acs_scratch", (NB, HEADS, T), F32).ap()

        def sig(name, **counts):
            return Signal(ctx.enter_context(nc.semaphore(name)), **counts)

        passed = ctx.enter_context(nc.semaphore("passed"))
        params_in = ctx.enter_context(nc.semaphore("params_in"))
        w_loaded = [ctx.enter_context(nc.semaphore(f"w_loaded{s}")) for s in range(RING)]
        x_in = sig("x_in", pre=1, O=1, step=16)
        acs_out = sig("acs_out", F=1, step=16)
        rows_in = [sig(f"rows_in{c}", F=1, G=1, step=16) for c in range(NC)]
        mix_in = sig("mix_in", F=1, G=1, step=16)
        x2_in = sig("x2_in", O=1, step=16)
        pin_in = sig("pin_in", O=1, step=16)
        fg_in = sig("fg_in", O=1, step=16)
        out_done = sig("out_done", O=NC, credit=1, step=16)
        consts = ctx.enter_context(nc.semaphore("consts"))
        w_ready = sig("w_ready", **UNITS)
        w_hi_done = ctx.enter_context(nc.semaphore("w_hi_done"))
        squares = sig("squares", pre=NC, O=5 * NC, credit=1)
        root = sig("root", O=2)
        root_x = sig("root_x", pre=1, O=1)
        x_hi = sig("x_hi", pre=KT, O=KT)
        t_hi = sig("t_hi", O=2 + KT)
        dt_exp = sig("dt_exp", F=1)
        acs_exp = sig("acs_exp", F=1)
        a_exp = ctx.enter_context(nc.semaphore("a_exp"))
        cbuf_full = sig("cbuf_full", F=6, G=6)
        silu_done = sig("silu_done", F=6, G=6)
        z_silu = sig("z_silu", F=NC, G=NC)
        decay = sig("decay", F=NC, G=NC)
        xt_full = sig("xt_full", F=NC, G=NC, credit=1)
        bt_full = sig("bt_full", F=2 * NC, G=2 * NC, credit=1)
        zp_full = sig("zp_full", F=PT, G=PT)
        u_full = sig("u_full", F=PT, G=PT)
        pl_hi_done = sig("pl_hi_done", F=PT, G=PT)
        yb_hi_done = sig("yb_hi_done", F=PT, G=PT)
        mx_hi_done = sig("mx_hi_done", F=1, G=1)
        y_squares = sig("y_squares", F=NC, G=NC, credit=1)
        y_root = sig("y_root", F=1, G=1)
        ya_hi_done = sig("ya_hi_done", G=GT, W=GT)
        gates = sig("gates", J=4)
        m_hi_done = sig("m_hi_done", J=2)
        up0_full = sig("up0_full", O=NC)
        ple_gate = sig("ple_gate", O=2 * NC)
        link_s = sig("vector_link", F=81, G=65, W=1, J=4, O=6)
        setup_link = ctx.enter_context(nc.semaphore("setup_link"))
        setup_done = ctx.enter_context(nc.semaphore("setup_done"))
        meansq = sig("meansq", O=2)
        meansq_x = sig("meansq_x", pre=1, O=1)
        xs_full = sig("xs_full", pre=NC, O=NC)
        x_lo = sig("x_lo", pre=KT, O=KT)
        xs2_full = sig("xs2_full", O=NC)
        t_lo = sig("t_lo", O=2 + KT)
        dt_abs = sig("dt_abs", F=1)
        dt_full = sig("dt_full", F=1)
        tok_full = sig("tok_full", F=1)
        conv_done = sig("conv_done", F=6, G=6, credit=2)
        seg_full = sig("seg_full", F=NC, G=NC)
        xdt_full = sig("xdt_full", F=NC, G=NC)
        m_full = sig("m_full", F=NC, G=NC)
        y_gated = sig("y_gated", F=NC, G=NC, credit=2)
        state_new = sig("state_new", F=NC, G=NC, credit=1)
        pf_full = sig("pf_full", F=PT, G=PT)
        pooled = sig("pooled", F=PT, G=PT)
        mx_full = sig("mx_full", F=1, G=1)
        mix_read = sig("mix_read", F=PT, G=PT)
        yb_val = sig("yb_val", F=PT, G=PT)
        yb_full = sig("yb_full", F=PT, G=PT)
        y_meansq = sig("y_meansq", F=1, G=1)
        y_normed = sig("y_normed", G=NC, W=NC)
        ya_full = sig("ya_full", G=GT, W=GT)
        acc_added = sig("acc_added", G=KT, W=KT, credit=2)
        m_val = sig("m_val", J=2)
        merged = sig("merged", J=2, credit=2)
        x2_sum = sig("x2_sum", O=2 * NC)
        up_gated = sig("up_gated", O=2 * NC)
        x3_sum = sig("x3_sum", O=2 * NC)
        out_full = sig("out_full", O=NC)
        unit_done = sig("unit_done", credit=RING, **UNITS)
        x_psum = sig("x_psum", pre=KT, O=KT)
        t_psum = sig("t_psum", O=2 + KT)
        dt_psum = sig("dt_psum", pre=1, O=1)
        tok_psum = sig("tok_psum", F=1)
        xt_psum = sig("xt_psum", F=NC, G=NC)
        bcb_psum = sig("bcb_psum", F=NC, G=NC)
        ssd_psum = sig("ssd_psum", F=3 * NC, G=3 * NC)
        mix_psum = sig("mix_psum", F=PT, G=PT, credit=1)
        yt_psum = sig("yt_psum", G=GT, W=GT)

        xb = x.rearrange("a (b c p) d -> (a b) p c d", c=NC, p=P)
        ob = out.rearrange("a (b c p) d -> (a b) c p d", c=NC, p=P)
        pb = p.rearrange("l a (b c p) d -> (l a b) p c d", c=NC, p=P)
        win = w_in.rearrange("l (k p) n -> p (l k) n", p=P)
        wa = w_branch_a.rearrange("l (g k p) n -> p (l g) k n", g=GROUPS, p=P)
        wb = w_branch_b.rearrange("l (k p) n -> p (l k) n", p=P)
        wo = w_out.rearrange("l (k p) n -> p (l k) n", p=P)
        wg = w_ple_gate.rearrange("l (k p) n -> p (l k) n", p=P)
        wu = w_ple_up.rearrange("l (k p) n -> p (l k) n", p=P)
        mixw = pool_mix_w.rearrange("l g (k p) n -> p (l g) k n", p=P)

        def one(ap, i):
            if isinstance(i, int):
                return ap[:, i]
            view = ap[:, bass.ds(i, 1)]
            names = "abcd"[: len(view.shape) - 2]
            return view.rearrange(f"p x {' '.join(names)} -> p (x {names[0]}) {' '.join(names[1:])}")

        def col(ap, i, j):
            return ap[:, bass.ds(i, 1), j:j + 1].rearrange("p a b -> p (a b)")

        def heads(ap):
            return ap.rearrange("p (h d) -> p h d", h=HG)

        def per_head(ap, n):
            return ap.unsqueeze(2).to_broadcast([P, HG, n])

        def on_its_own(eng):
            eng.sem_inc(passed, 1)

        block = ctx.enter_context(nc.Block())


        @block.sync
        def _(sp):
            loads = [
                (ng[:], norm_g.rearrange("l (k p) -> p (l k)", p=P)),
                (pg[:], ple_norm_g.rearrange("l (k p) -> p (l k)", p=P)),
                (gn[:], gnorm_g.rearrange("l (g k p) -> p (l g) k", p=P, g=GROUPS)),
                (mixb[:], pool_mix_b.rearrange("l (g k p) -> p (l g) k", p=P, g=GROUPS)),
                (pscale[:], pool_scale.rearrange("l (g k p) -> p (l g) k", p=P, g=GROUPS)),
                (dtb[:], dt_bias.rearrange("l (h a) -> (l h) a", a=1)),
                (aneg[:, 0:1], a_log.rearrange("l (h a) -> (l h) a", a=1)),
                (dskip[:], d_skip.rearrange("l h -> (l h)").partition_broadcast(P)),
                (wdt_raw[:, 0:KT * HEADS].rearrange("p (k h) -> p k h", k=KT),
                 win[:, :, COL_DT:COL_DT + HEADS]),
            ]
            loads += [(taps[:, j], conv_w[0, j].rearrange("(n p) -> p n", p=P)) for j in range(TAPS)]
            loads.append((taps[:, TAPS], conv_b[0].rearrange("(n p) -> p n", p=P)))
            assert len(loads) == N_LOADS
            sp.dma_start(xin[:], xb[0]).then_inc(x_in.sem, 16)
            for dst, src in loads:
                sp.dma_start(dst, src, allow_slow_non_contiguous=True).then_inc(params_in, 16)

            def load_unit(pos, k, src, parts):
                sp.wait_ge(unit_done.sem, unit_done.at(pos, k, back=RING))
                on_its_own(sp)
                s = slot(pos, k)
                dst = w_raw[s][:].rearrange("p (a b) -> p a b", a=parts)
                sp.dma_start(dst, src).then_inc(w_loaded[s], 16)

            def cols(first, i, stride=P):
                return win[:, :, bass.ds(i * stride + first, P)]

            def group(pos, g):
                load_unit(pos, U_B, cols(COL_B, g), KT)
                load_unit(pos, U_C, cols(COL_C, g), KT)
                load_unit(pos, U_X, cols(COL_X, g, GC), KT)
                if pos.phase == "F":
                    sp.wait_ge(x_psum.sem, x_psum.start_of(pos, "F"))
                    on_its_own(sp)
                sp.wait_ge(mix_psum.sem, mix_psum.at(pos, 0, back=1))
                on_its_own(sp)
                sp.dma_start(mx_raw[:], one(mixw, g)).then_inc(mix_in.sem, 16)
                for j in range(1, GT):
                    load_unit(pos, U_X + j, cols(COL_X + j * P, g, GC), KT)
                for j in range(PT):
                    load_unit(pos, U_ZP + j, cols(COL_ZP + j * P, g, PG), KT)
                for j in range(PT):
                    load_unit(pos, U_U + j, cols(COL_U + j * P, g, PG), KT)
                for k in range(4):
                    load_unit(pos, U_Z + k, win[:, 2 * k:2 * k + 2, bass.ds(g * GC, GC)], 2)

            def branch_a(pos, first, g):
                for k in range(4):
                    load_unit(pos, first + k, one(wa, g)[:, :, 256 * k:256 * k + 256], GT)

            with sp.Fori(0, NB) as b:
                group(Pos("F", b, 0), 0)
                with sp.Fori(0, GROUPS - 1) as i:
                    pos = Pos("G", b, i)
                    group(pos, i + 1)
                    branch_a(pos, U_A, i)
                branch_a(Pos("W", b, 0), 0, GROUPS - 1)
                with sp.Fori(0, KT // 2) as jj:
                    pos = Pos("J", b, jj)
                    for s in range(2):
                        load_unit(pos, 3 * s, cols(COL_GA + s * P, jj, 2 * P), KT)
                        load_unit(pos, 3 * s + 1, cols(COL_GB + s * P, jj, 2 * P), KT)
                        load_unit(pos, 3 * s + 2, wb[:, :, bass.ds(jj * 2 * P + s * P, P)], KT)
                pos = Pos("O", b, 0)

                def quarter(k, w, first, h):
                    load_unit(pos, first + k, w[:, 2 * k:2 * k + 2, 512 * h:512 * h + 512], 2)

                quarter(0, wo, 0, 0)
                quarter(1, wo, 0, 0)
                sp.wait_ge(merged.sem, merged.start_of(pos, "O"))
                on_its_own(sp)
                quarter(2, wo, 0, 0)
                sp.dma_start(x2[:], xb[bass.ds(b, 1)].rearrange("b p c d -> (b p) c d"))\
                    .then_inc(x2_in.sem, 16)
                sp.dma_start(pin[:], pb[bass.ds(b, 1)].rearrange("b p c d -> (b p) c d"))\
                    .then_inc(pin_in.sem, 16)
                quarter(3, wo, 0, 0)
                sp.dma_start(fg[:], final_g.partition_broadcast(P)).then_inc(fg_in.sem, 16)
                for k in range(4):
                    quarter(k, wo, 4, 1)
                quarter(0, wu, U_UP0, 0)
                for k in range(3):
                    quarter(k, wg, U_GATE, 0)
                sp.dma_start(xin[:], xb[bass.ds((b + 1) & (NB - 1), 1)].rearrange("b p c d -> (b p) c d"))\
                    .then_inc(x_in.sem, 16)
                quarter(3, wg, U_GATE, 0)
                for k in range(4):
                    quarter(k, wg, U_GATE + 4, 1)
                quarter(0, wu, U_UP1, 1)
            last = Pos("F", NB, 0)
            for k in range(RING):
                sp.wait_ge(unit_done.sem, unit_done.at(last, k, back=RING))
                sp.dma_start(w_raw[k][:].rearrange("p (a b) -> p a b", a=KT), win[:, :, 0:P])\
                    .then_inc(w_loaded[k], 16)

        @block.gpsimd
        def _(pool):
            pool.memset(ident[:], 0.0).then_inc(consts, 1)
            pool.memset(cap[:], 0.0).then_inc(consts, 1)
            pool.memset(state[:], 0.0).then_inc(consts, 1)
            pool.memset(conv_halo[:], 0.0).then_inc(consts, 1)
            pool.memset(pool_halo[:], 0.0).then_inc(consts, 1)
            pool.iota(pos16[:], [[1, 16]], base=1, channel_multiplier=0,
                      allow_small_or_imprecise_dtypes=True).then_inc(consts, 1)
            pool.wait_ge(consts, 2)
            pool.affine_select(out=ident[:], in_=ident[:], compare_op=ALU.not_equal, fill=1.0,
                               base=0, pattern=[[-1, P]], channel_multiplier=1).then_inc(consts, 1)
            pool.affine_select(out=cap[:], in_=cap[:], compare_op=ALU.is_ge, fill=-1e30,
                               base=0, pattern=[[1, P]], channel_multiplier=-1).then_inc(consts, 1)

            def lo_part(s, count):
                pool.wait_ge(w_hi_done, count)
                pool.tensor_tensor(w_lo[s][:], w_raw[s][:], w_hi[s][:].bitcast(F32), ALU.subtract)\
                    .then_inc(w_ready.sem, 1)

            for k in range(RING):
                lo_part(k, k + 1)
            per = 2 * RING
            with pool.Fori(0, NB * BLOCK_UNITS // per) as r:
                for k in range(per):
                    lo_part(k % RING, r * per + (RING + k + 1))

        @block.scalar
        def _(act):
            def split_ahead(pos, k):
                s = slot(pos, k + 2)
                act.wait_ge(w_loaded[s], loaded_at(pos, k + 2))
                act.wait_ge(unit_done.sem, unit_done.at(pos, k + 2, back=RING))
                act.activation(w_hi[s][:], w_raw[s][:], ACT.Copy).then_inc(w_hi_done, 1)

            for s in (squares, y_squares, xt_full, bt_full):
                act.sem_inc(s.sem, 1)
            act.sem_inc(out_done.sem, 16)

            def sums_of_squares(pos, k0, src, sums, ready):
                for c in range(NC):
                    if ready:
                        act.wait_ge(ready[0].sem, ready[0].at(pos, ready[1] + c))
                    act.wait_ge(squares.sem, squares.at(pos, k0 + c, back=1))
                    act.activation(junk[:, 0:src[c].shape[-1]], src[c], ACT.Square,
                                   accum_out=sums[:, c:c + 1]).then_inc(squares.sem, 1)

            def halves(h):
                return [x2[:, c, 512 * h:512 * h + 512] for c in range(NC)]

            def norm_x(pos, k0):
                act.wait_ge(x_in.sem, x_in.at(pos, 0))
                sums_of_squares(pos, k0, [xin[:, c] for c in range(NC)], ssx, None)
                act.wait_ge(meansq_x.sem, meansq_x.at(pos, 0))
                act.activation(rrx[:], ssx[:], ACT.Sqrt).then_inc(root_x.sem, 1)

            def x_his(pos):
                for k in range(KT):
                    act.wait_ge(x_psum.sem, x_psum.at(pos, k))
                    act.activation(h_hi[:, k], bank[k][:], ACT.Copy, scale=ng[:, k:k + 1])\
                        .then_inc(x_hi.sem, 1)

            def group(pos, g):
                prev = pos.phase == "G"

                def load_rows(c):
                    src = acs_dram[bass.ds(pos.b, 1), bass.ds(g * HG, HG), c * P:(c + 1) * P]
                    act.dma_start(m[c % 3][:, 0:HG * P].rearrange("p (h l) -> p h l", h=HG),
                                  src.rearrange("b h t -> (b h) t").partition_broadcast(P))\
                        .then_inc(rows_in[c].sem, 16)

                def silu(t):
                    dst = bc[t][:] if t < 2 else xc[:, t - 2]
                    act.wait_ge(conv_done.sem, conv_done.at(pos, t))
                    act.activation(dst, dst, ACT.Silu).then_inc(silu_done.sem, 1)

                def chunk_in(c):
                    act.wait_ge(y_gated.sem, y_gated.at(pos, c, back=2))
                    act.wait_ge(xt_psum.sem, xt_psum.at(pos, c))
                    act.activation(xt[c % 2][:], bank[6][:], ACT.Copy).then_inc(xt_full.sem, 1)
                    act.wait_ge(bcb_psum.sem, bcb_psum.at(pos, c))
                    act.activation(bt[c % 2][:], bank[7][:, 0:P], ACT.Copy).then_inc(bt_full.sem, 1)
                    act.activation(cbs[c % 2][:], bank[7][:, P:2 * P], ACT.Copy).then_inc(bt_full.sem, 1)

                def decays(c):
                    act.wait_ge(seg_full.sem, seg_full.at(pos, c))
                    act.activation(m[c % 3][:], m[c % 3][:], ACT.Exp).then_inc(decay.sem, 1)

                def square(c):
                    act.wait_ge(y_gated.sem, y_gated.at(pos, c))
                    act.wait_ge(y_squares.sem, y_squares.at(pos, c, back=1))
                    act.activation(junk_y[:], zs[:, c], ACT.Square, accum_out=ssy[:, c:c + 1])\
                        .then_inc(y_squares.sem, 1)

                if prev:
                    act.wait_ge(y_gated.sem, y_gated.at(pos, 0, back=1))
                    on_its_own(act)
                    for c in range(3):
                        load_rows(c)
                else:
                    act.wait_ge(dt_abs.sem, dt_abs.at(pos, 0))
                    act.activation(dtw[1][:], dtw[1][:], ACT.Exp).then_inc(dt_exp.sem, 1)
                for t in range(6):
                    if t or prev:
                        split_ahead(pos, t)
                    act.wait_ge(conv_done.sem, conv_done.at(pos, t, back=2))
                    act.wait_ge(unit_done.sem, unit_done.at(pos, t))
                    act.activation(cbuf[t % 2][:, TAPS - 1:], bank[t % 2][:], ACT.Copy)\
                        .then_inc(cbuf_full.sem, 1)
                    if t:
                        silu(t - 1)
                    if t == 3 and prev:
                        ya_his(pos, g - 1)
                    if t == 4 and not prev:
                        act.wait_ge(dt_full.sem, dt_full.at(pos, 0))
                        on_its_own(act)
                        act.dma_start(acs_dram[bass.ds(b, 1)].rearrange("b h t -> (b h) t"), dtw[6][:])\
                            .then_inc(acs_out.sem, 16)
                split_ahead(pos, 6)
                silu(5)
                if not prev:
                    act.wait_ge(acs_out.sem, acs_out.at(pos, 0))
                    act.wait_ge(tok_psum.sem, tok_psum.at(pos, 0))
                    on_its_own(act)
                    for c in range(3):
                        load_rows(c)
                for j in range(PT):
                    if j:
                        split_ahead(pos, U_ZP + j)
                    act.wait_ge(unit_done.sem, unit_done.at(pos, U_ZP + j))
                    act.activation(one(zps, g * PT + j), bank[j][:], ACT.Silu).then_inc(zp_full.sem, 1)
                act.wait_ge(mix_in.sem, mix_in.at(pos, 0))
                act.activation(mx_hi[:], mx_raw[:], ACT.Copy).then_inc(mx_hi_done.sem, 1)
                split_ahead(pos, U_U)
                act.wait_ge(unit_done.sem, unit_done.at(pos, U_U))
                act.activation(ubuf[:, 16:], bank[0][:], ACT.Copy).then_inc(u_full.sem, 1)
                if not prev:
                    act.wait_ge(tok_full.sem, tok_full.at(pos, 0))
                    act.activation(exp_acs[:], tok_acs[:], ACT.Exp).then_inc(acs_exp.sem, 1)
                decays(0)
                decays(1)
                split_ahead(pos, U_U + 1)
                act.wait_ge(pf_full.sem, pf_full.at(pos, 0))
                act.activation(pl_hi[:, 0], pf[:], ACT.Copy).then_inc(pl_hi_done.sem, 1)
                act.wait_ge(pooled.sem, pooled.at(pos, 0))
                act.wait_ge(unit_done.sem, unit_done.at(pos, U_U + 1))
                act.activation(ubuf[:, 16:], bank[1][:], ACT.Copy).then_inc(u_full.sem, 1)
                chunk_in(0)
                split_ahead(pos, U_Z)
                act.wait_ge(pf_full.sem, pf_full.at(pos, 1))
                act.activation(pl_hi[:, 1], pf[:], ACT.Copy).then_inc(pl_hi_done.sem, 1)
                split_ahead(pos, U_Z + 1)
                chunk_in(1)
                split_ahead(pos, U_Z + 2)
                decays(2)
                for j in range(PT):
                    act.wait_ge(yb_val.sem, yb_val.at(pos, j))
                    on_its_own(act)
                    act.activation(one(yb_hi, g * PT + j), pf[:], ACT.Copy).then_inc(yb_hi_done.sem, 1)
                split_ahead(pos, U_Z + 3)
                act.wait_ge(unit_done.sem, unit_done.at(pos, U_Z + 3))
                for c in range(NC):
                    act.activation(zs[:, c], bank[2 + c][:], ACT.Silu).then_inc(z_silu.sem, 1)
                if prev:
                    split_ahead(pos, U_A)
                chunk_in(2)
                act.wait_ge(y_gated.sem, y_gated.at(pos, 0))
                on_its_own(act)
                load_rows(3)
                square(0)
                if prev:
                    split_ahead(pos, U_A + 1)
                chunk_in(3)
                decays(3)
                square(1)
                if prev:
                    split_ahead(pos, U_A + 2)
                square(2)
                if prev:
                    split_ahead(pos, U_A + 3)
                square(3)
                act.wait_ge(y_meansq.sem, y_meansq.at(pos, 0))
                act.activation(rry[:], ssy[:], ACT.Sqrt).then_inc(y_root.sem, 1)

            def ya_his(pos, g):
                for k in range(GT):
                    act.wait_ge(yt_psum.sem, yt_psum.at(pos, k))
                    act.activation(ya_hi[:, k], bank[2 + k][:], ACT.Copy, scale=col(gn, g, k))\
                        .then_inc(ya_hi_done.sem, 1)

            before = Pos("PRE", 0, 0)
            norm_x(before, 0)
            act.wait_ge(params_in, 16 * N_LOADS)
            act.activation(aneg[:, 1:2], aneg[:, 0:1], ACT.Exp).then_inc(a_exp, 1)
            for k in range(RING):
                act.wait_ge(w_loaded[k], 16)
                act.activation(w_hi[k][:], w_raw[k][:], ACT.Copy).then_inc(w_hi_done, 1)
            x_his(before)
            with act.Fori(0, NB) as b:
                pos = Pos("F", b, 0)
                group(pos, 0)
                act.wait_ge(out_done.sem, out_done.start_of(pos, "F"))
                on_its_own(act)
                with act.Fori(0, GROUPS - 1) as i:
                    group(Pos("G", b, i), i + 1)
                pos = Pos("W", b, 0)
                split_ahead(pos, 0)
                ya_his(pos, GROUPS - 1)
                for k in range(1, 4):
                    split_ahead(pos, k)
                with act.Fori(0, KT // 2) as jj:
                    pos = Pos("J", b, jj)
                    for s in range(2):
                        j = jj * 2 + s
                        split_ahead(pos, 3 * s)
                        act.wait_ge(merged.sem, merged.at(pos, s, back=2))
                        act.wait_ge(unit_done.sem, unit_done.at(pos, 3 * s))
                        act.activation(sga[s][:], bank[2 + 3 * s][:], ACT.Sigmoid).then_inc(gates.sem, 1)
                        split_ahead(pos, 3 * s + 1)
                        act.wait_ge(unit_done.sem, unit_done.at(pos, 3 * s + 1))
                        act.activation(sgb[s][:], bank[3 + 3 * s][:], ACT.Sigmoid).then_inc(gates.sem, 1)
                        split_ahead(pos, 3 * s + 2)
                        act.wait_ge(m_val.sem, m_val.at(pos, s))
                        act.activation(one(m_hi, j), sga[s][:], ACT.Copy).then_inc(m_hi_done.sem, 1)
                pos = Pos("O", b, 0)
                for k in range(4):
                    split_ahead(pos, k)
                split_ahead(pos, 4)
                sums_of_squares(pos, 0, halves(0), ss[:, 0], (x2_sum, 0))
                split_ahead(pos, 5)
                for k in range(2):
                    act.wait_ge(t_psum.sem, t_psum.at(pos, k))
                    act.activation(p_hi[:, k], bank[k][:], ACT.Copy).then_inc(t_hi.sem, 1)
                split_ahead(pos, 6)
                split_ahead(pos, 7)
                sums_of_squares(pos, NC, halves(1), ss[:, 1], (x2_sum, NC))
                act.wait_ge(meansq.sem, meansq.at(pos, 0))
                act.activation(rr[:], ms[:], ACT.Sqrt).then_inc(root.sem, 1)
                split_ahead(pos, 8)
                act.wait_ge(unit_done.sem, unit_done.at(pos, U_UP0))
                for c in range(NC):
                    act.activation(up0[:, c], bank[half_bank(0, c)][:], ACT.Copy).then_inc(up0_full.sem, 1)
                for k in range(KT):
                    act.wait_ge(t_psum.sem, t_psum.at(pos, 2 + k))
                    act.activation(h_hi[:, k], bank[(4 + k) % 8][:], ACT.Copy, scale=pg[:, k:k + 1])\
                        .then_inc(t_hi.sem, 1)
                split_ahead(pos, 9)
                split_ahead(pos, 10)
                split_ahead(pos, 11)
                norm_x(pos, 2 * NC)
                split_ahead(pos, 12)
                for h in range(2):
                    act.wait_ge(unit_done.sem, unit_done.at(pos, U_GATE + 4 * h + 3))
                    for c in range(NC):
                        if h:
                            act.wait_ge(x3_sum.sem, x3_sum.at(pos, c))
                        act.activation(sg[:, c], bank[half_bank(1 - h, c)][:], ACT.Sigmoid)\
                            .then_inc(ple_gate.sem, 1)
                    if h == 0:
                        split_ahead(pos, 13)
                        sums_of_squares(pos, 3 * NC, halves(0), ss[:, 0], (x3_sum, 0))
                        for k in range(14, 17):
                            split_ahead(pos, k)
                split_ahead(pos, 17)
                x_his(pos)
                split_ahead(pos, 18)
                sums_of_squares(pos, 4 * NC, halves(1), ss[:, 1], (x3_sum, NC))
                act.wait_ge(meansq.sem, meansq.at(pos, 1))
                act.activation(rr[:], ms[:], ACT.Sqrt).then_inc(root.sem, 1)
                for c in range(NC):
                    act.wait_ge(out_full.sem, out_full.at(pos, c))
                    on_its_own(act)
                    act.dma_start(ob[bass.ds(b, 1), c].rearrange("b p d -> (b p) d"), xs2[:, c])\
                        .then_inc(out_done.sem, 16)
            act.wait_ge(out_done.sem, 16 * (NB * NC + 1))
            act.wait_ge(acs_out.sem, 16 * NB)

        @block.vector
        def _(dve):
            n_link = {"k": 0, "setup": 0}

            def link(pos, ins):
                if pos.phase == "PRE":
                    n_link["setup"] += 1
                    ins.then_inc(setup_link, 1)
                    dve.wait_ge(setup_link, n_link["setup"])
                else:
                    ins.then_inc(link_s.sem, 1)
                    dve.wait_ge(link_s.sem, link_s.at(pos, n_link["k"]))
                    n_link["k"] += 1

            def links_done(phase):
                assert n_link["k"] == link_s.n[phase], (phase, n_link["k"])
                n_link["k"] = 0

            for s in (conv_done, y_gated, acc_added, merged):
                dve.sem_inc(s.sem, 2)
            dve.sem_inc(state_new.sem, 1)

            def inv_rms(pos, sums, mean, mean_k, roots, inv, width, sq, sqk, rt, rtk, halves=False):
                dve.wait_ge(sq.sem, sqk)
                if halves:
                    link(pos, dve.tensor_tensor(ms[:], ss[:, 0], ss[:, 1], ALU.add))
                dve.tensor_scalar(sums[:], sums[:], 1.0 / width, EPS, ALU.mult, ALU.add)\
                    .then_inc(mean.sem, 1)
                dve.wait_ge(rt.sem, rtk)
                link(pos, dve.reciprocal(inv[:], roots[:]))

            def norm_x(pos, sqk):
                inv_rms(pos, ssx, meansq_x, 0, rrx, rqx, DM, squares, squares.at(pos, sqk),
                        root_x, root_x.at(pos, 0))
                for c in range(NC):
                    dve.tensor_scalar(xs[:, c], xin[:, c], rqx[:, c:c + 1], None, ALU.mult)\
                        .then_inc(xs_full.sem, 1)

            def x_los(pos):
                for k in range(KT):
                    dve.wait_ge(x_hi.sem, x_hi.at(pos, k))
                    dve.scalar_tensor_tensor(h_lo[:, k], bank[k][:], ng[:, k:k + 1],
                                             h_hi[:, k].bitcast(F32), ALU.mult, ALU.subtract)\
                        .then_inc(x_lo.sem, 1)

            before = Pos("PRE", 0, 0)
            dve.wait_ge(x_in.sem, x_in.at(before, 0))
            norm_x(before, NC - 1)
            dve.wait_ge(params_in, 16 * N_LOADS)
            dve.wait_ge(consts, 8)
            dve.wait_ge(a_exp, 1)
            for g in range(GROUPS):
                dve.memset(invw[:, g:g + 1], 1.0 / 2 ** (g + 1))
                link(before, dve.tensor_scalar(inv16[:, g], pos16[:], float(2 ** (g + 1)), None, ALU.min))
            link(before, dve.reciprocal(inv16[:].rearrange("p g n -> p (g n)"),
                                        inv16[:].rearrange("p g n -> p (g n)")))
            link(before, dve.tensor_scalar(aneg[:, 1:2], aneg[:, 1:2], -1.0, None, ALU.mult))
            link(before, dve.tensor_copy(wdt_raw[:, KT * HEADS:NDT], wdt_raw[:, 0:NDT - KT * HEADS]))
            link(before, dve.tensor_copy(wdt_hi[:], wdt_raw[:]))
            dve.tensor_tensor(wdt_lo[:], wdt_raw[:], wdt_hi[:].bitcast(F32), ALU.subtract)\
                .then_inc(setup_done, 1)
            dve.wait_ge(setup_done, 1)
            x_los(before)

            v, e, r_, s_, s2, q_, acs = (t[:] for t in dtw)

            def dt_start(pos):
                dve.wait_ge(dt_psum.sem, dt_psum.start_of(pos, "F"))
                link(pos, dve.tensor_scalar(v, bank[DT_BANK][0:HEADS, :], dtb[:, 0:1], None, ALU.add))
                dve.scalar_tensor_tensor(e, v, -1.0, v, ALU.mult, ALU.min).then_inc(dt_abs.sem, 1)

            def dt_series(pos):
                dve.wait_ge(dt_exp.sem, dt_exp.at(pos, 0))
                link(pos, dve.tensor_scalar(r_, e, 2.0, None, ALU.add))
                link(pos, dve.reciprocal(r_, r_))
                link(pos, dve.tensor_tensor(s_, e, r_, ALU.mult))
                link(pos, dve.tensor_tensor(s2, s_, s_, ALU.mult))
                link(pos, dve.tensor_scalar(q_, s2, ATANH[-1], None, ALU.mult))
                for coef in reversed(ATANH[3:-1]):
                    link(pos, dve.scalar_tensor_tensor(q_, q_, coef, s2, ALU.add, ALU.mult))

            def dt_end(pos):
                for coef in reversed(ATANH[:3]):
                    link(pos, dve.scalar_tensor_tensor(q_, q_, coef, s2, ALU.add, ALU.mult))
                link(pos, dve.scalar_tensor_tensor(q_, q_, 1.0, s_, ALU.add, ALU.mult))
                link(pos, dve.tensor_scalar(v, v, 0.0, None, ALU.max))
                link(pos, dve.scalar_tensor_tensor(v, q_, 2.0, v, ALU.mult, ALU.add))
                link(pos, dve.tensor_scalar(r_, v, aneg[:, 1:2], None, ALU.mult))
                link(pos, dve.memset(e, 0.0))
                for c in range(NC):
                    part = slice(c * P, (c + 1) * P)
                    scan = dve.tensor_tensor_scan(acs[:, part], r_[:, part], e[:, part], 0.0,
                                                  ALU.add, ALU.add)
                scan.then_inc(dt_full.sem, 1)

            def norm_y(pos):
                link_root = y_root.at(pos, 0, back=1)
                dve.wait_ge(y_root.sem, link_root)
                link(pos, dve.reciprocal(rqy[:], rry[:]))
                for c in range(NC):
                    dve.tensor_scalar(zs[:, c], zs[:, c], rqy[:, c:c + 1], None, ALU.mult)\
                        .then_inc(y_normed.sem, 1)

            def ya_los(pos, g):
                for k in range(GT):
                    dve.wait_ge(ya_hi_done.sem, ya_hi_done.at(pos, k))
                    dve.scalar_tensor_tensor(ya_lo[:, k], bank[2 + k][:], col(gn, g, k),
                                             ya_hi[:, k].bitcast(F32), ALU.mult, ALU.subtract)\
                        .then_inc(ya_full.sem, 1)

            def add_branch_a(pos, first, q):
                dve.wait_ge(unit_done.sem, unit_done.at(pos, first + q))
                for j in (2 * q, 2 * q + 1):
                    dve.tensor_tensor(a_acc[:, j], a_acc[:, j], bank[acc_bank(j)][:], ALU.add)\
                        .then_inc(acc_added.sem, 1)

            def group(pos, g):
                prev = pos.phase == "G"

                def conv(t):
                    buf = cbuf[t % 2]
                    dst = bc[t][:] if t < 2 else xc[:, t - 2]
                    halo = conv_halo[:, bass.ds(g, 1), t, :].rearrange("p a n -> p (a n)")
                    tile = g + (DI // P + GROUPS * t) if t < 2 else g * GT + (t - 2)
                    tap = [taps[:, j, bass.ds(tile, 1)] for j in range(TAPS + 1)]
                    dve.wait_ge(cbuf_full.sem, cbuf_full.at(pos, t))
                    link(pos, dve.tensor_copy(buf[:, 0:TAPS - 1], halo))
                    link(pos, dve.tensor_scalar(dst, buf[:, 0:T], tap[0], tap[TAPS], ALU.mult, ALU.add))
                    for j in range(1, TAPS - 1):
                        link(pos, dve.scalar_tensor_tensor(dst, buf[:, j:j + T], tap[j], dst,
                                                           ALU.mult, ALU.add))
                    dve.scalar_tensor_tensor(dst, buf[:, TAPS - 1:TAPS - 1 + T], tap[TAPS - 1],
                                             dst, ALU.mult, ALU.add)
                    dve.tensor_copy(halo, buf[:, T:T + TAPS - 1]).then_inc(conv_done.sem, 1)

                def views(c):
                    mat = m[c % 3]
                    return (mat[:, 0:MX].rearrange("p (h l) -> p h l", h=HG), mat[:, MX:MX + HG],
                            mat[:, MX + HG:MX + 2 * HG])

                def segments(c):
                    seg, to_end, chunk_decay = views(c)
                    acs_s = tok_acs[:, c, bass.ds(g * HG, HG)]
                    dve.wait_ge(rows_in[c].sem, rows_in[c].at(pos, 0))
                    dve.tensor_tensor(to_end, seg[:, :, P - 1], acs_s, ALU.subtract)
                    link(pos, dve.tensor_copy(chunk_decay, seg[:, :, P - 1]))
                    link(pos, dve.tensor_tensor(seg, seg, per_head(acs_s, P), ALU.subtract))
                    dve.tensor_tensor(seg, seg, cap[:].unsqueeze(1).to_broadcast([P, HG, P]), ALU.min)\
                        .then_inc(seg_full.sem, 1)

                def inputs(c):
                    seg, to_end, _ = views(c)
                    x_, xd, xe = xt[c % 2], xdt[c % 2], xdd[c % 2]
                    dt_s = tok_dt[:, c, bass.ds(g * HG, HG)]
                    dve.wait_ge(xt_full.sem, xt_full.at(pos, c))
                    link(pos, dve.tensor_tensor(heads(xd[:]), heads(x_[:]), per_head(dt_s, HD), ALU.mult))
                    link(pos, dve.tensor_tensor(heads(x_[:]), heads(x_[:]),
                                                per_head(dskip[:, bass.ds(g * HG, HG)], HD), ALU.mult))
                    dve.wait_ge(decay.sem, decay.at(pos, c))
                    dve.tensor_tensor(heads(xe[:]), heads(xd[:]), per_head(to_end, HD), ALU.mult)\
                        .then_inc(xdt_full.sem, 1)
                    dve.wait_ge(bt_full.sem, bt_full.at(pos, 2 * c + 1))
                    dve.tensor_tensor(seg, seg, cbs[c % 2][:].unsqueeze(1).to_broadcast([P, HG, P]),
                                      ALU.mult).then_inc(m_full.sem, 1)

                def outputs(c):
                    _, _, chunk_decay = views(c)
                    x_, y = xt[c % 2], xdt[c % 2]
                    ea = exp_acs[:, c, bass.ds(g * HG, HG)]
                    st = one(state, g)
                    dve.wait_ge(ssd_psum.sem, ssd_psum.at(pos, 3 * c + 1))
                    link(pos, dve.tensor_tensor(heads(st), heads(st), per_head(chunk_decay, HD), ALU.mult))
                    dve.tensor_tensor(st, st, bank[4][:], ALU.add).then_inc(state_new.sem, 1)
                    dve.wait_ge(ssd_psum.sem, ssd_psum.at(pos, 3 * c + 2))
                    link(pos, dve.tensor_tensor(heads(y[:]), heads(bank[3][:]), per_head(ea, HD), ALU.mult))
                    link(pos, dve.tensor_tensor(y[:], y[:], bank[2][:], ALU.add))
                    link(pos, dve.tensor_tensor(y[:], y[:], x_[:], ALU.add))
                    dve.tensor_tensor(zs[:, c], y[:], zs[:, c], ALU.mult).then_inc(y_gated.sem, 1)
                    dve.wait_ge(y_gated.sem, y_gated.at(pos, c))

                def pool_tile(j):
                    halo = pool_halo[:, bass.ds(g, 1), j, :].rearrange("p a n -> p (a n)")
                    inv = one(inv16, g)
                    dve.wait_ge(u_full.sem, u_full.at(pos, j))
                    link(pos, dve.tensor_copy(ubuf[:, 0:16], halo))
                    link(pos, dve.tensor_tensor_scan(cs[:], ubuf[:], ubuf[:], 0.0, ALU.add, ALU.bypass))
                    on_its_own(dve)
                    if j:
                        dve.wait_ge(pooled.sem, pooled.at(pos, j - 1))
                        on_its_own(dve)
                    lag = cs[:, bass.ds(16 - (2 << g), T)]
                    link(pos, dve.tensor_tensor(pf[:], cs[:, 16:16 + T], lag, ALU.subtract))
                    dve.scalar_tensor_tensor(pf[:, 16:T], pf[:, 16:T], invw[:, bass.ds(g, 1)],
                                             ubuf[:, 32:T + 16], ALU.mult, ALU.subtract)
                    dve.tensor_copy(halo, ubuf[:, T:T + 16])
                    link(pos, dve.tensor_tensor(pf[:, 0:16], pf[:, 0:16], inv, ALU.mult))
                    dve.tensor_tensor(pf[:, 0:16], pf[:, 0:16], ubuf[:, 16:32], ALU.subtract)\
                        .then_inc(pf_full.sem, 1)
                    dve.wait_ge(pl_hi_done.sem, pl_hi_done.at(pos, j))
                    dve.tensor_tensor(pl_lo[:, j], pf[:], pl_hi[:, j].bitcast(F32), ALU.subtract)\
                        .then_inc(pooled.sem, 1)

                if not prev:
                    dt_start(pos)
                conv(0)
                if prev:
                    norm_y(pos)
                conv(1)
                if not prev:
                    dt_series(pos)
                conv(2)
                conv(3)
                if prev:
                    ya_los(pos, g - 1)
                else:
                    dt_end(pos)
                conv(4)
                conv(5)
                if not prev:
                    dve.wait_ge(tok_psum.sem, tok_psum.at(pos, 0))
                    dve.tensor_copy(tok_dt[:].rearrange("p c h -> p (c h)"), bank[TOK_BANK][:, 0:NC * HEADS])
                    dve.tensor_copy(tok_acs[:].rearrange("p c h -> p (c h)"),
                                    bank[TOK_BANK][:, NC * HEADS:2 * NC * HEADS]).then_inc(tok_full.sem, 1)
                    dve.wait_ge(tok_full.sem, tok_full.at(pos, 0))
                segments(0)
                segments(1)
                pool_tile(0)
                dve.wait_ge(mx_hi_done.sem, mx_hi_done.at(pos, 0))
                dve.tensor_tensor(mx_lo[:], mx_raw[:], mx_hi[:].bitcast(F32), ALU.subtract)\
                    .then_inc(mx_full.sem, 1)
                pool_tile(1)
                inputs(0)
                segments(2)
                inputs(1)
                for j in range(PT):
                    dve.wait_ge(mix_psum.sem, mix_psum.at(pos, j))
                    if j:
                        dve.wait_ge(yb_full.sem, yb_full.at(pos, j - 1))
                    dve.tensor_scalar(pf[:], bank[j][:], col(mixb, g, j), col(pscale, g, j),
                                      ALU.add, ALU.mult).then_inc(mix_read.sem, 1)
                    dve.wait_ge(mix_read.sem, mix_read.at(pos, j))
                    dve.tensor_tensor(pf[:], pf[:], one(zps, g * PT + j), ALU.mult).then_inc(yb_val.sem, 1)
                    dve.wait_ge(yb_hi_done.sem, yb_hi_done.at(pos, j))
                    dve.tensor_tensor(one(yb_lo, g * PT + j), pf[:],
                                      one(yb_hi, g * PT + j).bitcast(F32), ALU.subtract)\
                        .then_inc(yb_full.sem, 1)
                for c in range(NC):
                    if prev:
                        add_branch_a(pos, U_A, c)
                    if c == 0:
                        dve.wait_ge(acs_exp.sem, acs_exp.start_of(pos, "G"))
                        dve.wait_ge(z_silu.sem, z_silu.at(pos, NC - 1))
                    outputs(c)
                    if c == 0:
                        inputs(2)
                        if not prev:
                            dve.memset(a_acc[:], 0.0)
                    if c == 1:
                        segments(3)
                        inputs(3)
                dve.wait_ge(y_squares.sem, y_squares.at(pos, NC - 1))
                dve.tensor_scalar(ssy[:], ssy[:], 1.0 / GC, EPS, ALU.mult, ALU.add).then_inc(y_meansq.sem, 1)
                dve.wait_ge(y_meansq.sem, y_meansq.at(pos, 0))
                links_done(pos.phase)

            with dve.Fori(0, NB) as b:
                group(Pos("F", b, 0), 0)
                on_its_own(dve)
                with dve.Fori(0, GROUPS - 1) as i:
                    group(Pos("G", b, i), i + 1)
                pos = Pos("W", b, 0)
                norm_y(pos)
                ya_los(pos, GROUPS - 1)
                for q in range(4):
                    add_branch_a(pos, 0, q)
                dve.wait_ge(acc_added.sem, acc_added.at(pos, KT - 1))
                on_its_own(dve)
                links_done("W")
                with dve.Fori(0, KT // 2) as jj:
                    pos = Pos("J", b, jj)
                    for s in range(2):
                        j = jj * 2 + s
                        dve.wait_ge(gates.sem, gates.at(pos, 2 * s + 1))
                        link(pos, dve.tensor_tensor(sga[s][:], sga[s][:], one(a_acc, j), ALU.mult))
                        dve.wait_ge(unit_done.sem, unit_done.at(pos, 3 * s + 2))
                        link(pos, dve.tensor_tensor(sgb[s][:], sgb[s][:], bank[4 + 3 * s][:], ALU.mult))
                        dve.tensor_tensor(sga[s][:], sga[s][:], sgb[s][:], ALU.add).then_inc(m_val.sem, 1)
                        dve.wait_ge(m_hi_done.sem, m_hi_done.at(pos, s))
                        dve.tensor_tensor(one(m_lo, j), sga[s][:], one(m_hi, j).bitcast(F32), ALU.subtract)\
                            .then_inc(merged.sem, 1)
                    links_done("J")
                pos = Pos("O", b, 0)
                for g in range(GROUPS):
                    ins = dve.memset(inv16[:, g], 1.0 / 2 ** (g + 1))
                link(pos, ins)
                dve.wait_ge(x2_in.sem, x2_in.at(pos, 0))
                for h in range(2):
                    dve.wait_ge(unit_done.sem, unit_done.at(pos, 4 * h + 3))
                    for c in range(NC):
                        part = x2[:, c, 512 * h:512 * h + 512]
                        dve.tensor_tensor(part, part, bank[half_bank(h, c)][:], ALU.add)\
                            .then_inc(x2_sum.sem, 1)
                    if h == 0:
                        for k in range(2):
                            dve.wait_ge(t_hi.sem, t_hi.at(pos, k))
                            dve.tensor_tensor(p_lo[:, k], bank[k][:], p_hi[:, k].bitcast(F32), ALU.subtract)\
                                .then_inc(t_lo.sem, 1)
                inv_rms(pos, ms, meansq, 0, rr, rq, DM, squares, squares.at(pos, 2 * NC - 1),
                        root, root.at(pos, 0), halves=True)
                for c in range(NC):
                    dve.tensor_scalar(xs2[:, c], x2[:, c], rq[:, c:c + 1], None, ALU.mult)\
                        .then_inc(xs2_full.sem, 1)
                for k in range(KT):
                    dve.wait_ge(t_hi.sem, t_hi.at(pos, 2 + k))
                    dve.scalar_tensor_tensor(h_lo[:, k], bank[(4 + k) % 8][:], pg[:, k:k + 1],
                                             h_hi[:, k].bitcast(F32), ALU.mult, ALU.subtract)\
                        .then_inc(t_lo.sem, 1)
                dve.wait_ge(x_in.sem, x_in.at(pos, 0))
                norm_x(pos, 3 * NC - 1)
                for c in range(NC):
                    part = x2[:, c, 0:512]
                    dve.wait_ge(ple_gate.sem, ple_gate.at(pos, c))
                    dve.tensor_tensor(sg[:, c], sg[:, c], up0[:, c], ALU.mult).then_inc(up_gated.sem, 1)
                    dve.wait_ge(up_gated.sem, up_gated.at(pos, c))
                    dve.tensor_tensor(part, part, sg[:, c], ALU.add).then_inc(x3_sum.sem, 1)
                dve.wait_ge(unit_done.sem, unit_done.at(pos, U_UP1))
                for c in range(NC):
                    dve.wait_ge(ple_gate.sem, ple_gate.at(pos, NC + c))
                    dve.tensor_tensor(sg[:, c], sg[:, c], bank[half_bank(1, c)][:], ALU.mult)\
                        .then_inc(up_gated.sem, 1)
                x_los(pos)
                dve.wait_ge(up_gated.sem, up_gated.at(pos, 2 * NC - 1))
                for c in range(NC):
                    part = x2[:, c, 512:1024]
                    dve.tensor_tensor(part, part, sg[:, c], ALU.add).then_inc(x3_sum.sem, 1)
                inv_rms(pos, ms, meansq, 1, rr, rq, DM, squares, squares.at(pos, 5 * NC - 1),
                        root, root.at(pos, 1), halves=True)
                dve.wait_ge(fg_in.sem, fg_in.at(pos, 0))
                for c in range(NC):
                    dve.scalar_tensor_tensor(xs2[:, c], x2[:, c], rq[:, c:c + 1], fg[:], ALU.mult, ALU.mult)\
                        .then_inc(out_full.sem, 1)
                links_done("O")

        @block.tensor
        def _(pe):
            def three(out_, lhs, rhs, start, stop):
                (lh, ll), (rh, rl) = lhs, rhs
                pe.matmul(out_, lh, rh, start=start, stop=False)
                pe.matmul(out_, lh, rl, start=False, stop=False)
                return pe.matmul(out_, ll, rh, start=False, stop=stop)

            def unit(pos, k, parts):
                pe.wait_ge(w_ready.sem, w_ready.at(pos, k))
                s = slot(pos, k)
                return [w[s][:].rearrange("p (a b) -> p a b", a=parts) for w in (w_hi, w_lo)]

            def stationary_unit(pos, k, dst, moving):
                hi, lo = unit(pos, k, KT)
                for i in range(KT):
                    last = three(dst, (hi[:, i], lo[:, i]), (moving[0][:, i], moving[1][:, i]),
                                 i == 0, i == KT - 1)
                last.then_inc(unit_done.sem, 1)

            def moving_unit(pos, k, dsts, still, k0, ktiles, ready=None):
                hi, lo = unit(pos, k, 2)
                for i in range(2):
                    kt = k0 + i
                    if ready:
                        ready(kt)
                    for c in range(NC):
                        part = slice(c * P, (c + 1) * P)
                        last = three(dsts[c][:], (still[0][:, kt, part], still[1][:, kt, part]),
                                     (hi[:, i], lo[:, i]), kt == 0, kt == ktiles - 1)
                last.then_inc(unit_done.sem, 1)

            def transposes(dst, src, first):
                for c in range(NC):
                    last = pe.transpose(dst[:, c * P:(c + 1) * P], src[:, c, first:first + P], ident[:])
                return last

            H = (h_hi, h_lo)

            def next_x(pos):
                pe.wait_ge(xs_full.sem, xs_full.at(pos, NC - 1))
                for k in range(KT):
                    if pos.phase == "O":
                        if k < 4:
                            pe.wait_ge(ple_gate.sem, ple_gate.at(pos, NC + k))
                        else:
                            pe.wait_ge(up_gated.sem, up_gated.at(pos, k))
                    transposes(bank[k], xs, k * P).then_inc(x_psum.sem, 1)
                for k in range(KT):
                    pe.wait_ge(x_lo.sem, x_lo.at(pos, max(k, DT_BANK)))
                    last = three(bank[DT_BANK][:], (wdt_hi[:, k * HEADS:k * HEADS + P],
                                                    wdt_lo[:, k * HEADS:k * HEADS + P]),
                                 (h_hi[:, k], h_lo[:, k]), k == 0, k == KT - 1)
                last.then_inc(dt_psum.sem, 1)

            def y_transposes(pos):
                pe.wait_ge(y_normed.sem, y_normed.at(pos, NC - 1))
                for k in range(GT):
                    transposes(bank[2 + k], zs, k * P).then_inc(yt_psum.sem, 1)

            def branch_a(pos, first, q):
                hi, lo = unit(pos, first + q, GT)
                for s in range(2):
                    j = 2 * q + s
                    if j >= 3:
                        pe.wait_ge(acc_added.sem, acc_added.at(pos, j - 3))
                    cols_ = slice(s * P, (s + 1) * P)
                    for i in range(GT):
                        last = three(bank[acc_bank(j)][:], (hi[:, i, cols_], lo[:, i, cols_]),
                                     (ya_hi[:, i], ya_lo[:, i]), i == 0, i == GT - 1)
                last.then_inc(unit_done.sem, 1)

            def group(pos, g):
                prev = pos.phase == "G"
                for t in range(6):
                    if t >= 2:
                        pe.wait_ge(cbuf_full.sem, cbuf_full.at(pos, t - 2))
                    elif prev:
                        pe.wait_ge(mix_read.sem, mix_read.at(pos, t, back=2))
                        pe.wait_ge(acc_added.sem, acc_added.at(pos, t, back=2))
                    stationary_unit(pos, t, bank[t % 2][:], H)
                    if t == 3 and prev:
                        y_transposes(pos)
                if not prev:
                    pe.wait_ge(dt_full.sem, dt_full.at(pos, 0))
                    on_its_own(pe)
                    for n_, src in enumerate((dtw[0], dtw[6])):
                        for c in range(NC):
                            at = (n_ * NC + c) * HEADS
                            last = pe.transpose(bank[TOK_BANK][:, at:at + HEADS],
                                                src[:, c * P:(c + 1) * P], ident[0:HEADS, 0:HEADS])
                    last.then_inc(tok_psum.sem, 1)

                def chunk_in(c):
                    part = slice(c * P, (c + 1) * P)
                    pe.wait_ge(xt_full.sem, xt_full.at(pos, c, back=1))
                    if c == 0:
                        pe.wait_ge(silu_done.sem, silu_done.at(pos, 5))
                        if not prev:
                            pe.wait_ge(tok_full.sem, tok_full.at(pos, 0))
                    for j in range(GT):
                        last = pe.transpose(bank[6][:, j * P:(j + 1) * P], xc[:, j, part], ident[:])
                    last.then_inc(xt_psum.sem, 1)
                    pe.wait_ge(bt_full.sem, bt_full.at(pos, 2 * c, back=1))
                    pe.transpose(bank[7][:, 0:P], bc[0][:, part], ident[:])
                    pe.matmul(bank[7][:, P:2 * P], bc[0][:, part], bc[1][:, part], start=True, stop=True)\
                        .then_inc(bcb_psum.sem, 1)

                def chunk_out(c):
                    part = slice(c * P, (c + 1) * P)
                    if c == 0:
                        pe.wait_ge(z_silu.sem, z_silu.at(pos, NC - 1))
                    pe.wait_ge(xdt_full.sem, xdt_full.at(pos, c))
                    pe.wait_ge(state_new.sem, state_new.at(pos, c, back=1))
                    pe.matmul(bank[4][:], bt[c % 2][:], xdd[c % 2][:], start=True, stop=True)\
                        .then_inc(ssd_psum.sem, 1)
                    if c:
                        pe.wait_ge(y_gated.sem, y_gated.at(pos, c - 1))
                    pe.matmul(bank[3][:], bc[1][:, part], one(state, g), start=True, stop=True)\
                        .then_inc(ssd_psum.sem, 1)
                    pe.wait_ge(m_full.sem, m_full.at(pos, c))
                    for h in range(HG):
                        cols_ = slice(h * HD, (h + 1) * HD)
                        last = pe.matmul(bank[2][:, cols_], m[c % 3][:, h * P:(h + 1) * P],
                                         xdt[c % 2][:, cols_], start=True, stop=True)
                    last.then_inc(ssd_psum.sem, 1)

                for k in range(PT):
                    pe.wait_ge(cbuf_full.sem, cbuf_full.at(pos, 4 + k))
                    stationary_unit(pos, U_ZP + k, bank[k][:], H)
                for k in range(PT):
                    pe.wait_ge(zp_full.sem, zp_full.at(pos, k))
                    stationary_unit(pos, U_U + k, bank[k][:], H)
                chunk_in(0)
                if prev:
                    pe.wait_ge(ya_full.sem, ya_full.at(pos, GT - 1))
                for k in range(4):
                    if k == 2:
                        chunk_in(1)
                    if k == 3:
                        pe.wait_ge(pooled.sem, pooled.at(pos, PT - 1))
                        pe.wait_ge(mx_full.sem, mx_full.at(pos, 0))
                        for j in range(PT):
                            pe.wait_ge(u_full.sem, u_full.at(pos, j))
                            cols_ = slice(j * P, (j + 1) * P)
                            for i in range(PT):
                                last = three(bank[j][:], (mx_hi[:, i, cols_], mx_lo[:, i, cols_]),
                                             (pl_hi[:, i], pl_lo[:, i]), i == 0, i == PT - 1)
                            last.then_inc(mix_psum.sem, 1)
                    moving_unit(pos, U_Z + k, bank[2:6], H, 2 * k, KT)
                if prev:
                    pe.wait_ge(mix_read.sem, mix_read.at(pos, PT - 1))
                for c in range(NC):
                    if prev:
                        if c == 1:
                            pe.wait_ge(z_silu.sem, z_silu.at(pos, NC - 1))
                        branch_a(pos, U_A, c)
                    chunk_out(c)
                    if c + 2 < NC:
                        chunk_in(c + 2)

            pe.sem_inc(unit_done.sem, RING)
            pe.sem_inc(mix_psum.sem, 1)
            pe.wait_ge(consts, 8)
            pe.wait_ge(setup_done, 1)
            next_x(Pos("PRE", 0, 0))
            with pe.Fori(0, NB) as b:
                group(Pos("F", b, 0), 0)
                with pe.Fori(0, GROUPS - 1) as i:
                    group(Pos("G", b, i), i + 1)
                pos = Pos("W", b, 0)
                y_transposes(pos)
                pe.wait_ge(ya_full.sem, ya_full.at(pos, GT - 1))
                for q in range(4):
                    branch_a(pos, 0, q)
                pe.wait_ge(acc_added.sem, acc_added.at(pos, 5))
                on_its_own(pe)
                with pe.Fori(0, KT // 2) as jj:
                    pos = Pos("J", b, jj)
                    for s in range(2):
                        pe.wait_ge(merged.sem, merged.at(pos, s, back=2))
                        stationary_unit(pos, 3 * s, bank[2 + 3 * s][:], H)
                        stationary_unit(pos, 3 * s + 1, bank[3 + 3 * s][:], H)
                        stationary_unit(pos, 3 * s + 2, bank[4 + 3 * s][:], (yb_hi, yb_lo))
                pos = Pos("O", b, 0)

                def half(h):
                    return [bank[half_bank(h, c)] for c in range(NC)]

                pe.wait_ge(merged.sem, merged.start_of(pos, "O") - 1)
                for h in range(2):
                    for k in range(4):
                        if (h, k) == (0, 3):
                            pe.wait_ge(merged.sem, merged.start_of(pos, "O"))
                        if (h, k) == (1, 2):
                            pe.wait_ge(x2_sum.sem, x2_sum.at(pos, NC - 1))
                            pe.wait_ge(pin_in.sem, pin_in.at(pos, 0))
                            for i in range(2):
                                transposes(bank[i], pin, i * P).then_inc(t_psum.sem, 1)
                        moving_unit(pos, 4 * h + k, half(h), (m_hi, m_lo), 2 * k, KT)
                pe.wait_ge(t_lo.sem, t_lo.at(pos, 1))
                moving_unit(pos, U_UP0, half(0), (p_hi, p_lo), 0, 2)
                pe.wait_ge(xs2_full.sem, xs2_full.at(pos, NC - 1))
                for k in range(KT):
                    if k >= 4:
                        pe.wait_ge(up0_full.sem, up0_full.at(pos, k - 4))
                    transposes(bank[(4 + k) % 8], xs2, k * P).then_inc(t_psum.sem, 1)
                pe.wait_ge(t_lo.sem, t_lo.at(pos, 2 + 3))
                for k in range(4):
                    moving_unit(pos, U_GATE + k, half(1), H, 2 * k, KT,
                                ready=lambda kt: pe.wait_ge(t_lo.sem, t_lo.at(pos, 2 + kt)))
                for k in range(4):
                    moving_unit(pos, U_GATE + 4 + k, half(0), H, 2 * k, KT)
                pe.wait_ge(ple_gate.sem, ple_gate.at(pos, NC - 1))
                moving_unit(pos, U_UP1, half(1), (p_hi, p_lo), 0, 2)
                next_x(pos)

INPUTS = ["x", "p", "norm_g", "w_in", "conv_w", "conv_b", "dt_bias", "a_log", "d_skip", "gnorm_g",
          "pool_mix_w", "pool_mix_b", "pool_scale", "w_branch_a", "w_branch_b", "w_out",
          "ple_norm_g", "w_ple_gate", "w_ple_up", "final_g"]


def kernel(**inputs):
    import concourse.bacc as bacc
    from concourse.bass_utils import run_bass_kernel_spmd

    nc = bacc.Bacc("TRN2", target_bir_lowering=False, num_devices=1)
    arrays, args = {}, []
    for name in INPUTS:
        a = np.ascontiguousarray(inputs[name])
        arrays[f"in_{name}"] = a
        args.append(nc.dram_tensor(f"in_{name}", a.shape, mybir.dt.from_np(a.dtype),
                                   kind="ExternalInput").ap())
    args.append(nc.dram_tensor("out", (1, SEQ, DM), F32, kind="ExternalOutput").ap())
    build(nc, *args)
    result = run_bass_kernel_spmd(nc, [arrays], core_ids=[0])
    return result.results[0]["out"]
```

```python
from collections import namedtuple
from contextlib import ExitStack

import concourse.bass as bass
import numpy as np
from concourse import mybir
from concourse.alu_op_type import AluOpType as ALU

ACT = mybir.ActivationFunctionType
F32 = mybir.dt.float32
F32R = mybir.dt.float32r
BF16 = mybir.dt.bfloat16

P = 128
SEQ, DM, PLE = 2048, 1024, 256
DI = 2 * DM
HEADS, HD, GROUPS, NS = 32, 64, 4, 128
HG = HEADS // GROUPS
GC = DI // GROUPS
TAPS = 4
T = 512
NB = SEQ // T
NC = T // P
KT = DM // P
GT = GC // P
PG = DM // GROUPS
PT = PG // P
EPS = 1e-6
COL_Z, COL_X = 0, DI
COL_B = COL_X + DI
COL_C = COL_B + GROUPS * NS
COL_DT = COL_C + GROUPS * NS
COL_U = COL_DT + HEADS
COL_ZP = COL_U + DM
COL_GA = COL_ZP + DM
COL_GB = COL_GA + DM
ATANH = [1.0 / (2 * k + 1) for k in range(1, 8)]

UW = 1024
RING = 3
U_B, U_C, U_X, U_ZP, U_U, U_Z, U_A = 0, 1, 2, 6, 8, 10, 14
F_Z, F_U, F_ZP = 6, 10, 12
W_GA, W_GB, W_A = 0, 1, 2
J_WB, J_GA, J_GB = (0, 3), (1, 4), (2, 5)
U_UP0, U_GATE, U_UP1 = 8, 9, 17
PHASES = "FGWJKO"
TRIPS = {"F": 1, "G": GROUPS - 1, "W": 1, "J": KT // 2 - 1, "K": 1, "O": 1}
UNITS = {"F": U_A, "G": 18, "W": 6, "J": 6, "K": 4, "O": 18}
UNIT_0 = {}
_n = 0
for _ph in PHASES:
    UNIT_0[_ph] = _n
    _n += UNITS[_ph] * TRIPS[_ph]
BLOCK_UNITS = _n
assert BLOCK_UNITS % (2 * RING) == 0 and UNITS["G"] % RING == 0 and UNITS["J"] % RING == 0
N_LOADS = 11
X_BANK = (4, 5, 6, 7, 0, 1, 2, 3)
X2_BANK = (0, 1, 0, 1, 4, 5, 6, 7)
GA_BANK, GB_BANK, WB_BANK = (6, 3), (7, 4), (2, 5)
F_MIX_BANK = (6, 7)
DT_BANK, TOK_BANK = 4, 7


def half_bank(h, c):
    return 4 * h + c


def projection_bank(pos, t):
    return t % 4 if pos.phase == "F" else t % 2


def x2_order(k):
    return k if k < 2 else k + 2


def acc_bank(j):
    return (0, 1, 5)[j % 3]


Pos = namedtuple("Pos", "phase b i")


def slot(pos, k):
    return (UNIT_0[pos.phase] + k) % RING


def loaded_at(pos, k):
    value = pos.b * (16 * BLOCK_UNITS // RING) + 16 * ((UNIT_0[pos.phase] + k) // RING + 1)
    if TRIPS[pos.phase] > 1:
        value = value + pos.i * (16 * UNITS[pos.phase] // RING)
    return value


class Signal:

    def __init__(self, sem, credit=0, step=1, pre=0, **turns):
        self.sem, self.credit, self.step, self.pre = sem, credit, step, pre
        self.n = {ph: turns.get(ph, 0) for ph in PHASES}
        self.total = sum(self.n[ph] * TRIPS[ph] for ph in PHASES)

    def before(self, phase):
        n = self.credit + self.pre
        for ph in PHASES:
            if ph == phase:
                break
            n += self.n[ph] * TRIPS[ph]
        return n

    def at(self, pos, k, back=0):
        if pos.phase == "PRE":
            return self.step * (self.credit + k + 1 - back)
        value = pos.b * (self.step * self.total) + self.step * (self.before(pos.phase) + k + 1 - back)
        if TRIPS[pos.phase] > 1 and self.n[pos.phase]:
            value = value + pos.i * (self.step * self.n[pos.phase])
        return value

    def start_of(self, pos, phase):
        return pos.b * (self.step * self.total) + self.step * self.before(phase)


def build(nc, x, p, norm_g, w_in, conv_w, conv_b, dt_bias, a_log, d_skip, gnorm_g, pool_mix_w,
          pool_mix_b, pool_scale, w_branch_a, w_branch_b, w_out, ple_norm_g, w_ple_gate,
          w_ple_up, final_g, out):
    ctx = ExitStack()
    with ctx:
        base = [16512]

        def sb(name, shape, dt=F32, at=None):
            size = int(np.prod(shape[1:])) * (2 if dt == BF16 else 4)
            size = (size + 31) // 32 * 32
            if at is None:
                at = base[0]
                base[0] += size
            assert at + size <= nc.sbuf_usable_end, (name, at + size)
            return nc.alloc_sbuf_tensor_at(name, shape, dt, offset=at)

        KB = 1024
        h_hi = sb("h_hi", [P, KT, T], F32R)
        h_lo = sb("h_lo", [P, KT, T], F32R)
        wring = base[0]
        w_hi = [sb(f"w_hi{s}", [P, UW], F32R) for s in range(RING)]
        w_raw = [sb(f"w_raw{s}", [P, UW]) for s in range(RING)]
        w_lo = [sb(f"w_lo{s}", [P, UW], F32R, at=wring + (RING + s) * UW * 4) for s in range(RING)]
        state = sb("state", [P, GROUPS, GC])
        yb_at = base[0]
        yb_hi = sb("yb_hi", [P, KT, T], F32R)
        yb_lo = sb("yb_lo", [P, KT, T], F32R)
        acc_at = base[0]
        a_acc = sb("a_acc", [P, KT, T])
        ya_at = base[0]
        ya_hi = sb("ya_hi", [P, GT, T], F32R)
        ya_lo = sb("ya_lo", [P, GT, T], F32R)
        zps = sb("zps", [P, KT, T], at=yb_at)
        plf_hi = sb("plf_hi", [P, PT, T], F32R, at=ya_at)
        plf_lo = sb("plf_lo", [P, PT, T], F32R, at=ya_at + PT * T * 4)
        NDT = (KT + 3) * HEADS
        wdt_hi = sb("wdt_hi", [P, NDT], F32R)
        wdt_lo = sb("wdt_lo", [P, NDT], F32R)
        conv_halo = sb("conv_halo", [P, GROUPS, 6, TAPS - 1])
        pool_halo = sb("pool_halo", [P, GROUPS, PT, 16])
        ident = sb("ident", [P, P])
        cap = sb("cap", [P, P])
        tok_dt = sb("tok_dt", [P, NC, HEADS])
        tok_acs = sb("tok_acs", [P, NC, HEADS])
        exp_acs = sb("exp_acs", [P, NC, HEADS])
        par = sb("par", [P, 2 * P])
        NT = (DI + 2 * GROUPS * NS) // P
        taps = par[:, 0:(TAPS + 1) * NT].rearrange("p (j n) -> p j n", n=NT)
        mixb = par[:, (TAPS + 1) * NT:P].rearrange("p (g k) -> p g k", k=PT)
        ng = par[:, P:P + KT]
        pg = par[:, P + KT:P + 2 * KT]
        gn = par[:, P + 2 * KT:P + 4 * KT].rearrange("p (g k) -> p g k", k=GT)
        pscale = par[:, P + 4 * KT:P + 5 * KT].rearrange("p (g k) -> p g k", k=PT)
        assert (TAPS + 1) * NT + KT == P
        dskip = sb("dskip", [P, HEADS])
        dtb = sb("dtb", [HEADS, 1])
        aneg = sb("aneg", [HEADS, 2])
        inv16 = sb("inv16", [P, GROUPS, 16])
        invw = sb("invw", [P, GROUPS])
        ssx, rrx, rqx = (sb(n, [P, NC]) for n in ("ssx", "rrx", "rqx"))
        ss = sb("ss", [P, 2, NC])
        ms, rr, rq = (sb(n, [P, NC]) for n in ("ms", "rr", "rq"))
        ssy, rry, rqy = (sb(n, [P, NC]) for n in ("ssy", "rry", "rqy"))
        junk = sb("junk", [P, DM], BF16)
        junk_root = sb("junk_root", [P, 8])
        junk_y = sb("junk_y", [P, GC], BF16)
        tmp = base[0]
        xc = sb("xc", [P, GT, T])
        zs_at = base[0]
        zs = sb("zs", [P, NC, GC])
        pl_hi = sb("pl_hi", [P, PT, T], F32R, at=zs_at)
        pl_lo = sb("pl_lo", [P, PT, T], F32R, at=zs_at + PT * T * 4)
        cbuf = [sb(f"cbuf{s}", [P, TAPS - 1 + T]) for s in range(2)]
        bc = [sb("b_ch", [P, T]), sb("c_ch", [P, T])]
        ubuf = [sb(f"ubuf{j}", [P, 16 + T]) for j in range(PT)]
        cs = sb("cs", [P, 16 + T])
        pf = sb("pf", [P, T])
        bt = [sb(f"bt{s}", [P, P]) for s in range(2)]
        cbs = [sb(f"cbs{s}", [P, P]) for s in range(2)]
        mx_hi = sb("mx_hi", [P, PT, PG], F32R)
        mx_at = base[0]
        mx_raw = sb("mx_raw", [P, PT, PG])
        mx_lo = sb("mx_lo", [P, PT, PG], F32R, at=mx_at)
        assert base[0] - tmp >= 32 * KB
        late = base[0]
        MX = HG * P
        m = [sb(f"m{s}", [P, MX + 2 * HG]) for s in range(NC)]
        dt_at = base[0]
        xt = [sb(f"xt{s}", [P, GC]) for s in range(2)]
        xdt = [sb(f"xdt{s}", [P, GC]) for s in range(2)]
        xdd = [sb(f"xdd{s}", [P, GC]) for s in range(2)]
        xin = sb("xin", [P, NC, DM], at=tmp)
        xs = sb("xs", [P, NC, DM], at=tmp + 16 * KB)
        dtw = [sb(f"dtw{s}", [HEADS, T], at=dt_at + 2 * s * KB) for s in range(7)]
        wdt_raw = sb("wdt_raw", [P, NDT], at=late)
        pos16 = sb("pos16", [P, 16], at=late + 2 * KB)
        par_rows = [sb(f"par_rows{s}", [P, P], at=late + (3 + s) * KB) for s in range(2)]
        m_hi = sb("m_hi", [P, KT, T], F32R, at=tmp)
        m_lo = sb("m_lo", [P, KT, T], F32R, at=tmp + 16 * KB)
        sga = [sb(f"sga{s}", [P, T], at=late + 4 * s * KB) for s in range(2)]
        sgb = [sb(f"sgb{s}", [P, T], at=late + (2 + 4 * s) * KB) for s in range(2)]
        x2 = sb("x2", [P, NC, DM], at=acc_at)
        y_out = sb("y_out", [P, NC, DM], at=ya_at)
        pin = sb("pin", [P, NC, PLE], at=yb_at)
        p_hi = sb("p_hi", [P, 2, T], F32R, at=yb_at + 4 * KB)
        p_lo = sb("p_lo", [P, 2, T], F32R, at=yb_at + 8 * KB)
        fg = sb("fg", [P, DM], at=yb_at + 12 * KB)
        sg = sb("sg", [P, NC, T], at=yb_at + 16 * KB)
        up0 = sb("up0", [P, NC, T], at=yb_at + 24 * KB)


        bank = [ctx.enter_context(nc.psum_tensor(f"bank{i}", [P, 512], F32)) for i in range(8)]
        acs_dram = nc.dram_tensor("acs_scratch", (NB, HEADS, T), F32).ap()

        def sig(name, **counts):
            return Signal(ctx.enter_context(nc.semaphore(name)), **counts)

        passed = ctx.enter_context(nc.semaphore("passed"))
        params_in = ctx.enter_context(nc.semaphore("params_in"))
        w_loaded = [ctx.enter_context(nc.semaphore(f"w_loaded{s}")) for s in range(RING)]
        x_in = [sig(f"x_in{c}", pre=1, O=1, step=16) for c in range(NC)]
        acs_out = sig("acs_out", F=1, step=16)
        rows_in = [sig(f"rows_in{c}", F=1, G=1, step=16) for c in range(NC)]
        mix_in = sig("mix_in", F=1, G=1, step=16)
        x2_in = [sig(f"x2_in{c}", O=1, step=16) for c in range(NC)]
        pin_in = sig("pin_in", O=1, step=16)
        fg_in = sig("fg_in", O=1, step=16)
        out_done = sig("out_done", O=NC, credit=1, step=16)
        consts = ctx.enter_context(nc.semaphore("consts"))
        acc_zero = sig("acc_zero", F=1)
        w_ready = sig("w_ready", **UNITS)
        w_hi_done = ctx.enter_context(nc.semaphore("w_hi_done"))
        squares = sig("squares", pre=NC, O=5 * NC, credit=1)
        root = sig("root", O=2)
        root_table = sig("root_table", pre=1, F=1, G=1, O=1)
        root_x = sig("root_x", pre=1, O=1)
        x_hi = sig("x_hi", pre=KT, O=KT)
        t_hi = sig("t_hi", O=2 + KT)
        dt_exp = sig("dt_exp", F=1)
        acs_exp = sig("acs_exp", F=1)
        a_exp = ctx.enter_context(nc.semaphore("a_exp"))
        cbuf_full = sig("cbuf_full", F=6, G=6)
        first_tap = sig("first_tap", F=6, G=6)
        silu_done = sig("silu_done", F=6, G=6)
        z_silu = sig("z_silu", F=NC, G=NC)
        decay = sig("decay", F=NC, G=NC)
        xt_full = sig("xt_full", F=NC, G=NC, credit=1)
        bt_full = sig("bt_full", F=2 * NC, G=2 * NC, credit=1)
        zp_full = sig("zp_full", F=PT, G=PT)
        u_full = sig("u_full", F=PT, G=PT)
        pl_hi_done = sig("pl_hi_done", F=PT, G=PT)
        yb_hi_done = sig("yb_hi_done", F=PT, G=PT)
        mx_hi_done = sig("mx_hi_done", F=1, G=1)
        y_squares = sig("y_squares", F=NC, G=NC, credit=1)
        y_root = sig("y_root", F=1, G=1)
        ya_hi_done = sig("ya_hi_done", G=GT, W=GT)
        gates = sig("gates", W=2, J=4, K=2)
        m_hi_done = sig("m_hi_done", J=2, K=2)
        up0_full = sig("up0_full", O=2)
        ple_gate = sig("ple_gate", O=2 * NC)
        link_s = sig("vector_link", F=61, G=45, W=1, J=4, K=4, O=5)
        setup_link = ctx.enter_context(nc.semaphore("setup_link"))
        setup_done = ctx.enter_context(nc.semaphore("setup_done"))
        meansq = sig("meansq", O=2)
        up0_full_v = sig("up0_full_v", O=2)
        meansq_x = sig("meansq_x", pre=1, O=1)
        xs_full = sig("xs_full", pre=NC, O=NC)
        x_lo = sig("x_lo", pre=KT, O=KT)
        rms_x2 = sig("rms_x2", O=1)
        par_full = ctx.enter_context(nc.semaphore("par_full"))
        t_lo = sig("t_lo", O=2 + KT)
        dt_abs = sig("dt_abs", F=1)
        dt_full = sig("dt_full", F=1)
        tok_full = sig("tok_full", F=1)
        conv_done = sig("conv_done", F=6, G=6, credit=2)
        seg_full = sig("seg_full", F=NC, G=NC)
        xdt_full = sig("xdt_full", F=NC, G=NC)
        m_full = sig("m_full", F=NC, G=NC)
        y_gated = sig("y_gated", F=NC, G=NC, credit=2)
        y_read = sig("y_read", F=NC, G=NC)
        state_new = sig("state_new", F=NC, G=NC, credit=1)
        pf_full = sig("pf_full", F=PT, G=PT)
        pooled = sig("pooled", F=PT, G=PT)
        mx_full = sig("mx_full", F=1, G=1)
        mix_read = sig("mix_read", F=PT, G=PT)
        yb_val = sig("yb_val", F=PT, G=PT)
        yb_full = sig("yb_full", F=PT, G=PT)
        y_meansq = sig("y_meansq", F=1, G=1)
        y_normed = sig("y_normed", G=NC, W=NC)
        ya_full = sig("ya_full", G=GT, W=GT)
        acc_added = sig("acc_added", G=KT, W=KT, credit=2)
        m_val = sig("m_val", J=2, K=2)
        merged = sig("merged", J=2, K=2, credit=2)
        x2_sum = sig("x2_sum", O=2 * NC)
        up_gated = sig("up_gated", O=2 * NC)
        x3_sum = sig("x3_sum", O=2 * NC)
        out_full = sig("out_full", O=NC, credit=1)
        unit_done = sig("unit_done", credit=RING, **UNITS)
        x_psum = sig("x_psum", pre=KT, O=KT)
        par_psum = ctx.enter_context(nc.semaphore("par_psum"))
        t_psum = sig("t_psum", O=2 + KT)
        dt_psum = sig("dt_psum", pre=1, O=1)
        tok_psum = sig("tok_psum", F=1)
        xt_psum = sig("xt_psum", F=NC, G=NC)
        bcb_psum = sig("bcb_psum", F=NC, G=NC)
        ssd_psum = sig("ssd_psum", F=3 * NC, G=3 * NC)
        mix_psum = sig("mix_psum", F=PT, G=PT, credit=1)
        yt_psum = sig("yt_psum", G=GT, W=GT)

        xb = x.rearrange("a (b c p) d -> (a b) p c d", c=NC, p=P)
        ob = out.rearrange("a (b c p) d -> (a b) c p d", c=NC, p=P)
        pb = p.rearrange("l a (b c p) d -> (l a b) p c d", c=NC, p=P)
        win = w_in.rearrange("l (k p) n -> p (l k) n", p=P)
        wa = w_branch_a.rearrange("l (g k p) n -> p (l g) k n", g=GROUPS, p=P)
        wb = w_branch_b.rearrange("l (k p) n -> p (l k) n", p=P)
        wo = w_out.rearrange("l (k p) n -> p (l k) n", p=P)
        wg = w_ple_gate.rearrange("l (k p) n -> p (l k) n", p=P)
        wu = w_ple_up.rearrange("l (k p) n -> p (l k) n", p=P)
        mixw = pool_mix_w.rearrange("l g (k p) n -> p (l g) k n", p=P)

        def one(ap, i):
            if isinstance(i, int):
                return ap[:, i]
            view = ap[:, bass.ds(i, 1)]
            names = "abcd"[: len(view.shape) - 2]
            return view.rearrange(f"p x {' '.join(names)} -> p (x {names[0]}) {' '.join(names[1:])}")

        def col(ap, i, j):
            return ap[:, bass.ds(i, 1), j:j + 1].rearrange("p a b -> p (a b)")

        def conv_tile(g, t):
            tile = g + (DI // P + GROUPS * t) if t < 2 else g * GT + (t - 2)
            return (bc[t][:] if t < 2 else xc[:, t - 2],
                    [taps[:, j, bass.ds(tile, 1)] for j in range(TAPS + 1)],
                    conv_halo[:, bass.ds(g, 1), t, :].rearrange("p a n -> p (a n)"))

        def heads(ap):
            return ap.rearrange("p (h d) -> p h d", h=HG)

        def per_head(ap, n):
            return ap.unsqueeze(2).to_broadcast([P, HG, n])

        def on_its_own(eng):
            eng.sem_inc(passed, 1)

        block = ctx.enter_context(nc.Block())


        @block.sync
        def _(sp):
            for c in range(NC):
                sp.dma_start(xin[:, c], xb[0, :, c]).then_inc(x_in[c].sem, 16)
            rows_a, rows_b = par_rows
            loads = [
                (rows_a[0:TAPS * NT], conv_w.rearrange("l j (n p) -> (l j n) p", p=P)),
                (rows_a[TAPS * NT:(TAPS + 1) * NT], conv_b.rearrange("l (n p) -> (l n) p", p=P)),
                (rows_a[(TAPS + 1) * NT:P], pool_mix_b.rearrange("l (n p) -> (l n) p", p=P)),
                (rows_b[0:KT], norm_g.rearrange("l (n p) -> (l n) p", p=P)),
                (rows_b[KT:2 * KT], ple_norm_g.rearrange("l (n p) -> (l n) p", p=P)),
                (rows_b[2 * KT:4 * KT], gnorm_g.rearrange("l (n p) -> (l n) p", p=P)),
                (rows_b[4 * KT:5 * KT], pool_scale.rearrange("l (n p) -> (l n) p", p=P)),
                (dtb[:], dt_bias.rearrange("l (h a) -> (l h) a", a=1)),
                (aneg[:, 0:1], a_log.rearrange("l (h a) -> (l h) a", a=1)),
                (dskip[:], d_skip.rearrange("l h -> (l h)").partition_broadcast(P)),
                (wdt_raw[:, 0:KT * HEADS].rearrange("p (k h) -> p k h", k=KT),
                 win[:, :, COL_DT:COL_DT + HEADS]),
            ]
            assert len(loads) == N_LOADS
            sp.wait_ge(consts, 1)
            for dst, src in loads:
                sp.dma_start(dst, src, allow_slow_non_contiguous=True).then_inc(params_in, 16)

            def load_unit(pos, k, src, parts):
                sp.wait_ge(unit_done.sem, unit_done.at(pos, k, back=RING))
                on_its_own(sp)
                s = slot(pos, k)
                dst = w_raw[s][:].rearrange("p (a b) -> p a b", a=parts)
                sp.dma_start(dst, src).then_inc(w_loaded[s], 16)

            def cols(first, i, stride=P):
                return win[:, :, bass.ds(i * stride + first, P)]

            def group(pos, g):
                load_unit(pos, U_B, cols(COL_B, g), KT)
                load_unit(pos, U_C, cols(COL_C, g), KT)
                load_unit(pos, U_X, cols(COL_X, g, GC), KT)
                if pos.phase == "F":
                    sp.wait_ge(x_psum.sem, x_psum.start_of(pos, "F"))
                    on_its_own(sp)
                sp.wait_ge(mix_psum.sem, mix_psum.at(pos, 0, back=1))
                on_its_own(sp)
                sp.dma_start(mx_raw[:], one(mixw, g)).then_inc(mix_in.sem, 16)
                for j in range(1, GT):
                    load_unit(pos, U_X + j, cols(COL_X + j * P, g, GC), KT)

                def z(first):
                    for k in range(4):
                        load_unit(pos, first + k, win[:, 2 * k:2 * k + 2, bass.ds(g * GC, GC)], 2)

                def pair(first, column):
                    for j in range(PT):
                        load_unit(pos, first + j, cols(column + j * P, g, PG), KT)

                if pos.phase == "F":
                    z(F_Z)
                    pair(F_U, COL_U)
                    pair(F_ZP, COL_ZP)
                else:
                    pair(U_ZP, COL_ZP)
                    pair(U_U, COL_U)
                    z(U_Z)

            def branch_a(pos, first, g):
                for k in range(4):
                    load_unit(pos, first + k, one(wa, g)[:, :, 256 * k:256 * k + 256], GT)

            with sp.Fori(0, NB) as b:
                group(Pos("F", b, 0), 0)
                with sp.Fori(0, GROUPS - 1) as i:
                    pos = Pos("G", b, i)
                    group(pos, i + 1)
                    branch_a(pos, U_A, i)
                pos = Pos("W", b, 0)
                load_unit(pos, W_GA, win[:, :, COL_GA:COL_GA + P], KT)
                load_unit(pos, W_GB, win[:, :, COL_GB:COL_GB + P], KT)
                branch_a(pos, W_A, GROUPS - 1)

                def merge_units(pos, jj, s, with_gates=True):
                    load_unit(pos, J_WB[s], wb[:, :, bass.ds(jj * (2 * P) + s * P, P)], KT)
                    if with_gates:
                        load_unit(pos, J_GA[s], cols(COL_GA + (s + 1) * P, jj, 2 * P), KT)
                        load_unit(pos, J_GB[s], cols(COL_GB + (s + 1) * P, jj, 2 * P), KT)

                with sp.Fori(0, KT // 2 - 1) as jj:
                    for s in range(2):
                        merge_units(Pos("J", b, jj), jj, s)
                for s in range(2):
                    merge_units(Pos("K", b, 0), KT // 2 - 1, s, with_gates=s == 0)
                pos = Pos("O", b, 0)

                def quarter(k, w, first, h):
                    load_unit(pos, first + k, w[:, 2 * k:2 * k + 2, 512 * h:512 * h + 512], 2)

                def chunks(dst, src, sems, which):
                    for c in which:
                        sp.dma_start(dst[:, c], src[:, :, c].rearrange("b p d -> (b p) d"))\
                            .then_inc(sems[c].sem, 16)

                quarter(0, wo, 0, 0)
                quarter(1, wo, 0, 0)
                sp.wait_ge(merged.sem, merged.start_of(pos, "O"))
                on_its_own(sp)
                quarter(2, wo, 0, 0)
                chunks(x2, xb[bass.ds(b, 1)], x2_in, (0, 1))
                quarter(3, wo, 0, 0)
                chunks(x2, xb[bass.ds(b, 1)], x2_in, (2, 3))
                quarter(0, wo, 4, 1)
                sp.dma_start(pin[:], pb[bass.ds(b, 1)].rearrange("b p c d -> (b p) c d"))\
                    .then_inc(pin_in.sem, 16)
                quarter(1, wo, 4, 1)
                sp.dma_start(fg[:], final_g.partition_broadcast(P)).then_inc(fg_in.sem, 16)
                for k in range(2, 4):
                    quarter(k, wo, 4, 1)
                quarter(0, wu, U_UP0, 0)
                for k in range(3):
                    quarter(k, wg, U_GATE, 0)
                next_x = xb[bass.ds((b + 1) & (NB - 1), 1)]
                chunks(xin, next_x, x_in, (0, 1))
                quarter(3, wg, U_GATE, 0)
                chunks(xin, next_x, x_in, (2, 3))
                for k in range(4):
                    quarter(k, wg, U_GATE + 4, 1)
                quarter(0, wu, U_UP1, 1)
            last = Pos("F", NB, 0)
            for k in range(RING):
                sp.wait_ge(unit_done.sem, unit_done.at(last, k, back=RING))
                sp.dma_start(w_raw[k][:].rearrange("p (a b) -> p a b", a=KT), win[:, :, 0:P])\
                    .then_inc(w_loaded[k], 16)

        @block.gpsimd
        def _(pool):
            pool.memset(par_rows[1][:], 0.0).then_inc(consts, 1)
            pool.memset(ident[:], 0.0).then_inc(consts, 1)
            pool.memset(cap[:], 0.0).then_inc(consts, 1)
            pool.memset(state[:], 0.0).then_inc(consts, 1)
            pool.memset(conv_halo[:], 0.0).then_inc(consts, 1)
            pool.memset(pool_halo[:], 0.0).then_inc(consts, 1)
            pool.iota(pos16[:], [[1, 16]], base=1, channel_multiplier=0,
                      allow_small_or_imprecise_dtypes=True).then_inc(consts, 1)
            pool.wait_ge(consts, 3)
            pool.affine_select(out=ident[:], in_=ident[:], compare_op=ALU.not_equal, fill=1.0,
                               base=0, pattern=[[-1, P]], channel_multiplier=1).then_inc(consts, 1)
            pool.affine_select(out=cap[:], in_=cap[:], compare_op=ALU.is_ge, fill=-1e30,
                               base=0, pattern=[[1, P]], channel_multiplier=-1).then_inc(consts, 1)

            def lo_part(s, count):
                pool.wait_ge(w_hi_done, count)
                pool.tensor_tensor(w_lo[s][:], w_raw[s][:], w_hi[s][:].bitcast(F32), ALU.subtract)\
                    .then_inc(w_ready.sem, 1)

            for k in range(RING):
                lo_part(k, k + 1)
            def turn(count):
                for k in range(2 * RING):
                    lo_part(k % RING, count + (RING + k + 1))

            per = 2 * RING
            with pool.Fori(0, NB) as b:
                with pool.Fori(0, 2) as r:
                    turn(b * BLOCK_UNITS + r * per)
                pos = Pos("F", b, 0)
                pool.wait_ge(out_full.sem, out_full.start_of(pos, "F"))
                on_its_own(pool)
                pool.memset(a_acc[:], 0.0).then_inc(acc_zero.sem, 1)
                with pool.Fori(2, BLOCK_UNITS // per) as r:
                    turn(b * BLOCK_UNITS + r * per)

        @block.scalar
        def _(act):
            def split_ahead(pos, k):
                s = slot(pos, k + 2)
                act.wait_ge(w_loaded[s], loaded_at(pos, k + 2))
                act.wait_ge(unit_done.sem, unit_done.at(pos, k + 2, back=RING))
                act.activation(w_hi[s][:], w_raw[s][:], ACT.Copy).then_inc(w_hi_done, 1)

            for s in (squares, y_squares, xt_full, bt_full):
                act.sem_inc(s.sem, 1)
            act.sem_inc(out_done.sem, 16)

            def sums_of_squares(pos, k0, src, sums, ready):
                for c in range(NC):
                    act.wait_ge(*ready(c))
                    act.wait_ge(squares.sem, squares.at(pos, k0 + c, back=1))
                    act.activation(junk[:, 0:src[c].shape[-1]], src[c], ACT.Square,
                                   accum_out=sums[:, c:c + 1]).then_inc(squares.sem, 1)

            def halves(h):
                return [x2[:, c, 512 * h:512 * h + 512] for c in range(NC)]

            def load_root_table(pos):
                act.activation(junk_root[:], ident[:, 0:8], ACT.Sqrt).then_inc(root_table.sem, 1)
                act.wait_ge(root_table.sem, root_table.at(pos, 0))

            def norm_x(pos, k0):
                sums_of_squares(pos, k0, [xin[:, c] for c in range(NC)], ssx,
                                lambda c: (x_in[c].sem, x_in[c].at(pos, 0)))
                act.wait_ge(meansq_x.sem, meansq_x.at(pos, 0))
                act.activation(rrx[:], ssx[:], ACT.Sqrt).then_inc(root_x.sem, 1)

            def x_his(pos):
                for k in range(KT):
                    act.wait_ge(x_psum.sem, x_psum.at(pos, k))
                    act.activation(h_hi[:, k], bank[X_BANK[k]][:], ACT.Copy, scale=ng[:, k:k + 1])\
                        .then_inc(x_hi.sem, 1)

            def group(pos, g):
                prev = pos.phase == "G"

                def load_rows(c):
                    src = acs_dram[bass.ds(pos.b, 1), bass.ds(g * HG, HG), c * P:(c + 1) * P]
                    act.dma_start(m[c][:, 0:HG * P].rearrange("p (h l) -> p h l", h=HG),
                                  src.rearrange("b h t -> (b h) t").partition_broadcast(P))\
                        .then_inc(rows_in[c].sem, 16)

                def silu(t):
                    dst, tap, _ = conv_tile(g, t)
                    act.wait_ge(conv_done.sem, conv_done.at(pos, t))
                    act.activation(dst, dst, ACT.Silu, bias=tap[TAPS]).then_inc(silu_done.sem, 1)

                def chunk_in(c):
                    act.wait_ge(y_gated.sem, y_gated.at(pos, c, back=2))
                    act.wait_ge(xt_psum.sem, xt_psum.at(pos, c))
                    act.activation(xt[c % 2][:], bank[6][:], ACT.Copy).then_inc(xt_full.sem, 1)
                    act.wait_ge(bcb_psum.sem, bcb_psum.at(pos, c))
                    act.activation(bt[c % 2][:], bank[7][:, 0:P], ACT.Copy).then_inc(bt_full.sem, 1)
                    act.activation(cbs[c % 2][:], bank[7][:, P:2 * P], ACT.Copy).then_inc(bt_full.sem, 1)

                def decays(c):
                    act.wait_ge(seg_full.sem, seg_full.at(pos, c))
                    act.activation(m[c][:], m[c][:], ACT.Exp).then_inc(decay.sem, 1)

                def square(c):
                    act.wait_ge(y_gated.sem, y_gated.at(pos, c))
                    act.wait_ge(y_squares.sem, y_squares.at(pos, c, back=1))
                    act.activation(junk_y[:], zs[:, c], ACT.Square, accum_out=ssy[:, c:c + 1])\
                        .then_inc(y_squares.sem, 1)

                for t in range(6):
                    if t and prev:
                        split_ahead(pos, t)
                    act.wait_ge(conv_done.sem, conv_done.at(pos, t, back=2))
                    act.wait_ge(unit_done.sem, unit_done.at(pos, t))
                    dst, tap, halo = conv_tile(g, t)
                    buf = cbuf[t % 2]
                    act.activation(buf[:, TAPS - 1:], bank[projection_bank(pos, t)][:], ACT.Copy)
                    act.activation(buf[:, 0:TAPS - 1], halo, ACT.Copy).then_inc(cbuf_full.sem, 1)
                    act.wait_ge(cbuf_full.sem, cbuf_full.at(pos, t))
                    act.activation(dst, buf[:, 0:T], ACT.Copy, scale=tap[0]).then_inc(first_tap.sem, 1)
                    if not prev:
                        for k in ((1,), (2,), (3,), (4, 5), (), (6,))[t]:
                            split_ahead(pos, k)
                    if t == 2 and not prev:
                        act.wait_ge(dt_abs.sem, dt_abs.at(pos, 0))
                        act.activation(dtw[1][:], dtw[1][:], ACT.Exp).then_inc(dt_exp.sem, 1)
                    if t == 5 and not prev:
                        act.wait_ge(dt_full.sem, dt_full.at(pos, 0))
                        on_its_own(act)
                        act.dma_start(acs_dram[bass.ds(b, 1)].rearrange("b h t -> (b h) t"), dtw[6][:])\
                            .then_inc(acs_out.sem, 16)
                        split_ahead(pos, F_Z + 1)
                        act.wait_ge(acs_out.sem, acs_out.at(pos, 0))
                        on_its_own(act)
                        for c in range(NC):
                            load_rows(c)
                    if t == 2 and prev:
                        act.wait_ge(y_gated.sem, y_gated.at(pos, 0, back=1))
                        on_its_own(act)
                        for c in range(NC):
                            load_rows(c)
                    if t:
                        silu(t - 1)
                    if t == 3 and prev:
                        ya_his(pos, g - 1)
                if prev:
                    split_ahead(pos, 6)
                silu(5)

                def silu_zp(j):
                    k = (U_ZP if prev else F_ZP) + j
                    act.wait_ge(unit_done.sem, unit_done.at(pos, k))
                    act.activation(one(zps, g * PT + j), bank[j][:], ACT.Silu).then_inc(zp_full.sem, 1)

                def silu_z():
                    act.wait_ge(unit_done.sem, unit_done.at(pos, (U_Z if prev else F_Z) + 3))
                    for c in range(NC):
                        act.activation(zs[:, c], bank[2 + c][:], ACT.Silu).then_inc(z_silu.sem, 1)

                def mixing_weights():
                    act.wait_ge(mix_in.sem, mix_in.at(pos, 0))
                    act.activation(mx_hi[:], mx_raw[:], ACT.Copy).then_inc(mx_hi_done.sem, 1)

                def u_out(j):
                    act.wait_ge(unit_done.sem, unit_done.at(pos, (U_U if prev else F_U) + j))
                    act.activation(ubuf[j][:, 16:], bank[j][:], ACT.Copy).then_inc(u_full.sem, 1)

                def pooled_hi(j):
                    act.wait_ge(pf_full.sem, pf_full.at(pos, j))
                    act.activation((pl_hi if prev else plf_hi)[:, j], pf[:], ACT.Copy)\
                        .then_inc(pl_hi_done.sem, 1)

                def pooling_his():
                    for j in range(PT):
                        act.wait_ge(yb_val.sem, yb_val.at(pos, j))
                        on_its_own(act)
                        act.activation(one(yb_hi, g * PT + j), pf[:], ACT.Copy).then_inc(yb_hi_done.sem, 1)

                def root_y():
                    act.wait_ge(y_meansq.sem, y_meansq.at(pos, 0))
                    act.activation(rry[:], ssy[:], ACT.Sqrt).then_inc(y_root.sem, 1)

                if prev:
                    for j in range(PT):
                        if j:
                            split_ahead(pos, U_ZP + j)
                        silu_zp(j)
                    mixing_weights()
                    split_ahead(pos, U_U)
                    u_out(0)
                    decays(0)
                    decays(1)
                    split_ahead(pos, U_U + 1)
                    pooled_hi(0)
                    u_out(1)
                    chunk_in(0)
                    split_ahead(pos, U_Z)
                    pooled_hi(1)
                    split_ahead(pos, U_Z + 1)
                    chunk_in(1)
                    split_ahead(pos, U_Z + 2)
                    decays(2)
                    decays(3)
                    pooling_his()
                    split_ahead(pos, U_Z + 3)
                    silu_z()
                    split_ahead(pos, U_A)
                    chunk_in(2)
                    square(0)
                    split_ahead(pos, U_A + 1)
                    chunk_in(3)
                    square(1)
                    split_ahead(pos, U_A + 2)
                    square(2)
                    split_ahead(pos, U_A + 3)
                    split_ahead(pos, U_A + 4)
                    load_root_table(pos)
                    square(3)
                    root_y()
                else:
                    split_ahead(pos, F_Z + 2)
                    chunk_in(0)
                    act.wait_ge(tok_full.sem, tok_full.at(pos, 0))
                    act.activation(exp_acs[:], tok_acs[:], ACT.Exp).then_inc(acs_exp.sem, 1)
                    decays(0)
                    decays(1)
                    split_ahead(pos, F_Z + 3)
                    chunk_in(1)
                    silu_z()
                    mixing_weights()
                    split_ahead(pos, F_U)
                    u_out(0)
                    decays(2)
                    decays(3)
                    split_ahead(pos, F_U + 1)
                    u_out(1)
                    act.wait_ge(out_done.sem, out_done.start_of(pos, "F"))
                    chunk_in(2)
                    square(0)
                    split_ahead(pos, F_ZP)
                    silu_zp(0)
                    chunk_in(3)
                    pooled_hi(0)
                    split_ahead(pos, F_ZP + 1)
                    pooled_hi(1)
                    square(1)
                    silu_zp(1)
                    square(2)
                    split_ahead(pos, F_ZP + 2)
                    load_root_table(pos)
                    square(3)
                    pooling_his()
                    root_y()

            def ya_his(pos, g):
                for k in range(GT):
                    act.wait_ge(yt_psum.sem, yt_psum.at(pos, k))
                    act.activation(ya_hi[:, k], bank[2 + k][:], ACT.Copy, scale=col(gn, g, k))\
                        .then_inc(ya_hi_done.sem, 1)

            before = Pos("PRE", 0, 0)
            act.wait_ge(consts, 9)
            load_root_table(before)
            norm_x(before, 0)
            act.wait_ge(params_in, 16 * N_LOADS)
            act.activation(aneg[:, 1:2], aneg[:, 0:1], ACT.Exp).then_inc(a_exp, 1)
            for k in range(RING):
                act.wait_ge(w_loaded[k], 16)
                act.activation(w_hi[k][:], w_raw[k][:], ACT.Copy).then_inc(w_hi_done, 1)
            act.wait_ge(par_full, 1)
            x_his(before)
            with act.Fori(0, NB) as b:
                pos = Pos("F", b, 0)
                group(pos, 0)
                with act.Fori(0, GROUPS - 1) as i:
                    group(Pos("G", b, i), i + 1)
                pos = Pos("W", b, 0)

                def gate(pos, k, dst, src):
                    act.wait_ge(unit_done.sem, unit_done.at(pos, k))
                    act.activation(dst[:], bank[src][:], ACT.Sigmoid).then_inc(gates.sem, 1)

                def merged_hi(pos, s, j):
                    act.wait_ge(m_val.sem, m_val.at(pos, s))
                    act.activation(one(m_hi, j), sga[s][:], ACT.Copy).then_inc(m_hi_done.sem, 1)

                gate(pos, W_GA, sga[0], GA_BANK[0])
                split_ahead(pos, 1)
                ya_his(pos, GROUPS - 1)
                gate(pos, W_GB, sgb[0], GB_BANK[0])
                split_ahead(pos, 2)
                for k in range(3, 6):
                    split_ahead(pos, k)
                with act.Fori(0, KT // 2 - 1) as jj:
                    pos = Pos("J", b, jj)
                    for s in range(2):
                        split_ahead(pos, 3 * s)
                        split_ahead(pos, 3 * s + 1)
                        merged_hi(pos, s, jj * 2 + s)
                        act.wait_ge(merged.sem, merged.at(pos, s + 1, back=2))
                        gate(pos, J_GA[s], sga[1 - s], GA_BANK[1 - s])
                        split_ahead(pos, 3 * s + 2)
                        gate(pos, J_GB[s], sgb[1 - s], GB_BANK[1 - s])
                pos = Pos("K", b, 0)
                split_ahead(pos, 0)
                split_ahead(pos, 1)
                merged_hi(pos, 0, KT - 2)
                act.wait_ge(merged.sem, merged.at(pos, 1, back=2))
                gate(pos, J_GA[0], sga[1], GA_BANK[1])
                split_ahead(pos, 2)
                gate(pos, J_GB[0], sgb[1], GB_BANK[1])
                split_ahead(pos, 3)
                merged_hi(pos, 1, KT - 1)
                pos = Pos("O", b, 0)

                def x2_his(which):
                    for k in which:
                        act.wait_ge(t_psum.sem, t_psum.at(pos, x2_order(k)))
                        act.activation(h_hi[:, k], bank[X2_BANK[k]][:], ACT.Copy, scale=pg[:, k:k + 1])\
                            .then_inc(t_hi.sem, 1)

                for k in range(5):
                    split_ahead(pos, k)
                sums_of_squares(pos, 0, halves(0), ss[:, 0], lambda c: (x2_sum.sem, x2_sum.at(pos, c)))
                split_ahead(pos, 5)
                split_ahead(pos, 6)
                x2_his((0, 1))
                for k in range(2):
                    act.wait_ge(t_psum.sem, t_psum.at(pos, 2 + k))
                    act.activation(p_hi[:, k], bank[2 + k][:], ACT.Copy).then_inc(t_hi.sem, 1)
                x2_his((2, 3))
                split_ahead(pos, 7)
                split_ahead(pos, 8)
                act.wait_ge(unit_done.sem, unit_done.at(pos, U_UP0))
                for c in range(2):
                    act.activation(up0[:, c], bank[half_bank(0, c)][:], ACT.Copy).then_inc(up0_full.sem, 1)
                x2_his((4, 5, 6, 7))
                sums_of_squares(pos, NC, halves(1), ss[:, 1],
                                lambda c: (x2_sum.sem, x2_sum.at(pos, NC + c)))
                act.wait_ge(meansq.sem, meansq.at(pos, 0))
                act.activation(rr[:], ms[:], ACT.Sqrt).then_inc(root.sem, 1)
                split_ahead(pos, 9)
                split_ahead(pos, 10)
                split_ahead(pos, 11)
                norm_x(pos, 2 * NC)
                split_ahead(pos, 12)
                act.wait_ge(rms_x2.sem, rms_x2.at(pos, 0))
                for h in range(2):
                    act.wait_ge(unit_done.sem, unit_done.at(pos, U_GATE + 4 * h + 3))
                    for c in range(NC):
                        if h:
                            act.wait_ge(x3_sum.sem, x3_sum.at(pos, c))
                        act.activation(sg[:, c], bank[half_bank(h, c)][:], ACT.Sigmoid,
                                       scale=rq[:, c:c + 1]).then_inc(ple_gate.sem, 1)
                    if h == 0:
                        split_ahead(pos, 13)
                        sums_of_squares(pos, 3 * NC, halves(0), ss[:, 0],
                                        lambda c: (x3_sum.sem, x3_sum.at(pos, c)))
                        for k in range(14, 17):
                            split_ahead(pos, k)
                split_ahead(pos, 17)
                x_his(pos)
                split_ahead(pos, 18)
                load_root_table(pos)
                sums_of_squares(pos, 4 * NC, halves(1), ss[:, 1],
                                lambda c: (x3_sum.sem, x3_sum.at(pos, NC + c)))
                act.wait_ge(meansq.sem, meansq.at(pos, 1))
                act.activation(rr[:], ms[:], ACT.Sqrt).then_inc(root.sem, 1)
                for c in range(NC):
                    act.wait_ge(out_full.sem, out_full.at(pos, c))
                    on_its_own(act)
                    act.dma_start(ob[bass.ds(b, 1), c].rearrange("b p d -> (b p) d"), y_out[:, c])\
                        .then_inc(out_done.sem, 16)
            act.wait_ge(out_done.sem, 16 * (NB * NC + 1))
            act.wait_ge(acs_out.sem, 16 * NB)

        @block.vector
        def _(dve):
            n_link = {"k": 0, "setup": 0}

            def link(pos, ins):
                if pos.phase == "PRE":
                    n_link["setup"] += 1
                    ins.then_inc(setup_link, 1)
                    dve.wait_ge(setup_link, n_link["setup"])
                else:
                    ins.then_inc(link_s.sem, 1)
                    dve.wait_ge(link_s.sem, link_s.at(pos, n_link["k"]))
                    n_link["k"] += 1

            def links_done(phase):
                assert n_link["k"] == link_s.n[phase], (phase, n_link["k"])
                n_link["k"] = 0

            for s in (conv_done, y_gated, acc_added, merged):
                dve.sem_inc(s.sem, 2)
            dve.sem_inc(state_new.sem, 1)
            dve.sem_inc(out_full.sem, 1)

            def mean_square(pos, sums, mean, count, width, halves=False):
                dve.wait_ge(squares.sem, count)
                if halves:
                    link(pos, dve.tensor_tensor(ms[:], ss[:, 0], ss[:, 1], ALU.add))
                dve.tensor_scalar(sums[:], sums[:], 1.0 / width, EPS, ALU.mult, ALU.add)\
                    .then_inc(mean.sem, 1)

            def norm_x(pos, sqk):
                for c in range(NC):
                    dve.wait_ge(x_in[c].sem, x_in[c].at(pos, 0))
                mean_square(pos, ssx, meansq_x, squares.at(pos, sqk), DM)
                dve.wait_ge(root_x.sem, root_x.at(pos, 0))
                link(pos, dve.reciprocal(rqx[:], rrx[:]))
                for c in range(NC):
                    dve.tensor_scalar(xs[:, c], xin[:, c], rqx[:, c:c + 1], None, ALU.mult)\
                        .then_inc(xs_full.sem, 1)

            def x_los(pos):
                for k in range(KT):
                    dve.wait_ge(x_hi.sem, x_hi.at(pos, k))
                    dve.scalar_tensor_tensor(h_lo[:, k], bank[X_BANK[k]][:], ng[:, k:k + 1],
                                             h_hi[:, k].bitcast(F32), ALU.mult, ALU.subtract)\
                        .then_inc(x_lo.sem, 1)

            before = Pos("PRE", 0, 0)
            norm_x(before, NC - 1)
            dve.wait_ge(params_in, 16 * N_LOADS)
            dve.wait_ge(consts, 9)
            dve.wait_ge(a_exp, 1)
            dve.wait_ge(par_psum, 1)
            dve.tensor_copy(par[:], bank[0][:, 0:2 * P]).then_inc(par_full, 1)
            dve.wait_ge(par_full, 1)
            link(before, dve.tensor_copy(wdt_raw[:, KT * HEADS:NDT], wdt_raw[:, 0:NDT - KT * HEADS]))
            link(before, dve.tensor_copy(wdt_hi[:], wdt_raw[:]))
            dve.tensor_tensor(wdt_lo[:], wdt_raw[:], wdt_hi[:].bitcast(F32), ALU.subtract)\
                .then_inc(setup_done, 1)
            dve.wait_ge(setup_done, 1)
            x_los(before)
            for g in range(GROUPS):
                dve.memset(invw[:, g:g + 1], 1.0 / 2 ** (g + 1))
                last = dve.tensor_scalar(inv16[:, g], pos16[:], float(2 ** (g + 1)), None, ALU.min)
            link(before, last)
            link(before, dve.reciprocal(inv16[:].rearrange("p g n -> p (g n)"),
                                        inv16[:].rearrange("p g n -> p (g n)")))
            link(before, dve.tensor_scalar(aneg[:, 1:2], aneg[:, 1:2], -1.0, None, ALU.mult))

            v, e, r_, s_, s2, q_, acs = (t[:] for t in dtw)

            def dt_start(pos):
                dve.wait_ge(dt_psum.sem, dt_psum.start_of(pos, "F"))
                link(pos, dve.tensor_scalar(v, bank[DT_BANK][0:HEADS, :], dtb[:, 0:1], None, ALU.add))
                dve.scalar_tensor_tensor(e, v, -1.0, v, ALU.mult, ALU.min).then_inc(dt_abs.sem, 1)

            def dt_series(pos):
                dve.wait_ge(dt_exp.sem, dt_exp.at(pos, 0))
                link(pos, dve.tensor_scalar(r_, e, 2.0, None, ALU.add))
                link(pos, dve.reciprocal(r_, r_))
                link(pos, dve.tensor_tensor(s_, e, r_, ALU.mult))
                link(pos, dve.tensor_tensor(s2, s_, s_, ALU.mult))
                link(pos, dve.tensor_scalar(q_, s2, ATANH[-1], None, ALU.mult))
                for coef in reversed(ATANH[3:-1]):
                    link(pos, dve.scalar_tensor_tensor(q_, q_, coef, s2, ALU.add, ALU.mult))

            def dt_end(pos):
                for coef in reversed(ATANH[:3]):
                    link(pos, dve.scalar_tensor_tensor(q_, q_, coef, s2, ALU.add, ALU.mult))
                link(pos, dve.scalar_tensor_tensor(q_, q_, 1.0, s_, ALU.add, ALU.mult))
                link(pos, dve.tensor_scalar(v, v, 0.0, None, ALU.max))
                link(pos, dve.scalar_tensor_tensor(v, q_, 2.0, v, ALU.mult, ALU.add))
                link(pos, dve.tensor_scalar(r_, v, aneg[:, 1:2], None, ALU.mult))
                link(pos, dve.memset(e, 0.0))
                for c in range(NC):
                    part = slice(c * P, (c + 1) * P)
                    scan = dve.tensor_tensor_scan(acs[:, part], r_[:, part], e[:, part], 0.0,
                                                  ALU.add, ALU.add)
                scan.then_inc(dt_full.sem, 1)

            def norm_y(pos):
                dve.wait_ge(y_root.sem, y_root.at(pos, 0, back=1))
                link(pos, dve.reciprocal(rqy[:], rry[:]))
                for c in range(NC):
                    dve.tensor_scalar(zs[:, c], zs[:, c], rqy[:, c:c + 1], None, ALU.mult)\
                        .then_inc(y_normed.sem, 1)

            def ya_los(pos, g):
                for k in range(GT):
                    dve.wait_ge(ya_hi_done.sem, ya_hi_done.at(pos, k))
                    dve.scalar_tensor_tensor(ya_lo[:, k], bank[2 + k][:], col(gn, g, k),
                                             ya_hi[:, k].bitcast(F32), ALU.mult, ALU.subtract)\
                        .then_inc(ya_full.sem, 1)

            def add_branch_a(pos, first, q):
                dve.wait_ge(unit_done.sem, unit_done.at(pos, first + q))
                for j in (2 * q, 2 * q + 1):
                    dve.tensor_tensor(a_acc[:, j], a_acc[:, j], bank[acc_bank(j)][:], ALU.add)\
                        .then_inc(acc_added.sem, 1)

            def group(pos, g):
                prev = pos.phase == "G"

                def conv(t):
                    buf = cbuf[t % 2]
                    dst, tap, halo = conv_tile(g, t)
                    dve.wait_ge(first_tap.sem, first_tap.at(pos, t))
                    for j in range(1, TAPS - 1):
                        link(pos, dve.scalar_tensor_tensor(dst, buf[:, j:j + T], tap[j], dst,
                                                           ALU.mult, ALU.add))
                    dve.scalar_tensor_tensor(dst, buf[:, TAPS - 1:TAPS - 1 + T], tap[TAPS - 1],
                                             dst, ALU.mult, ALU.add)
                    dve.tensor_copy(halo, buf[:, T:T + TAPS - 1]).then_inc(conv_done.sem, 1)

                def views(c):
                    mat = m[c]
                    return (mat[:, 0:MX].rearrange("p (h l) -> p h l", h=HG), mat[:, MX:MX + HG],
                            mat[:, MX + HG:MX + 2 * HG])

                def segments(c):
                    seg, to_end, chunk_decay = views(c)
                    acs_s = tok_acs[:, c, bass.ds(g * HG, HG)]
                    dve.wait_ge(rows_in[c].sem, rows_in[c].at(pos, 0))
                    dve.tensor_tensor(to_end, seg[:, :, P - 1], acs_s, ALU.subtract)
                    link(pos, dve.tensor_copy(chunk_decay, seg[:, :, P - 1]))
                    for h in range(HG):
                        last = dve.scalar_tensor_tensor(seg[:, h], seg[:, h], acs_s[:, h:h + 1], cap[:],
                                                        ALU.subtract, ALU.min)
                    last.then_inc(seg_full.sem, 1)

                def inputs(c):
                    seg, to_end, _ = views(c)
                    x_, xd, xe = xt[c % 2], xdt[c % 2], xdd[c % 2]
                    dt_s = tok_dt[:, c, bass.ds(g * HG, HG)]
                    dve.wait_ge(xt_full.sem, xt_full.at(pos, c))
                    link(pos, dve.tensor_tensor(heads(xd[:]), heads(x_[:]), per_head(dt_s, HD), ALU.mult))
                    link(pos, dve.tensor_tensor(heads(x_[:]), heads(x_[:]),
                                                per_head(dskip[:, bass.ds(g * HG, HG)], HD), ALU.mult))
                    dve.wait_ge(decay.sem, decay.at(pos, c))
                    dve.tensor_tensor(heads(xe[:]), heads(xd[:]), per_head(to_end, HD), ALU.mult)\
                        .then_inc(xdt_full.sem, 1)
                    dve.wait_ge(bt_full.sem, bt_full.at(pos, 2 * c + 1))
                    dve.tensor_tensor(seg, seg, cbs[c % 2][:].unsqueeze(1).to_broadcast([P, HG, P]),
                                      ALU.mult).then_inc(m_full.sem, 1)

                def outputs(c):
                    _, _, chunk_decay = views(c)
                    x_, y = xt[c % 2], xdt[c % 2]
                    ea = exp_acs[:, c, bass.ds(g * HG, HG)]
                    st = one(state, g)
                    dve.wait_ge(ssd_psum.sem, ssd_psum.at(pos, 3 * c + 1))
                    link(pos, dve.tensor_tensor(heads(st), heads(st), per_head(chunk_decay, HD), ALU.mult))
                    dve.tensor_tensor(st, st, bank[4][:], ALU.add).then_inc(state_new.sem, 1)
                    dve.wait_ge(ssd_psum.sem, ssd_psum.at(pos, 3 * c + 2))
                    link(pos, dve.tensor_tensor(heads(y[:]), heads(bank[3][:]), per_head(ea, HD), ALU.mult))
                    dve.tensor_tensor(y[:], y[:], bank[2][:], ALU.add).then_inc(y_read.sem, 1)
                    dve.wait_ge(y_read.sem, y_read.at(pos, c))
                    link(pos, dve.tensor_tensor(y[:], y[:], x_[:], ALU.add))
                    dve.tensor_tensor(zs[:, c], y[:], zs[:, c], ALU.mult).then_inc(y_gated.sem, 1)
                    dve.wait_ge(y_gated.sem, y_gated.at(pos, c))

                def pool_tile(j):
                    halo = pool_halo[:, bass.ds(g, 1), j, :].rearrange("p a n -> p (a n)")
                    inv, u = one(inv16, g), ubuf[j]
                    dve.wait_ge(u_full.sem, u_full.at(pos, j))
                    link(pos, dve.tensor_copy(u[:, 0:16], halo))
                    link(pos, dve.tensor_tensor_scan(cs[:], u[:], u[:], 0.0, ALU.add, ALU.bypass))
                    on_its_own(dve)
                    if j:
                        dve.wait_ge(pooled.sem, pooled.at(pos, j - 1))
                        on_its_own(dve)
                    lag = cs[:, bass.ds(16 - (2 << g), T)]
                    link(pos, dve.tensor_tensor(pf[:], cs[:, 16:16 + T], lag, ALU.subtract))
                    dve.scalar_tensor_tensor(pf[:, 16:T], pf[:, 16:T], invw[:, bass.ds(g, 1)],
                                             u[:, 32:T + 16], ALU.mult, ALU.subtract)
                    dve.tensor_copy(halo, u[:, T:T + 16])
                    link(pos, dve.tensor_tensor(pf[:, 0:16], pf[:, 0:16], inv, ALU.mult))
                    dve.tensor_tensor(pf[:, 0:16], pf[:, 0:16], u[:, 16:32], ALU.subtract)\
                        .then_inc(pf_full.sem, 1)
                    dve.wait_ge(pl_hi_done.sem, pl_hi_done.at(pos, j))
                    hi, lo = (pl_hi, pl_lo) if prev else (plf_hi, plf_lo)
                    dve.tensor_tensor(lo[:, j], pf[:], hi[:, j].bitcast(F32), ALU.subtract)\
                        .then_inc(pooled.sem, 1)

                conv(0)
                if prev:
                    norm_y(pos)
                else:
                    dt_start(pos)
                conv(1)
                if not prev:
                    dt_series(pos)
                conv(2)
                conv(3)
                if prev:
                    ya_los(pos, g - 1)
                else:
                    dt_end(pos)
                conv(4)
                conv(5)
                if not prev:
                    dve.wait_ge(tok_psum.sem, tok_psum.at(pos, 0))
                    dve.tensor_copy(tok_dt[:].rearrange("p c h -> p (c h)"), bank[TOK_BANK][:, 0:NC * HEADS])
                    dve.tensor_copy(tok_acs[:].rearrange("p c h -> p (c h)"),
                                    bank[TOK_BANK][:, NC * HEADS:2 * NC * HEADS]).then_inc(tok_full.sem, 1)
                    dve.wait_ge(tok_full.sem, tok_full.at(pos, 0))

                def mixing_weights():
                    dve.wait_ge(mx_hi_done.sem, mx_hi_done.at(pos, 0))
                    dve.tensor_tensor(mx_lo[:], mx_raw[:], mx_hi[:].bitcast(F32), ALU.subtract)\
                        .then_inc(mx_full.sem, 1)

                def pooling_branch():
                    for j in range(PT):
                        dve.wait_ge(mix_psum.sem, mix_psum.at(pos, j))
                        if j:
                            dve.wait_ge(yb_full.sem, yb_full.at(pos, j - 1))
                        src = bank[j if prev else F_MIX_BANK[j]]
                        dve.tensor_scalar(pf[:], src[:], col(mixb, g, j), col(pscale, g, j),
                                          ALU.add, ALU.mult).then_inc(mix_read.sem, 1)
                        dve.wait_ge(mix_read.sem, mix_read.at(pos, j))
                        dve.wait_ge(zp_full.sem, zp_full.at(pos, j))
                        dve.tensor_tensor(pf[:], pf[:], one(zps, g * PT + j), ALU.mult)\
                            .then_inc(yb_val.sem, 1)
                        dve.wait_ge(yb_hi_done.sem, yb_hi_done.at(pos, j))
                        dve.tensor_tensor(one(yb_lo, g * PT + j), pf[:],
                                          one(yb_hi, g * PT + j).bitcast(F32), ALU.subtract)\
                            .then_inc(yb_full.sem, 1)

                def ready_for_outputs():
                    dve.wait_ge(acs_exp.sem, acs_exp.start_of(pos, "G"))
                    dve.wait_ge(z_silu.sem, z_silu.at(pos, NC - 1))

                if prev:
                    segments(0)
                    segments(1)
                    pool_tile(0)
                    mixing_weights()
                    pool_tile(1)
                    inputs(0)
                    segments(2)
                    segments(3)
                    inputs(1)
                    pooling_branch()
                    dve.wait_ge(acc_zero.sem, acc_zero.start_of(pos, "G"))
                    add_branch_a(pos, U_A, 0)
                    ready_for_outputs()
                    outputs(0)
                    inputs(2)
                    add_branch_a(pos, U_A, 1)
                    outputs(1)
                    inputs(3)
                    add_branch_a(pos, U_A, 2)
                    outputs(2)
                    add_branch_a(pos, U_A, 3)
                    outputs(3)
                else:
                    segments(0)
                    segments(1)
                    inputs(0)
                    segments(2)
                    segments(3)
                    inputs(1)
                    ready_for_outputs()
                    outputs(0)
                    inputs(2)
                    outputs(1)
                    pool_tile(0)
                    mixing_weights()
                    pool_tile(1)
                    inputs(3)
                    outputs(2)
                    outputs(3)
                    pooling_branch()
                dve.wait_ge(y_squares.sem, y_squares.at(pos, NC - 1))
                dve.tensor_scalar(ssy[:], ssy[:], 1.0 / GC, EPS, ALU.mult, ALU.add).then_inc(y_meansq.sem, 1)
                dve.wait_ge(y_meansq.sem, y_meansq.at(pos, 0))
                links_done(pos.phase)

            with dve.Fori(0, NB) as b:
                group(Pos("F", b, 0), 0)
                on_its_own(dve)
                with dve.Fori(0, GROUPS - 1) as i:
                    group(Pos("G", b, i), i + 1)
                pos = Pos("W", b, 0)
                norm_y(pos)
                ya_los(pos, GROUPS - 1)
                for q in range(4):
                    add_branch_a(pos, W_A, q)
                dve.wait_ge(acc_added.sem, acc_added.at(pos, KT - 1))
                on_its_own(dve)
                links_done("W")
                def merge(pos, s, j):
                    dve.wait_ge(gates.sem, gates.at(pos, 2 * s + 1, back=2))
                    link(pos, dve.tensor_tensor(sga[s][:], sga[s][:], one(a_acc, j), ALU.mult))
                    dve.wait_ge(unit_done.sem, unit_done.at(pos, J_WB[s]))
                    link(pos, dve.tensor_tensor(sgb[s][:], sgb[s][:], bank[WB_BANK[s]][:], ALU.mult))
                    dve.tensor_tensor(sga[s][:], sga[s][:], sgb[s][:], ALU.add).then_inc(m_val.sem, 1)
                    dve.wait_ge(m_hi_done.sem, m_hi_done.at(pos, s))
                    dve.tensor_tensor(one(m_lo, j), sga[s][:], one(m_hi, j).bitcast(F32), ALU.subtract)\
                        .then_inc(merged.sem, 1)

                with dve.Fori(0, KT // 2 - 1) as jj:
                    for s in range(2):
                        merge(Pos("J", b, jj), s, jj * 2 + s)
                    links_done("J")
                for s in range(2):
                    merge(Pos("K", b, 0), s, KT - 2 + s)
                links_done("K")
                pos = Pos("O", b, 0)
                for g in range(GROUPS):
                    ins = dve.memset(inv16[:, g], 1.0 / 2 ** (g + 1))
                link(pos, ins)

                def x2_los(which):
                    for k in which:
                        dve.wait_ge(t_hi.sem, t_hi.at(pos, x2_order(k)))
                        dve.scalar_tensor_tensor(h_lo[:, k], bank[X2_BANK[k]][:], pg[:, k:k + 1],
                                                 h_hi[:, k].bitcast(F32), ALU.mult, ALU.subtract)\
                            .then_inc(t_lo.sem, 1)

                for h in range(2):
                    dve.wait_ge(unit_done.sem, unit_done.at(pos, 4 * h + 3))
                    for c in range(NC):
                        part = x2[:, c, 512 * h:512 * h + 512]
                        dve.wait_ge(x2_in[c].sem, x2_in[c].at(pos, 0))
                        dve.tensor_tensor(part, part, bank[half_bank(h, c)][:], ALU.add)\
                            .then_inc(x2_sum.sem, 1)
                    if h == 0:
                        x2_los((0, 1))
                        for k in range(2):
                            dve.wait_ge(t_hi.sem, t_hi.at(pos, 2 + k))
                            dve.tensor_tensor(p_lo[:, k], bank[2 + k][:], p_hi[:, k].bitcast(F32),
                                              ALU.subtract).then_inc(t_lo.sem, 1)
                        x2_los((2, 3))
                dve.wait_ge(unit_done.sem, unit_done.at(pos, U_UP0))
                for c in range(2, NC):
                    dve.tensor_copy(up0[:, c], bank[half_bank(0, c)][:]).then_inc(up0_full_v.sem, 1)
                x2_los((4, 5, 6, 7))
                mean_square(pos, ms, meansq, squares.at(pos, 2 * NC - 1), DM, halves=True)
                dve.wait_ge(root.sem, root.at(pos, 0))
                dve.reciprocal(rq[:], rr[:]).then_inc(rms_x2.sem, 1)
                norm_x(pos, 3 * NC - 1)
                for c in range(NC):
                    part = x2[:, c, 0:512]
                    dve.wait_ge(ple_gate.sem, ple_gate.at(pos, c))
                    dve.tensor_tensor(sg[:, c], sg[:, c], up0[:, c], ALU.mult).then_inc(up_gated.sem, 1)
                    dve.wait_ge(up_gated.sem, up_gated.at(pos, c))
                    dve.tensor_tensor(part, part, sg[:, c], ALU.add).then_inc(x3_sum.sem, 1)
                dve.wait_ge(unit_done.sem, unit_done.at(pos, U_UP1))
                for c in range(NC):
                    dve.wait_ge(ple_gate.sem, ple_gate.at(pos, NC + c))
                    dve.tensor_tensor(sg[:, c], sg[:, c], bank[half_bank(0, c)][:], ALU.mult)\
                        .then_inc(up_gated.sem, 1)
                x_los(pos)
                dve.wait_ge(up_gated.sem, up_gated.at(pos, 2 * NC - 1))
                for c in range(NC):
                    part = x2[:, c, 512:1024]
                    dve.tensor_tensor(part, part, sg[:, c], ALU.add).then_inc(x3_sum.sem, 1)
                mean_square(pos, ms, meansq, squares.at(pos, 5 * NC - 1), DM, halves=True)
                dve.wait_ge(root.sem, root.at(pos, 1))
                link(pos, dve.reciprocal(rq[:], rr[:]))
                dve.wait_ge(fg_in.sem, fg_in.at(pos, 0))
                for c in range(NC):
                    dve.scalar_tensor_tensor(y_out[:, c], x2[:, c], rq[:, c:c + 1], fg[:], ALU.mult, ALU.mult)\
                        .then_inc(out_full.sem, 1)
                links_done("O")

        @block.tensor
        def _(pe):
            def three(out_, lhs, rhs, start, stop):
                (lh, ll), (rh, rl) = lhs, rhs
                pe.matmul(out_, lh, rh, start=start, stop=False)
                pe.matmul(out_, lh, rl, start=False, stop=False)
                return pe.matmul(out_, ll, rh, start=False, stop=stop)

            def unit(pos, k, parts):
                pe.wait_ge(w_ready.sem, w_ready.at(pos, k))
                s = slot(pos, k)
                return [w[s][:].rearrange("p (a b) -> p a b", a=parts) for w in (w_hi, w_lo)]

            def stationary_unit(pos, k, dst, moving):
                hi, lo = unit(pos, k, KT)
                for i in range(KT):
                    last = three(dst, (hi[:, i], lo[:, i]), (moving[0][:, i], moving[1][:, i]),
                                 i == 0, i == KT - 1)
                last.then_inc(unit_done.sem, 1)

            def moving_unit(pos, k, dsts, still, k0, ktiles, ready=None):
                hi, lo = unit(pos, k, 2)
                for i in range(2):
                    kt = k0 + i
                    if ready:
                        ready(kt)
                    for c in range(NC):
                        part = slice(c * P, (c + 1) * P)
                        last = three(dsts[c][:], (still[0][:, kt, part], still[1][:, kt, part]),
                                     (hi[:, i], lo[:, i]), kt == 0, kt == ktiles - 1)
                last.then_inc(unit_done.sem, 1)

            def transposes(dst, src, first):
                for c in range(NC):
                    last = pe.transpose(dst[:, c * P:(c + 1) * P], src[:, c, first:first + P], ident[:])
                return last

            H = (h_hi, h_lo)

            def next_x(pos):
                pe.wait_ge(xs_full.sem, xs_full.at(pos, NC - 1))
                for k in range(KT):
                    if pos.phase == "O":
                        if X_BANK[k] >= 4:
                            pe.wait_ge(ple_gate.sem, ple_gate.at(pos, X_BANK[k]))
                        else:
                            pe.wait_ge(up_gated.sem, up_gated.at(pos, NC + X_BANK[k]))
                    elif k == 4:
                        pe.wait_ge(par_full, 1)
                    transposes(bank[X_BANK[k]], xs, k * P).then_inc(x_psum.sem, 1)
                if pos.phase == "PRE":
                    pe.wait_ge(setup_done, 1)
                for k in range(KT):
                    pe.wait_ge(x_lo.sem, x_lo.at(pos, max(k, X_BANK.index(DT_BANK))))
                    last = three(bank[DT_BANK][:], (wdt_hi[:, k * HEADS:k * HEADS + P],
                                                    wdt_lo[:, k * HEADS:k * HEADS + P]),
                                 (h_hi[:, k], h_lo[:, k]), k == 0, k == KT - 1)
                last.then_inc(dt_psum.sem, 1)

            def y_transposes(pos):
                for c in range(NC):
                    pe.wait_ge(y_normed.sem, y_normed.at(pos, c))
                    for k in range(GT):
                        last = pe.transpose(bank[2 + k][:, c * P:(c + 1) * P],
                                            zs[:, c, k * P:(k + 1) * P], ident[:])
                        if c == NC - 1:
                            last.then_inc(yt_psum.sem, 1)

            def branch_a(pos, first, q, ready=None):
                hi, lo = unit(pos, first + q, GT)
                for s in range(2):
                    j = 2 * q + s
                    if j >= 3:
                        pe.wait_ge(acc_added.sem, acc_added.at(pos, j - 3))
                    cols_ = slice(s * P, (s + 1) * P)
                    for i in range(GT):
                        if ready and s == 0:
                            ready(i)
                        last = three(bank[acc_bank(j)][:], (hi[:, i, cols_], lo[:, i, cols_]),
                                     (ya_hi[:, i], ya_lo[:, i]), i == 0, i == GT - 1)
                last.then_inc(unit_done.sem, 1)

            def group(pos, g):
                prev = pos.phase == "G"
                for t in range(6):
                    turns = 2 if prev else 4
                    if t >= turns:
                        pe.wait_ge(cbuf_full.sem, cbuf_full.at(pos, t - turns))
                    elif prev:
                        pe.wait_ge(zp_full.sem, zp_full.at(pos, t, back=2))
                        pe.wait_ge(acc_added.sem, acc_added.at(pos, t, back=2))
                    stationary_unit(pos, t, bank[projection_bank(pos, t)][:], H)
                    if t == 3 and prev:
                        y_transposes(pos)

                def token_major_dt():
                    pe.wait_ge(dt_full.sem, dt_full.at(pos, 0))
                    on_its_own(pe)
                    for n_, src in enumerate((dtw[0], dtw[6])):
                        for c in range(NC):
                            at = (n_ * NC + c) * HEADS
                            last = pe.transpose(bank[TOK_BANK][:, at:at + HEADS],
                                                src[:, c * P:(c + 1) * P], ident[0:HEADS, 0:HEADS])
                    last.then_inc(tok_psum.sem, 1)

                def chunk_in(c):
                    part = slice(c * P, (c + 1) * P)
                    pe.wait_ge(xt_full.sem, xt_full.at(pos, c, back=1))
                    if c == 0:
                        pe.wait_ge(silu_done.sem, silu_done.at(pos, 5))
                        if prev:
                            pe.wait_ge(mix_read.sem, mix_read.at(pos, 0, back=1))
                    for j in range(GT):
                        last = pe.transpose(bank[6][:, j * P:(j + 1) * P], xc[:, j, part], ident[:])
                    last.then_inc(xt_psum.sem, 1)
                    pe.wait_ge(bt_full.sem, bt_full.at(pos, 2 * c, back=1))
                    if c == 0 and not prev:
                        pe.wait_ge(tok_full.sem, tok_full.at(pos, 0))
                    pe.transpose(bank[7][:, 0:P], bc[0][:, part], ident[:])
                    pe.matmul(bank[7][:, P:2 * P], bc[0][:, part], bc[1][:, part], start=True, stop=True)\
                        .then_inc(bcb_psum.sem, 1)

                def chunk_out(c):
                    part = slice(c * P, (c + 1) * P)
                    if c == 0:
                        pe.wait_ge(z_silu.sem, z_silu.at(pos, NC - 1))
                    pe.wait_ge(xdt_full.sem, xdt_full.at(pos, c))
                    pe.wait_ge(state_new.sem, state_new.at(pos, c, back=1))
                    pe.matmul(bank[4][:], bt[c % 2][:], xdd[c % 2][:], start=True, stop=True)\
                        .then_inc(ssd_psum.sem, 1)
                    if c:
                        pe.wait_ge(y_read.sem, y_read.at(pos, c - 1))
                    pe.matmul(bank[3][:], bc[1][:, part], one(state, g), start=True, stop=True)\
                        .then_inc(ssd_psum.sem, 1)
                    pe.wait_ge(m_full.sem, m_full.at(pos, c))
                    for h in range(HG):
                        cols_ = slice(h * HD, (h + 1) * HD)
                        last = pe.matmul(bank[2][:, cols_], m[c][:, h * P:(h + 1) * P],
                                         xdt[c % 2][:, cols_], start=True, stop=True)
                    last.then_inc(ssd_psum.sem, 1)

                def z_unit(k):
                    moving_unit(pos, (U_Z if prev else F_Z) + k, bank[2:6], H, 2 * k, KT)

                def mix():
                    pe.wait_ge(pooled.sem, pooled.at(pos, PT - 1))
                    pe.wait_ge(mx_full.sem, mx_full.at(pos, 0))
                    rhs = (pl_hi, pl_lo) if prev else (plf_hi, plf_lo)
                    for j in range(PT):
                        if prev:
                            pe.wait_ge(u_full.sem, u_full.at(pos, j))
                            dst = bank[j]
                        else:
                            before = (xt_full, bt_full)[j]
                            pe.wait_ge(before.sem, before.at(pos, (j + 1) * NC - 1))
                            dst = bank[F_MIX_BANK[j]]
                        cols_ = slice(j * P, (j + 1) * P)
                        for i in range(PT):
                            last = three(dst[:], (mx_hi[:, i, cols_], mx_lo[:, i, cols_]),
                                         (rhs[0][:, i], rhs[1][:, i]), i == 0, i == PT - 1)
                        last.then_inc(mix_psum.sem, 1)

                def pair(first, k, before, n):
                    pe.wait_ge(before.sem, before.at(pos, n + k))
                    stationary_unit(pos, first + k, bank[k][:], H)

                if prev:
                    for k in range(PT):
                        pair(U_ZP, k, cbuf_full, 4)
                    for k in range(PT):
                        pair(U_U, k, zp_full, 0)
                    chunk_in(0)
                    pe.wait_ge(ya_full.sem, ya_full.at(pos, GT - 1))
                    z_unit(0)
                    z_unit(1)
                    chunk_in(1)
                    z_unit(2)
                    mix()
                    z_unit(3)
                    pe.wait_ge(mix_read.sem, mix_read.at(pos, PT - 1))
                    for c in range(NC):
                        if c == 1:
                            pe.wait_ge(z_silu.sem, z_silu.at(pos, NC - 1))
                        branch_a(pos, U_A, c)
                        chunk_out(c)
                        if c + 2 < NC:
                            chunk_in(c + 2)
                else:
                    pe.wait_ge(dt_abs.sem, dt_abs.at(pos, 0))
                    pe.wait_ge(cbuf_full.sem, cbuf_full.at(pos, 3))
                    z_unit(0)
                    z_unit(1)
                    z_unit(2)
                    token_major_dt()
                    chunk_in(0)
                    z_unit(3)
                    chunk_in(1)
                    pair(F_U, 0, cbuf_full, 4)
                    chunk_out(0)
                    pair(F_U, 1, cbuf_full, 4)
                    chunk_in(2)
                    chunk_out(1)
                    pair(F_ZP, 0, u_full, 0)
                    chunk_in(3)
                    chunk_out(2)
                    pair(F_ZP, 1, u_full, 0)
                    mix()
                    chunk_out(3)

            pe.sem_inc(unit_done.sem, RING)
            pe.sem_inc(mix_psum.sem, 1)
            pe.wait_ge(consts, 9)
            pe.wait_ge(params_in, 16 * N_LOADS)
            for i, rows in enumerate(par_rows):
                last = pe.transpose(bank[0][:, i * P:(i + 1) * P], rows[:], ident[:])
            last.then_inc(par_psum, 1)
            next_x(Pos("PRE", 0, 0))
            with pe.Fori(0, NB) as b:
                group(Pos("F", b, 0), 0)
                with pe.Fori(0, GROUPS - 1) as i:
                    group(Pos("G", b, i), i + 1)
                pos = Pos("W", b, 0)
                pe.wait_ge(xt_full.sem, xt_full.at(pos, 0, back=1))
                pe.wait_ge(bt_full.sem, bt_full.at(pos, 0, back=1))
                stationary_unit(pos, W_GA, bank[GA_BANK[0]][:], H)
                y_transposes(pos)
                stationary_unit(pos, W_GB, bank[GB_BANK[0]][:], H)
                for q in range(4):
                    branch_a(pos, W_A, q, ready=None if q else
                             lambda i: pe.wait_ge(ya_full.sem, ya_full.at(pos, i)))

                def merge_units(pos, s, with_gates=True):
                    pe.wait_ge(merged.sem, merged.at(pos, s, back=2))
                    stationary_unit(pos, J_WB[s], bank[WB_BANK[s]][:], (yb_hi, yb_lo))
                    if with_gates:
                        pe.wait_ge(merged.sem, merged.at(pos, s + 1, back=2))
                        stationary_unit(pos, J_GA[s], bank[GA_BANK[1 - s]][:], H)
                        stationary_unit(pos, J_GB[s], bank[GB_BANK[1 - s]][:], H)

                pe.wait_ge(acc_added.sem, acc_added.at(pos, 5))
                on_its_own(pe)
                with pe.Fori(0, KT // 2 - 1) as jj:
                    for s in range(2):
                        merge_units(Pos("J", b, jj), s)
                for s in range(2):
                    merge_units(Pos("K", b, 0), s, with_gates=s == 0)
                pos = Pos("O", b, 0)

                def half(h):
                    return [bank[half_bank(h, c)] for c in range(NC)]

                def x2_transposes(which):
                    for k in which:
                        transposes(bank[X2_BANK[k]], x2, k * P).then_inc(t_psum.sem, 1)

                pe.wait_ge(merged.sem, merged.start_of(pos, "O") - 1)
                pe.wait_ge(gates.sem, gates.start_of(pos, "O"))
                pe.wait_ge(acc_added.sem, acc_added.start_of(pos, "O"))
                for k in range(8):
                    if k == 3:
                        pe.wait_ge(merged.sem, merged.start_of(pos, "O"))
                    moving_unit(pos, k, half(k // 4), (m_hi, m_lo), 2 * (k % 4), KT)
                    if k == 5:
                        pe.wait_ge(x2_sum.sem, x2_sum.at(pos, NC - 1))
                        x2_transposes((0, 1))
                        pe.wait_ge(pin_in.sem, pin_in.at(pos, 0))
                        for i in range(2):
                            transposes(bank[2 + i], pin, i * P).then_inc(t_psum.sem, 1)
                    if k == 6:
                        pe.wait_ge(t_lo.sem, t_lo.at(pos, 1))
                        x2_transposes((2, 3))
                pe.wait_ge(t_lo.sem, t_lo.at(pos, x2_order(3)))
                moving_unit(pos, U_UP0, half(0), (p_hi, p_lo), 0, 2)
                pe.wait_ge(x2_sum.sem, x2_sum.at(pos, 2 * NC - 1))
                x2_transposes((4, 5, 6, 7))
                for s in (up0_full, up0_full_v):
                    pe.wait_ge(s.sem, s.at(pos, 1))
                for k in range(4):
                    moving_unit(pos, U_GATE + k, half(0), H, 2 * k, KT,
                                ready=lambda kt: pe.wait_ge(t_lo.sem, t_lo.at(pos, x2_order(kt)))
                                if kt >= 4 else None)
                for k in range(4):
                    moving_unit(pos, U_GATE + 4 + k, half(1), H, 2 * k, KT)
                pe.wait_ge(ple_gate.sem, ple_gate.at(pos, NC - 1))
                moving_unit(pos, U_UP1, half(0), (p_hi, p_lo), 0, 2)
                next_x(pos)

INPUTS = ["x", "p", "norm_g", "w_in", "conv_w", "conv_b", "dt_bias", "a_log", "d_skip", "gnorm_g",
          "pool_mix_w", "pool_mix_b", "pool_scale", "w_branch_a", "w_branch_b", "w_out",
          "ple_norm_g", "w_ple_gate", "w_ple_up", "final_g"]


def kernel(**inputs):
    import concourse.bacc as bacc
    from concourse.bass_utils import run_bass_kernel_spmd

    nc = bacc.Bacc("TRN2", target_bir_lowering=False, num_devices=1)
    arrays, args = {}, []
    for name in INPUTS:
        a = np.ascontiguousarray(inputs[name])
        arrays[f"in_{name}"] = a
        args.append(nc.dram_tensor(f"in_{name}", a.shape, mybir.dt.from_np(a.dtype),
                                   kind="ExternalInput").ap())
    args.append(nc.dram_tensor("out", (1, SEQ, DM), F32, kind="ExternalOutput").ap())
    build(nc, *args)
    result = run_bass_kernel_spmd(nc, [arrays], core_ids=[0])
    return result.results[0]["out"]
```
